# Optimizing a Trainium2 kernel written in Bass

```python
import jax
import jax.numpy as jnp
from jax import lax
import numpy as np

D_MODEL = 1024
BATCH = 1
SEQ = 512
DEPTH = 1
DEC_BATCH = 8
DEC_SEQ = 8
PAST_LEN = 4096
PAGE_SIZE = 128

N_HEADS = 8
HEAD_K = D_MODEL // N_HEADS
HEAD_V = D_MODEL // N_HEADS
QK_WIDTH = N_HEADS * HEAD_K
V_WIDTH = N_HEADS * HEAD_V
QKV_WIDTH = 2 * QK_WIDTH + V_WIDTH
SHORT_CONV = 4
CHUNK = 64
CONF_WIDTH = D_MODEL
CONF_KERNEL = 31
D_FF = 4 * D_MODEL
EPS = 1e-6
IN_WIDTH = QKV_WIDTH + 2 * N_HEADS + V_WIDTH + 2 * CONF_WIDTH + 2 * D_MODEL

kernel_name = 'hybrid_gdn_conformer_step'

def rmsnorm(x, g):
    xf = x.astype(jnp.float32)
    y = xf * lax.rsqrt(jnp.mean(xf * xf, axis=-1, keepdims=True) + EPS)
    return (y * g.astype(jnp.float32)).astype(x.dtype)

def layernorm(x, g, b):
    xf = x.astype(jnp.float32)
    mu = jnp.mean(xf, axis=-1, keepdims=True)
    xc = xf - mu
    var = jnp.mean(xc * xc, axis=-1, keepdims=True)
    y = xc * lax.rsqrt(var + EPS) * g.astype(jnp.float32) + b.astype(jnp.float32)
    return y.astype(x.dtype)

def l2norm(x):
    xf = x.astype(jnp.float32)
    return xf * lax.rsqrt(jnp.sum(xf * xf, axis=-1, keepdims=True) + EPS)

def causal_dwconv(x_ext, w):
    c = x_ext.shape[-1]
    return lax.conv_general_dilated(
        x_ext, w[:, None, :].astype(x_ext.dtype), window_strides=(1,), padding='VALID',
        dimension_numbers=('NWC', 'WIO', 'NWC'), feature_group_count=c)

def gated_delta_chunked(q, k, v, g, beta, s0):
    B, L, H, DK = q.shape
    DV = v.shape[-1]
    n = -(-L // CHUNK)
    pad = n * CHUNK - L

    def blocks(t):
        t = jnp.pad(t, [(0, 0), (0, pad)] + [(0, 0)] * (t.ndim - 2))
        t = t.reshape((B, n, CHUNK) + t.shape[2:])
        return jnp.moveaxis(t, 3, 2)

    q, k, v, g, beta = blocks(q), blocks(k), blocks(v), blocks(g), blocks(beta)
    gam = jnp.cumsum(g, axis=-1)
    idx = jnp.arange(CHUNK)
    causal = idx[:, None] >= idx[None, :]
    strict = idx[:, None] > idx[None, :]
    decay = jnp.exp(jnp.where(causal, gam[..., :, None] - gam[..., None, :], -jnp.inf))
    a = jnp.where(strict, beta[..., :, None] * jnp.einsum('bnhid,bnhjd->bnhij', k, k) * decay, 0.0)
    lhs = a + jnp.eye(CHUNK, dtype=a.dtype)
    rhs = jnp.concatenate([beta[..., None] * v, (beta * jnp.exp(gam))[..., None] * k], axis=-1)
    sol = lax.linalg.triangular_solve(lhs, rhs, left_side=True, lower=True, unit_diagonal=True)
    vw, kd = sol[..., :DV], sol[..., DV:]
    qk = jnp.einsum('bnhid,bnhjd->bnhij', q, k) * decay
    qd = q * jnp.exp(gam)[..., None]
    ko = k * jnp.exp(gam[..., -1:] - gam)[..., None]
    gl = jnp.exp(gam[..., -1])
    xs = tuple(jnp.moveaxis(t, 1, 0) for t in (vw, kd, qk, qd, ko, gl))

    def step(s, c):
        vw_c, kd_c, qk_c, qd_c, ko_c, gl_c = c
        u = vw_c - jnp.einsum('bhcd,bhde->bhce', kd_c, s)
        o = jnp.einsum('bhcd,bhde->bhce', qd_c, s) + jnp.einsum('bhij,bhje->bhie', qk_c, u)
        s = gl_c[..., None, None] * s + jnp.einsum('bhcd,bhce->bhde', ko_c, u)
        return s, o

    s_fin, o = lax.scan(step, s0, xs)
    o = jnp.transpose(o, (1, 0, 3, 2, 4)).reshape(B, n * CHUNK, H, DV)[:, :L]
    return o, s_fin

def hybrid_layer(x, s_delta, buf_qkv, buf_conf, w_in, conv_qkv_w, a_log, dt_bias, delta_norm_g,
                 conf_dw_w, conf_dw_b, conf_ln_g, conf_ln_b, w_out,
                 g_pre_mix, g_post_mix, g_pre_ffn, g_post_ffn, w_up, w_down):
    B, L, _ = x.shape
    f32 = jnp.float32
    h = rmsnorm(x, g_pre_mix)
    proj = jnp.einsum('bld,de->ble', h, w_in)
    o0 = QKV_WIDTH
    o1 = o0 + N_HEADS
    o2 = o1 + N_HEADS
    o3 = o2 + V_WIDTH
    o4 = o3 + 2 * CONF_WIDTH
    qkv_pre = proj[..., :o0]
    b_logit = proj[..., o0:o1]
    a_logit = proj[..., o1:o2]
    z = proj[..., o2:o3]
    glu_in = proj[..., o3:o4]
    gate_a = proj[..., o4:o4 + D_MODEL]
    gate_b = proj[..., o4 + D_MODEL:]

    qkv_ext = jnp.concatenate([buf_qkv.astype(x.dtype), qkv_pre], axis=1)
    qkv = jax.nn.silu(causal_dwconv(qkv_ext, conv_qkv_w))
    q = l2norm(qkv[..., :QK_WIDTH].reshape(B, L, N_HEADS, HEAD_K)) * (HEAD_K ** -0.5)
    k = l2norm(qkv[..., QK_WIDTH:2 * QK_WIDTH].reshape(B, L, N_HEADS, HEAD_K))
    v = qkv[..., 2 * QK_WIDTH:].reshape(B, L, N_HEADS, HEAD_V).astype(f32)
    beta = jax.nn.sigmoid(b_logit.astype(f32))
    g = -jnp.exp(a_log.astype(f32)) * jax.nn.softplus(a_logit.astype(f32) + dt_bias.astype(f32))
    o, s_new = gated_delta_chunked(q, k, v, g, beta, s_delta.astype(f32))
    o = o * lax.rsqrt(jnp.mean(o * o, axis=-1, keepdims=True) + EPS) * delta_norm_g.astype(f32)
    o = o * jax.nn.silu(z.astype(f32).reshape(B, L, N_HEADS, HEAD_V))
    o_a = o.reshape(B, L, V_WIDTH).astype(x.dtype)

    glu = glu_in[..., :CONF_WIDTH] * jax.nn.sigmoid(glu_in[..., CONF_WIDTH:])
    conf_ext = jnp.concatenate([buf_conf.astype(x.dtype), glu], axis=1)
    c = causal_dwconv(conf_ext, conf_dw_w) + conf_dw_b.astype(x.dtype)
    o_b = jax.nn.silu(layernorm(c, conf_ln_g, conf_ln_b))

    mixed = jax.nn.sigmoid(gate_a) * o_a + jax.nn.sigmoid(gate_b) * o_b
    x = x + rmsnorm(jnp.einsum('ble,ed->bld', mixed, w_out), g_post_mix)

    hf = jnp.einsum('bld,df->blf', rmsnorm(x, g_pre_ffn), w_up)
    f = jnp.square(jax.nn.relu(hf))
    y = x + rmsnorm(jnp.einsum('blf,fd->bld', f, w_down), g_post_ffn)
    return (y, s_new.astype(s_delta.dtype),
            qkv_ext[:, -(SHORT_CONV - 1):], conf_ext[:, -(CONF_KERNEL - 1):])

def setup_inputs(seed: int = 0) -> dict:
    key = jax.random.key(seed)
    ks = jax.random.split(key, 24)
    nrm = jax.random.normal
    x_prompt = nrm(ks[0], (BATCH, SEQ, D_MODEL), jnp.float32)
    x_sample = nrm(ks[1], (DEC_BATCH, DEC_SEQ, D_MODEL), jnp.float32)
    state_delta = nrm(ks[2], (DEPTH, DEC_BATCH, N_HEADS, HEAD_K, HEAD_V), jnp.float32) * HEAD_K ** -0.5
    state_qkv_conv = nrm(ks[3], (DEPTH, DEC_BATCH, SHORT_CONV - 1, QKV_WIDTH), jnp.float32)
    state_conf_conv = nrm(ks[4], (DEPTH, DEC_BATCH, CONF_KERNEL - 1, CONF_WIDTH), jnp.float32)
    w_in = nrm(ks[5], (DEPTH, D_MODEL, IN_WIDTH), jnp.float32) * D_MODEL ** -0.5
    conv_qkv_w = nrm(ks[6], (DEPTH, SHORT_CONV, QKV_WIDTH), jnp.float32) * SHORT_CONV ** -0.5
    a_log = jnp.log(jax.random.uniform(ks[7], (DEPTH, N_HEADS), jnp.float32, 1.0, 16.0))
    dt = jnp.exp(jax.random.uniform(ks[8], (DEPTH, N_HEADS), jnp.float32, np.log(1e-3), np.log(1e-1)))
    dt_bias = dt + jnp.log(-jnp.expm1(-dt))
    delta_norm_g = 1.0 + 0.1 * nrm(ks[9], (DEPTH, HEAD_V), jnp.float32)
    conf_dw_w = nrm(ks[10], (DEPTH, CONF_KERNEL, CONF_WIDTH), jnp.float32) * CONF_KERNEL ** -0.5
    conf_dw_b = 0.02 * nrm(ks[11], (DEPTH, CONF_WIDTH), jnp.float32)
    conf_ln_g = 1.0 + 0.1 * nrm(ks[12], (DEPTH, CONF_WIDTH), jnp.float32)
    conf_ln_b = 0.02 * nrm(ks[13], (DEPTH, CONF_WIDTH), jnp.float32)
    w_out = nrm(ks[14], (DEPTH, D_MODEL, D_MODEL), jnp.float32) * D_MODEL ** -0.5
    g_pre_mix = 1.0 + 0.1 * nrm(ks[15], (DEPTH, D_MODEL), jnp.float32)
    g_post_mix = 1.0 + 0.1 * nrm(ks[16], (DEPTH, D_MODEL), jnp.float32)
    g_pre_ffn = 1.0 + 0.1 * nrm(ks[17], (DEPTH, D_MODEL), jnp.float32)
    g_post_ffn = 1.0 + 0.1 * nrm(ks[18], (DEPTH, D_MODEL), jnp.float32)
    w_up = nrm(ks[19], (DEPTH, D_MODEL, D_FF), jnp.float32) * D_MODEL ** -0.5
    w_down = nrm(ks[20], (DEPTH, D_FF, D_MODEL), jnp.float32) * D_FF ** -0.5
    return {'x_prompt': x_prompt, 'x_sample': x_sample,
            'state_delta': state_delta, 'state_qkv_conv': state_qkv_conv,
            'state_conf_conv': state_conf_conv,
            'w_in': w_in, 'conv_qkv_w': conv_qkv_w, 'a_log': a_log, 'dt_bias': dt_bias,
            'delta_norm_g': delta_norm_g, 'conf_dw_w': conf_dw_w, 'conf_dw_b': conf_dw_b,
            'conf_ln_g': conf_ln_g, 'conf_ln_b': conf_ln_b, 'w_out': w_out,
            'g_pre_mix': g_pre_mix, 'g_post_mix': g_post_mix, 'g_pre_ffn': g_pre_ffn,
            'g_post_ffn': g_post_ffn, 'w_up': w_up, 'w_down': w_down}

def reference(x_prompt, x_sample, state_delta, state_qkv_conv, state_conf_conv,
              w_in, conv_qkv_w, a_log, dt_bias, delta_norm_g, conf_dw_w, conf_dw_b,
              conf_ln_g, conf_ln_b, w_out, g_pre_mix, g_post_mix, g_pre_ffn, g_post_ffn,
              w_up, w_down):
    B = x_prompt.shape[0]
    xp, xs = x_prompt, x_sample
    dp, qp, cp, ds, qs, cs = [], [], [], [], [], []
    for l in range(DEPTH):
        lw = (w_in[l], conv_qkv_w[l], a_log[l], dt_bias[l], delta_norm_g[l], conf_dw_w[l],
              conf_dw_b[l], conf_ln_g[l], conf_ln_b[l], w_out[l], g_pre_mix[l], g_post_mix[l],
              g_pre_ffn[l], g_post_ffn[l], w_up[l], w_down[l])
        xp, s_p, bq_p, bc_p = hybrid_layer(
            xp, jnp.zeros((B, N_HEADS, HEAD_K, HEAD_V), state_delta.dtype),
            jnp.zeros((B, SHORT_CONV - 1, QKV_WIDTH), x_prompt.dtype),
            jnp.zeros((B, CONF_KERNEL - 1, CONF_WIDTH), x_prompt.dtype), *lw)
        xs, s_s, bq_s, bc_s = hybrid_layer(
            xs, state_delta[l], state_qkv_conv[l], state_conf_conv[l], *lw)
        dp.append(s_p)
        qp.append(bq_p)
        cp.append(bc_p)
        ds.append(s_s)
        qs.append(bq_s)
        cs.append(bc_s)
    return (xp, xs, jnp.stack(dp), jnp.stack(qp), jnp.stack(cp),
            jnp.stack(ds), jnp.stack(qs), jnp.stack(cs))


_drawn_inputs = setup_inputs


def setup_inputs(seed=0):
    import zlib

    import numpy as np

    out = dict(_drawn_inputs(seed))
    spreads = {}
    factors = {'conf_ln_b': 5.136}
    for name, (base, spread) in spreads.items():
        noise = np.random.default_rng([zlib.crc32(name.encode()), seed]).standard_normal(out[name].shape)
        drawn = base * np.exp(spread * noise) if base else spread * noise
        out[name] = jnp.asarray(drawn.astype(out[name].dtype))
    for name, factor in factors.items():
        out[name] = (out[name] * factor).astype(out[name].dtype)
    return out
```

```python
from contextlib import ExitStack

import numpy as np

import concourse.bass as bass
import concourse.mybir as mybir

F32 = mybir.dt.float32
F32R = mybir.dt.float32r
ACT = mybir.ActivationFunctionType
ALU = mybir.AluOpType

P = 128
D = 1024
H = 8
KB = D // P
SEQ = 512
NS, LS = 8, 8
SMP = NS * LS
TOK = SEQ + SMP
HALF = TOK // 2
TILES = SEQ // P
QK_TAPS, CF_TAPS = 4, 31
EXT = SEQ + QK_TAPS - 1
EXS = LS + QK_TAPS - 1
GXT = SEQ + CF_TAPS - 1
GXS = LS + CF_TAPS - 1
EPS = 1e-6
BIG = 1e30
FFN_GROUPS = 4
PROJ_JOBS = 8 * H
OUT_JOB0 = PROJ_JOBS
FFN_JOB0 = PROJ_JOBS + H
JOBS = FFN_JOB0 + FFN_GROUPS * 2 * H
RING = 4
LEVELS = 7
LEVELS_S = 3
STEPS_1 = 14
Z, GA, GB, CA, CB, Q, K, V = range(8)
FIRST = {3: CA, 4: CB, 5: Q, 6: K, 7: V}
MIDDLE = {0: Q, 1: K, 2: V, 3: CA, 4: CB, 5: Z, 6: GA, 7: GB}
LAST = {0: Z, 1: GA, 2: GB}
LAST_SEGS = (0, 3, 6, 8, 10, 12, 14, 16, 18, 21, 24, 27)

_LAYOUT = [("ident", P), ("ones", P), ("tri", P), ("suf", P), ("big", P), ("tri_s", SMP),
           ("suf_s", SMP), ("big_s", SMP), ("lvl", LEVELS * P), ("lvl_s", LEVELS_S * SMP),
           ("colm", NS * SMP), ("rowm", NS), ("eps", 1), ("eps128", 1)]
OFF, _o = {}, 0
for _n, _w in _LAYOUT:
    OFF[_n] = (_o, _o + _w)
    _o += _w
CONSTS = _o
PARAMS = ["pre_mix", "post_mix", "pre_ffn", "post_ffn", "ln_g", "ln_b", "delta_g"]
TAPW = 3 * QK_TAPS + CF_TAPS + 1
HALO = 3 * NS * (QK_TAPS - 1) + NS * (CF_TAPS - 1)


def build(nc, x_t, w_all, w_log, log_par, consts, params, taps, halos, s_in,
          y_out, s_prompt, s_sample, qkv_rows, conf_rows):
    with ExitStack() as ctx:
        def sb(name, width, dt=F32):
            return ctx.enter_context(nc.sbuf_tensor(name, [P, width], dt))

        def sem(name):
            return ctx.enter_context(nc.semaphore(name))

        names = [("kn", TOK), ("qn", TOK), ("eg", TOK), ("dm", TOK), ("db", TOK), ("at", TOK),
                 ("qk", TOK), ("ui", TOK), ("c0", TOK), ("c1", TOK),
                 ("gk", SEQ + P), ("ko", SEQ + P), ("vt", SEQ + P), ("u", SEQ + P),
                 ("s", P), ("ss", NS * P), ("um", NS * P),
                 ("extq", EXT + NS * EXS), ("extk", EXT + NS * EXS), ("extv", EXT + NS * EXS),
                 ("gext", GXT + NS * GXS), ("c4", TOK), ("c31", TOK),
                 ("qc", TOK), ("kc", TOK), ("vc", TOK),
                 ("pad", 28 * TOK - 16031), ("sig", TOK), ("zs", TOK)]
        work_at = -(-nc.sbuf_base // 32) * 32
        work = sb("work", sum(w for _, w in names))
        at, v = 0, {}
        for nm, w in names:
            v[nm] = work[:, at:at + w]
            at += w
        xt = nc.alloc_sbuf_tensor_at("xt", [P, KB, TOK], F32, offset=work_at)
        f_hi = nc.alloc_sbuf_tensor_at("f_hi", [P, KB, TOK], F32R, offset=work_at + 4 * KB * TOK)
        f_lo = nc.alloc_sbuf_tensor_at("f_lo", [P, KB, TOK], F32R, offset=work_at + 8 * KB * TOK)
        f_tmp = nc.alloc_sbuf_tensor_at("f_tmp", [P, 4, TOK], F32, offset=work_at + 12 * KB * TOK)

        def blocks(name, dt=F32):
            return ctx.enter_context(nc.sbuf_tensor(name, [P, KB, TOK], dt))

        in_hi, in_lo = blocks("in_hi", F32R), blocks("in_lo", F32R)
        o_a = blocks("o_a")
        gate = blocks("gate")
        conf = blocks("conf")
        raw = ctx.enter_context(nc.sbuf_tensor("raw", [P, RING, KB, P], F32))
        w_hi = ctx.enter_context(nc.sbuf_tensor("w_hi", [P, 2, KB, P], F32R))
        w_lo = ctx.enter_context(nc.sbuf_tensor("w_lo", [P, 2, KB, P], F32R))
        cst = sb("cst", CONSTS)
        par = sb("par", len(PARAMS) * KB)
        tap = sb("tap", KB * TAPW)
        halo = sb("halo", HALO)
        lpar = sb("lpar", 2 * H)
        wlog = sb("wlog", KB * 2 * H)
        cols = sb("cols", 5 * 5 * H)
        hc = sb("hc", 25)
        qt, ct = sb("qt", 3 * QK_TAPS), sb("ct", CF_TAPS + 1)
        q_rows, c_rows = sb("q_rows", 3 * 27), sb("c_rows", 9 * (CF_TAPS - 1))
        csum = sb("csum", TOK)
        ps = ctx.enter_context(nc.psum_tensor("ps", [P, 8, 512], F32))

        def con(nm, rows=P):
            a, b = OFF[nm]
            return cst[0:rows, a:b]

        def lvl(l):
            a = OFF["lvl"][0] + (l - 1) * P
            return cst[:, a:a + P].unsqueeze(1).to_broadcast([P, TILES, P])

        def lvl_s(l):
            a = OFF["lvl_s"][0] + (l - 1) * SMP
            return cst[0:SMP, a:a + SMP]

        def pcol(nm, k):
            a = PARAMS.index(nm) * KB + k
            return par[:, a:a + 1]

        def job_ps(j2):
            return ps[:, 2 * j2:2 * j2 + 2, 0:HALF]

        def g(i):
            return ps[:, 4 + i, :]

        def g2(i):
            return ps[:, 4 + i:6 + i, 0:HALF]

        def two(ap):
            return ap.rearrange("p (a b) -> p a b", a=2)

        def pr(ap):
            return ap[:, 0:SEQ].rearrange("p (a b) -> p a b", a=TILES)

        def tile(ap, c):
            return ap[:, c * P:c * P + P]

        def sm(ap, rows=SMP):
            return ap[0:rows, SEQ:SEQ + SMP]

        def smw(ap):
            return ap[0:SMP, SEQ:SEQ + P]

        def g4(i):
            return g(i).rearrange("p (a b) -> p a b", a=TILES)

        def hcol(kind):
            return hc[:, 5 * kind:5 * kind + TILES].unsqueeze(2).to_broadcast([P, TILES, P])

        def hcol_s(kind, width):
            return hc[0:SMP, 5 * kind + 4:5 * kind + 5].to_broadcast([SMP, width])

        def seqs(ap, first, width, start, n):
            return ap[:, first:first + NS * width].rearrange("p (s t) -> p s t", s=NS)[
                :, :, start:start + n]

        EXTS = (v["extq"], v["extk"], v["extv"])
        CONV = (v["qc"], v["kc"], v["vc"])
        G, GAM, EGAM, KOF, BETA = range(5)
        C = (v["c0"], v["c1"])

        raw_landed = [sem(f"raw_landed{r}") for r in range(RING)]
        consts_landed, x_landed, taps_landed = sem("consts_landed"), sem("x_landed"), sem("taps_landed")
        log_landed, halo_landed, ss_landed = sem("log_landed"), sem("halo_landed"), sem("ss_landed")
        x_again = sem("x_again")
        states_stored, crows_stored, qrows_stored = sem("states_stored"), sem("crows_stored"), sem("qrows_stored")
        y_stored = sem("y_stored")
        w_high, w_low, job_done = sem("w_high"), sem("w_low"), sem("job_done")
        act_read = sem("act_read")
        dve_read = sem("dve_read")
        in_ready = sem("in_ready")
        squares, sums, scale = sem("squares"), sem("sums"), sem("scale")
        x_scaled, high_ready = sem("x_scaled"), sem("high_ready")
        log_ps, log_zero, log_act, log_dve = sem("log_ps"), sem("log_zero"), sem("log_act"), sem("log_dve")
        cum_ps, cols_ready = sem("cum_ps"), sem("cols_ready")
        gext_ready, halo_used = sem("gext_ready"), sem("halo_used")
        conv4, conv4_done, act_conv = sem("conv4"), sem("conv4_done"), sem("act_conv")
        conv31, conv31_done, conf_ready, csum_done = sem("conv31"), sem("conv31_done"), sem("conf_ready"), sem("csum_done")
        taps_cur = sem("taps_cur")
        zs_ready = sem("zs_ready")
        crows_ready, qrows_ready = sem("crows_ready"), sem("qrows_ready")
        hc_ready, gtri_ready, gm_ready = sem("hc_ready"), sem("gtri_ready"), sem("gm_ready")
        kq_sq, kq_sums, kq_scale, kq_ready = sem("kq_sq"), sem("kq_sums"), sem("kq_scale"), sem("kq_ready")
        k_tr, v_tr, gk_ready, vt_ready = sem("k_tr"), sem("v_tr"), sem("gk_ready"), sem("vt_ready")
        gam_ps, kk_ps, qk_ps = sem("gam_ps"), sem("kk_ps"), sem("qk_ps")
        dm_diff, eg_ready, dm_ready, db_ready = sem("dm_diff"), sem("eg_ready"), sem("dm_ready"), sem("db_ready")
        at_ready, qk_ready, qd_ready, c_ready = sem("at_ready"), sem("qk_ready"), sem("qd_ready"), sem("c_ready")
        c_tr, t_ready, u0_ready, ui_ready = sem("c_tr"), sem("t_ready"), sem("u0_ready"), sem("ui_ready")
        x_ps, x_ready, dt_ps, du_ps = sem("x_ps"), sem("x_ready"), sem("dt_ps"), sem("du_ps")
        kd_ps, kd_ready, kdm_ready = sem("kd_ps"), sem("kd_ready"), sem("kdm_ready")
        u_ps, u_ready, s_ps, s_ready = sem("u_ps"), sem("u_ready"), sem("s_ps"), sem("s_ready")
        us_ps, us_ready, um_ready, os_ps = sem("us_ps"), sem("us_ready"), sem("um_ready"), sem("os_ps")
        o_ps, o_read, o_sq, o_sums = sem("o_ps"), sem("o_read"), sem("o_sq"), sem("o_sums")
        o_scale, o_scaled, ss_decayed, ss_ps = sem("o_scale"), sem("o_scaled"), sem("ss_decayed"), sem("ss_ps")
        ss_ready, head_out = sem("ss_ready"), sem("head_out")
        mu_ps, mu_ready, xc_ready, xc_sq = sem("mu_ps"), sem("mu_ready"), sem("xc_ready"), sem("xc_sq")
        var_ps = sem("var_ps")
        ln_scale, ln_scaled, b_silu, b_gated = sem("ln_scale"), sem("ln_scaled"), sem("b_silu"), sem("b_gated")
        mixed = sem("mixed")
        y_sq, y_sum, ms_ps, ms_scale = sem("y_sq"), sem("y_sum"), sem("ms_ps"), sem("ms_scale")
        y_scaled, mid_ready = sem("y_scaled"), sem("mid_ready")
        mid_sq, ms2_ps, ms2_log = sem("mid_sq"), sem("ms2_ps"), sem("ms2_log")
        f_ready, f_high = sem("f_ready"), sem("f_high")
        out_sq, ms3_ps, var3, ms3_log = sem("out_sq"), sem("ms3_ps"), sem("var3"), sem("ms3_log")
        expo, out_scale, out_scaled, y_ready = sem("expo"), sem("out_scale"), sem("out_scaled"), sem("y_ready")

        def last(n):
            return isinstance(n, int) and n == H

        def first(n):
            return isinstance(n, int) and n == 0

        def jobs(n):
            return FIRST if first(n) else LAST if last(n) else MIDDLE

        def done_slot(n, j):
            return (8, 16, 27)[j] if last(n) else 4 * j + 3

        mid_sum, out_sum = sem("mid_sum"), sem("out_sum")
        o_log, f_square = sem("o_log"), sem("f_square")

        block = ctx.enter_context(nc.Block())

        @block.sync
        def _(sp):
            def weights(m, off, dst=None):
                j = 8 * m + off
                if not (isinstance(j, int) and j < RING):
                    sp.wait_ge(w_high, j - RING + 1)
                    sp.wait_ge(w_low, j - RING + 1)
                sp.dma_start(raw[:, off % RING], w_all[j] if isinstance(j, int) else
                             w_all[bass.ds(j, 1)].rearrange("a p k c -> p (a k) c")).then_inc(
                                 raw_landed[off % RING], 16)

            sp.dma_start(xt[:, 0:4], x_t[:, 0:4]).then_inc(x_landed, 16)
            sp.dma_start(xt[:, 4:8], x_t[:, 4:8]).then_inc(x_landed, 16)
            for dst, src in ((cst, consts), (par, params)):
                sp.dma_start(dst[:], src).then_inc(consts_landed, 16)
            weights(0, 0)
            sp.dma_start(tap[:], taps).then_inc(taps_landed, 16)
            sp.dma_start(lpar[:], log_par).then_inc(log_landed, 16)
            sp.dma_start(wlog[:], w_log).then_inc(log_landed, 16)
            for j in range(1, 5):
                weights(0, j)

            def phase(n):
                if first(n):
                    sp.dma_start(halo[:], halos[0]).then_inc(halo_landed, 16)
                for j in jobs(n):
                    weights(n, j + 2)
                if not last(n):
                    sp.wait_ge(halo_used, 4 * n + 4)
                    sp.dma_start(halo[:], halos[n + 1] if isinstance(n, int) else
                                 halos[bass.ds(n + 1, 1)].rearrange("a p c -> (a p) c")).then_inc(
                                     halo_landed, 16)
                    sp.wait_ge(crows_ready, n + 1)
                    sp.dma_start(conf_rows[n] if isinstance(n, int) else
                                 conf_rows[bass.ds(n, 1)].rearrange("a p c -> (a p) c"),
                                 c_rows[:]).then_inc(crows_stored, 16)
                if not first(n):
                    d = n - 1
                    sp.wait_ge(s_ready, TILES * n)
                    sp.dma_start(s_prompt[d] if isinstance(n, int) else
                                 s_prompt[bass.ds(d, 1)].rearrange("a p c -> (a p) c"),
                                 v["s"]).then_inc(states_stored, 16)
                    sp.wait_ge(ss_ready, n + 1)
                    sp.dma_start(s_sample[d] if isinstance(n, int) else
                                 s_sample[bass.ds(d, 1)].rearrange("a p c -> (a p) c"),
                                 v["ss"]).then_inc(states_stored, 16)
                if not last(n):
                    sp.wait_ge(qrows_ready, 3 * n + 3)
                    sp.dma_start(qkv_rows[n] if isinstance(n, int) else
                                 qkv_rows[bass.ds(n, 1)].rearrange("a p c -> (a p) c"),
                                 q_rows[:]).then_inc(qrows_stored, 16)
                    if not first(n):
                        sp.wait_ge(states_stored, 32 * n)
                    sp.dma_start(v["ss"], s_in[n] if isinstance(n, int) else
                                 s_in[bass.ds(n, 1)].rearrange("a p c -> (a p) c")).then_inc(
                                     ss_landed, 16)

            phase(0)
            with sp.Fori(1, H) as n:
                phase(n)
            phase(H)
            sp.wait_ge(states_stored, 32 * H)
            for off in (5, 6, 7):
                weights(8, off)
            sp.wait_ge(head_out, H + 1)
            sp.dma_start(xt[:], x_t).then_inc(x_again, 16)
            with sp.Fori(9, 9 + 2 * FFN_GROUPS) as m:
                for off in range(8):
                    weights(m, off)
            for k in range(KB):
                sp.wait_ge(y_ready, k + 1)
                sp.dma_start(y_out[:, k], o_a[:, k]).then_inc(y_stored, 16)
            sp.wait_ge(y_stored, 16 * KB)
            sp.wait_ge(crows_stored, 16 * H)
            sp.wait_ge(qrows_stored, 16 * H)

        @block.tensor
        def _(pe):
            mm = nc.tensor.matmul

            def segment(m, off, i, hi, lo, waits=None, free=()):
                if i == 0:
                    pe.wait_ge(w_high, 8 * m + off + 1)
                    pe.wait_ge(w_low, 8 * m + off + 1)
                    for s_, n_ in free:
                        pe.wait_ge(s_, n_)
                w = off % 2
                for k in (2 * i, 2 * i + 1):
                    if waits:
                        pe.wait_ge(waits[0], waits[1] + k + 1)
                    for p3, (a, b) in enumerate(((w_hi, hi), (w_lo, hi), (w_hi, lo))):
                        for h in range(2):
                            r = mm(ps[:, 2 * w + h, 0:HALF], a[:, w, k],
                                   b[:, k, h * HALF:(h + 1) * HALF],
                                   start=k == 0 and p3 == 0, stop=k == KB - 1 and p3 == 2)
                if i == 3:
                    r.then_inc(job_done, 1)

            def ones_sum(dst, src, start=True, stop=True):
                for h in range(2):
                    r = mm(dst[:, h], con("ones"), src[:, h * HALF:(h + 1) * HALF],
                           start=start, stop=stop)
                return r

            pe.wait_ge(consts_landed, 32)
            for k in range(KB):
                if k % 2 == 0:
                    pe.wait_ge(squares, k // 2 + 1)
                r = ones_sum(g2(0), conf[:, k], k == 0, k == KB - 1)
            r.then_inc(sums, 1)

            def logits():
                pe.wait_ge(log_landed, 32)
                pe.wait_ge(log_zero, 1)
                for t in range(5):
                    n = P if t < TILES else SMP
                    for k in range(KB):
                        for part in (in_hi, in_lo):
                            r = mm(g(3)[0:n, 16 * t:16 * t + 16],
                                   part[:, k, P * t:P * t + n].bitcast(F32),
                                   wlog[:, 16 * k:16 * k + 16],
                                   start=k == 0 and part is in_hi, stop=k == KB - 1 and part is in_lo)
                r.then_inc(log_ps, 1)
                pe.wait_ge(log_dve, 4)
                for i, (a, b) in enumerate((("tri", "tri_s"), ("suf", "suf_s"))):
                    mm(g(2)[:, 64 * i:64 * i + 32], con(a), cols[:, 0:32], start=True, stop=True)
                    r = mm(g(2)[0:SMP, 64 * i + 32:64 * i + 40], con(b, SMP), cols[0:SMP, 32:40],
                           start=True, stop=True)
                r.then_inc(cum_ps, 1)

            def phase(n):
                gdn, proj = not first(n), not last(n)
                segs = 0
                for s in range(32):
                    if last(n):
                        if s in LAST_SEGS:
                            i = LAST_SEGS.index(s)
                            segment(n, i // 4 - 3, i % 4, in_hi, in_lo,
                                    free=[(act_read, 8 * n + i // 4 - 4)])
                    elif s >= 12 or gdn:
                        j = s // 4
                        fr = [] if first(n) and j <= 4 else [(act_read, 8 * n + j - 4)]
                        w_ = (in_ready, 0) if first(n) and j == 3 else None
                        segment(n, j - 3, s % 4, in_hi, in_lo, waits=w_, free=fr)
                    if first(n) and s == 19:
                        logits()
                    if not gdn:
                        continue
                    if s == 0:
                        pe.wait_ge(ss_ready, n)
                        pe.wait_ge(kq_sq, 2 * n - 1)
                        ones_sum(g2(0), C[0]).then_inc(kq_sums, 1)
                        pe.wait_ge(o_log, n)
                        pe.wait_ge(kq_sq, 2 * n)
                        ones_sum(g2(2), C[1]).then_inc(kq_sums, 1)
                    if s == 2:
                        pe.wait_ge(kq_scale, 4 * n)
                        pe.wait_ge(kq_ready, 2 * n - 1)
                        for c in range(TILES):
                            nc.tensor.transpose(tile(g(0), c), tile(v["kn"], c), con("ident"))
                        nc.tensor.transpose(g(2)[0:SMP, 0:P], sm(v["kn"], P), con("ident")).then_inc(k_tr, 1)
                        for c in range(TILES):
                            nc.tensor.transpose(tile(g(1), c), tile(v["vc"], c), con("ident"))
                        nc.tensor.transpose(g(3)[0:SMP, 0:P], sm(v["vc"], P), con("ident")).then_inc(v_tr, 1)
                    if s == 3:
                        pe.wait_ge(gtri_ready, n)
                        pe.wait_ge(vt_ready, n)
                        mm(g(1), con("ones"), v["dm"][:, 0:SEQ], start=True, stop=True)
                        mm(g(3)[:, 0:SMP], con("ones", SMP), sm(v["dm"]), start=True,
                           stop=True).then_inc(gam_ps, 1)
                        pe.wait_ge(gk_ready, n)
                        for c in range(TILES):
                            mm(tile(g(0), c), tile(v["kn"], c), tile(v["kn"], c), start=True, stop=True)
                        mm(g(2)[0:SMP, 0:SMP], sm(v["kn"], P), sm(v["kn"], P), start=True,
                           stop=True).then_inc(kk_ps, 1)
                    if s == 4:
                        pe.wait_ge(eg_ready, n)
                        pe.wait_ge(kq_ready, 2 * n)
                        for c in range(TILES):
                            mm(tile(g(1), c), tile(v["kn"], c), tile(v["qn"], c), start=True, stop=True)
                        mm(g(3)[0:SMP, 0:SMP], sm(v["kn"], P), sm(v["qn"], P), start=True,
                           stop=True).then_inc(qk_ps, 1)
                    if s == 7:
                        pe.wait_ge(c_ready, LEVELS * n - 6)
                        for c in range(TILES):
                            nc.tensor.transpose(tile(g(0), c), tile(C[0], c), con("ident"))
                        nc.tensor.transpose(g(2)[0:SMP, 0:SMP], sm(C[0]),
                                            con("ident", SMP)[:, 0:SMP]).then_inc(c_tr, 1)
                    if s in (9, 11, 13, 15, 17, 19):
                        l = (s - 5) // 2
                        ci = C[(l - 1) % 2]
                        pe.wait_ge(c_ready, LEVELS * n - 7 + l)
                        pe.wait_ge(t_ready, 6 * n - 7 + l)
                        for c in range(TILES):
                            r = mm(tile(g(0), c), tile(ci, c), tile(v["dm"], c), start=True, stop=True)
                        if l <= LEVELS_S:
                            r = mm(g(2)[0:SMP, 0:SMP], sm(ci), sm(v["dm"]), start=True, stop=True)
                        r.then_inc(x_ps, 1)
                    if s in (10, 12, 14, 16, 18, 20):
                        l = (s - 6) // 2
                        pe.wait_ge(x_ready, 6 * n - 7 + l)
                        if l == 2:
                            pe.wait_ge(u0_ready, n)
                        else:
                            pe.wait_ge(ui_ready, 6 * n - 8 + l)
                        if l < LEVELS:
                            for c in range(TILES):
                                r = mm(tile(g(0), c), tile(v["ui"], c), tile(v["db"], c), start=True, stop=True)
                            if l < LEVELS_S:
                                r = mm(g(2)[0:SMP, 0:SMP], sm(v["ui"]), sm(v["db"]), start=True, stop=True)
                            r.then_inc(dt_ps, 1)
                        for c in range(TILES):
                            r = mm(tile(g(1), c), tile(v["db"], c), tile(v["ui"], c), start=True, stop=True)
                        if l <= LEVELS_S:
                            r = mm(g(3)[0:SMP, 0:SMP], sm(v["db"]), sm(v["ui"]), start=True, stop=True)
                        r.then_inc(du_ps, 1)
                    if s == 21:
                        pe.wait_ge(ui_ready, 6 * n)
                        for c in range(TILES):
                            mm(tile(g(0), c), tile(v["gk"], c), tile(v["ui"], c), start=True, stop=True)
                        mm(g(2)[:, 0:SMP], smw(v["gk"]), sm(v["ui"]), start=True,
                           stop=True).then_inc(kd_ps, 1)
                    if s in (21, 23, 25, 27):
                        c = (s - 21) // 2
                        if c:
                            pe.wait_ge(s_ready, TILES * n - 4 + c)
                        r = mm(g(1)[:, 0:P], tile(v["ui"], c), tile(v["vt"], c), start=True,
                               stop=c == 0)
                        if c:
                            r = mm(g(1)[:, 0:P], tile(v["kn"], c), v["s"], start=False, stop=True)
                        r.then_inc(u_ps, 1)
                        if c:
                            mm(tile(g(3), c), v["s"], tile(v["qn"], c), start=True, stop=False)
                    if s in (22, 24, 26, 28):
                        c = (s - 22) // 2
                        if c == 0:
                            pe.wait_ge(kd_ready, 2 * n - 1)
                            pe.wait_ge(qd_ready, n)
                        pe.wait_ge(u_ready, TILES * n - 3 + c)
                        mm(g(0)[:, 0:P], tile(v["ko"], c), tile(v["u"], c), start=True,
                           stop=True).then_inc(s_ps, 1)
                        r = mm(tile(g(3), c), tile(v["u"], c), tile(v["qk"], c), start=c == 0, stop=True)
                        if c == TILES - 1:
                            r.then_inc(o_ps, 1)
                    if s == 24:
                        pe.wait_ge(kdm_ready, n)
                        pe.wait_ge(kd_ready, 2 * n)
                        pe.wait_ge(ss_landed, 16 * n)
                        pe.nop(nofuse=True)
                        mm(g(2)[0:SMP, 0:P], sm(v["ui"]), smw(v["vt"]), start=True, stop=False)
                        for q in range(NS):
                            r = mm(g(2)[0:SMP, 0:P], v["um"][:, q * SMP:(q + 1) * SMP],
                                   tile(v["ss"], q), start=False, stop=q == NS - 1)
                        r.then_inc(us_ps, 1)
                    if s == 26:
                        pe.wait_ge(us_ready, n)
                        for q in range(NS):
                            cols_q = slice(q * LS, (q + 1) * LS)
                            mm(g(2)[:, cols_q], smw(v["u"]), sm(v["qk"])[:, cols_q],
                               start=True, stop=False)
                            r = mm(g(2)[:, cols_q], tile(v["ss"], q), sm(v["qn"], P)[:, cols_q],
                                   start=False, stop=True)
                        r.then_inc(os_ps, 1)
                    if s == 29:
                        pe.wait_ge(um_ready, n)
                        pe.wait_ge(s_ready, TILES * n)
                        for q in range(2):
                            r = mm(g(q), smw(v["ko"]), v["um"][0:SMP, q * SEQ:(q + 1) * SEQ],
                                   start=True, stop=True)
                        r.then_inc(ss_ps, 1)
                    if s == 30:
                        pe.wait_ge(o_sq, n)
                        pe.wait_ge(o_read, 2 * n)
                        ones_sum(g2(2), C[0]).then_inc(o_sums, 1)
                    if last(n) and s == 20:
                        pe.wait_ge(csum_done, H + 1)
                        pe.wait_ge(act_read, 63)
                        ones_sum(job_ps(0), csum).then_inc(mu_ps, 1)
                    if last(n) and 23 <= s < 31:
                        k = s - 23
                        pe.wait_ge(xc_sq, k + 1)
                        ones_sum(job_ps(0), v[("c4", "extq")[k % 2]][:, 0:TOK], k == 0,
                                 k == KB - 1).then_inc(var_ps, 1)

            phase(0)
            with pe.Fori(1, H) as n:
                phase(n)
            phase(H)

            for j in range(8):
                for i in range(4):
                    free = [(act_read, 64 + j - 1)] if j else [(ln_scale, 1)]
                    segment(8, j, i, in_hi, in_lo, waits=(in_ready, 8) if j == 0 else None, free=free)
            pe.wait_ge(y_sum, 8)
            ones_sum(g2(0), csum).then_inc(ms_ps, 1)

            def group(gr, tail=False):
                m = 2 * gr + 9
                for j in range(8):
                    free = [(dve_read, 8 * gr + 7 + j)] if j < 2 else [(act_read, 8 * gr + 72 + j - 1)]
                    for i in range(4):
                        segment(m, j, i, in_hi, in_lo, waits=(in_ready, 16) if j == 0 else None, free=free)
                for j in range(8):
                    free = [(act_read, 8 * gr + 79 + j)] if j < 2 else [(dve_read, 8 * gr + 8 + j - 1)]
                    for i in range(4):
                        segment(m + 1, j, i, f_hi, f_lo, waits=(f_ready, 8 * gr) if j == 0 else None, free=free)

            pe.wait_ge(act_read, 72)
            with pe.Fori(0, FFN_GROUPS - 1) as gr:
                group(gr)
            pe.wait_ge(mid_sum, 8)
            ones_sum(g2(0), csum).then_inc(ms2_ps, 1)
            group(FFN_GROUPS - 1)
            pe.wait_ge(out_sum, 8)
            ones_sum(g2(2), gate[:, 5]).then_inc(ms3_ps, 1)

        def split_off(n, s):
            if last(n):
                return {0: -2, 9: -1, 17: 0}.get(s)
            if s % 4 or s == 32 or (first(n) and s < 12):
                return None
            return s // 4 - 2

        def conv_slots(n, d):
            return (24 + d, 28 + d, 32) if first(n) else (4 + d, 8 + d, 12 + d)

        def evac(n, s):
            for j, kind in jobs(n).items():
                if done_slot(n, j) + 1 == s:
                    return j, kind
            return None, None

        @block.scalar
        def _(act):
            A = nc.scalar.activation

            def log_exp():
                act.preload_act_table_set("natural_log_exp_and_others")

            def split(m, off):
                act.wait_ge(raw_landed[off % RING], 32 * m + 16 * (off // RING) + 16)
                if not (isinstance(m, int) and 8 * m + off < 2):
                    act.wait_ge(job_done, 8 * m + off - 1)
                nc.scalar.copy(w_hi[:, off % 2], raw[:, off % RING]).then_inc(w_high, 1)

            act.sem_inc(o_log, 1)
            act.wait_ge(x_landed, 32)
            for k in range(4):
                A(conf[:, 2 * k:2 * k + 2], xt[:, 2 * k:2 * k + 2], ACT.Square).then_inc(squares, 1)
            act.wait_ge(consts_landed, 32)
            split(0, 0)
            log_exp()
            act.wait_ge(sums, 1)
            A(two(v["c31"]), g2(0), ACT.Ln, scale=1.0 / D, bias=con("eps")).then_inc(scale, 1)
            act.wait_ge(scale, 1)
            A(v["c31"], v["c31"], ACT.Exp, scale=-0.5).then_inc(scale, 1)
            for k in range(KB):
                act.wait_ge(x_scaled, k + 1)
                A(in_hi[:, k], o_a[:, k], ACT.Copy, scale=pcol("pre_mix", k)).then_inc(high_ready, 1)

            def logits():
                sc = v["gk"]
                lp = g(3)[:, 0:80].rearrange("p (t c) -> p t c", t=5)
                log_exp()
                act.wait_ge(log_landed, 32)
                A(sc[:, 160:168], lpar[:, H:2 * H], ACT.Exp)
                act.wait_ge(log_dve, 1)
                A(cols[:, 160:200].rearrange("p (t h) -> p t h", t=5), lp[:, :, 0:H],
                  ACT.Sigmoid).then_inc(log_act, 1)
                A(sc[:, 40:80], sc[:, 0:40], ACT.Abs).then_inc(log_act, 1)
                act.wait_ge(log_act, 2)
                A(sc[:, 80:120], sc[:, 40:80], ACT.Exp, scale=-1.0).then_inc(log_act, 1)
                act.wait_ge(log_act, 3)
                A(sc[:, 120:160], sc[:, 80:120], ACT.Ln, bias=1.0).then_inc(log_act, 1)
                act.wait_ge(log_dve, 5)
                A(cols[:, 80:120], g(2)[:, 0:40], ACT.Exp).then_inc(cols_ready, 1)
                A(cols[:, 120:160], g(2)[:, 64:104], ACT.Exp).then_inc(cols_ready, 1)

            def squares_kq(n):
                act.wait_ge(act_conv, 3 * n + 2)
                A(C[0], v["kc"], ACT.Square).then_inc(kq_sq, 1)
                A(C[1], v["qc"], ACT.Square).then_inc(kq_sq, 1)

            def phase(n):
                gdn = not first(n)
                for s in range(33):
                    off = split_off(n, s)
                    if off is not None:
                        split(n, off)
                    pos, j = evac(n, s)
                    if pos is not None:
                        act.wait_ge(job_done, 8 * n - 2 + pos)
                        src = job_ps((pos + 1) % 2)
                        if j == Z:
                            A(two(v["zs"]), src, ACT.Silu).then_inc(act_read, 1)
                        if j == GA:
                            act.wait_ge(gext_ready, n if last(n) else n + 1)
                            A(two(v["sig"]), src, ACT.Sigmoid).then_inc(act_read, 1)
                        if j == GB:
                            dst = gate[:, n - 1] if isinstance(n, int) else gate[:, bass.ds(n - 1, 1)]
                            A(dst.rearrange("p (a b) -> p a b", a=2) if isinstance(n, int) else
                              dst.rearrange("p o (a b) -> p (o a) b", a=2), src,
                              ACT.Sigmoid).then_inc(act_read, 1)
                        if j == CA:
                            if gdn:
                                act.wait_ge(act_conv, 3 * n + 3)
                            A(two(v["c4"]), src, ACT.Copy).then_inc(act_read, 1)
                        if j == CB:
                            if gdn:
                                act.wait_ge(zs_ready, n)
                            A(two(v["sig"]), src, ACT.Sigmoid).then_inc(act_read, 1)
                        if j is not None and j >= Q:
                            e = EXTS[j - Q]
                            if gdn:
                                act.wait_ge(qrows_ready, 3 * n - 2 + j - Q)
                            A(e[:, 3:3 + HALF], src[:, 0], ACT.Copy)
                            A(e[:, 3 + HALF:EXT], src[:, 1, 0:SEQ - HALF], ACT.Copy)
                            A(seqs(e, EXT, EXS, 3, LS),
                              src[:, 1, SEQ - HALF:HALF].rearrange("p (s t) -> p s t", s=NS),
                              ACT.Copy).then_inc(act_read, 1)
                    if not last(n) and s in conv_slots(n, 2):
                        i = conv_slots(n, 2).index(s)
                        act.wait_ge(conv4_done, 3 * n + i + 1)
                        A(CONV[i], v["c4"], ACT.Silu).then_inc(act_conv, 1)
                    if first(n) and s == 20:
                        logits()
                    if gdn and s == (17 if last(n) else 20):
                        act.wait_ge(conv31_done, n)
                        dst = conf[:, n - 1] if isinstance(n, int) else \
                            conf[:, bass.ds(n - 1, 1)].rearrange("p a b -> p (a b)")
                        A(dst, v["c31"], ACT.Identity, bias=ct[:, CF_TAPS:CF_TAPS + 1]).then_inc(conf_ready, 1)
                    if not last(n) and s == 31:
                        squares_kq(n)
                    if last(n) and s == 21:
                        act.wait_ge(mu_ps, 1)
                        A(two(csum[:]), job_ps(0), ACT.Copy, scale=1.0 / D).then_inc(mu_ready, 1)
                    if not gdn:
                        continue
                    if s == 0:
                        log_exp()
                        act.wait_ge(head_out, n)
                        act.wait_ge(kq_sums, 2 * n - 1)
                        A(two(v["at"]), g2(0), ACT.Ln, bias=con("eps")).then_inc(kq_scale, 1)
                        act.wait_ge(kq_scale, 4 * n - 3)
                        A(v["at"], v["at"], ACT.Exp, scale=-0.5).then_inc(kq_scale, 1)
                        act.wait_ge(kq_sums, 2 * n)
                        A(two(v["ui"]), g2(2), ACT.Ln, scale=float(P), bias=con("eps128")).then_inc(kq_scale, 1)
                        act.wait_ge(kq_scale, 4 * n - 1)
                        A(v["ui"], v["ui"], ACT.Exp, scale=-0.5).then_inc(kq_scale, 1)
                    if s == 2:
                        act.wait_ge(v_tr, n)
                        A(v["vt"][:, 0:SEQ], g(1), ACT.Copy)
                        A(smw(v["vt"]), g(3)[0:SMP, 0:P], ACT.Copy).then_inc(vt_ready, 1)
                    if s == 3:
                        act.wait_ge(dm_diff, n)
                        A(v["eg"][:, 0:SEQ], g(1), ACT.Exp)
                        A(sm(v["eg"], P), g(3)[:, 0:SMP], ACT.Exp).then_inc(eg_ready, 1)
                        A(v["dm"][:, 0:SEQ], v["dm"][:, 0:SEQ], ACT.Exp)
                        A(sm(v["dm"]), sm(v["dm"]), ACT.Exp).then_inc(dm_ready, 1)
                    if s in (9, 11, 13, 15, 17, 19):
                        l = (s - 5) // 2
                        act.wait_ge(x_ps, 6 * n - 7 + l)
                        r = A(v["db"][:, 0:SEQ], g(0), ACT.Copy)
                        if l <= LEVELS_S:
                            r = A(sm(v["db"]), g(2)[0:SMP, 0:SMP], ACT.Copy)
                        r.then_inc(x_ready, 1)
                    if s == 21:
                        act.wait_ge(kd_ps, n)
                        A(v["kn"][:, 0:SEQ], g(0), ACT.Copy, scale=-1.0).then_inc(kd_ready, 1)
                        A(sm(v["kn"], P), g(2)[:, 0:SMP], ACT.Copy, scale=-1.0).then_inc(kd_ready, 1)
                    if s in (21, 23, 25, 27):
                        c = (s - 21) // 2
                        act.wait_ge(u_ps, TILES * n - 3 + c)
                        A(tile(v["u"], c), g(1)[:, 0:P], ACT.Copy,
                          scale=hc[:, 5 * BETA + c:5 * BETA + c + 1]).then_inc(u_ready, 1)
                    if s == 24:
                        act.wait_ge(us_ps, n)
                        A(smw(v["u"]), g(2)[0:SMP, 0:P], ACT.Copy,
                          scale=hc[0:SMP, 5 * BETA + 4:5 * BETA + 5]).then_inc(us_ready, 1)
                    if s == 26:
                        act.wait_ge(os_ps, n)
                        dst = o_a[:, n - 1, SEQ:TOK] if isinstance(n, int) else \
                            o_a[:, bass.ds(n - 1, 1), SEQ:TOK].rearrange("p a b -> p (a b)")
                        A(dst, g(2)[:, 0:SMP], ACT.Copy).then_inc(o_read, 1)
                    if s == 28:
                        act.wait_ge(o_ps, n)
                        dst = o_a[:, n - 1, 0:SEQ] if isinstance(n, int) else \
                            o_a[:, bass.ds(n - 1, 1), 0:SEQ].rearrange("p a b -> p (a b)")
                        A(dst, g(3), ACT.Copy).then_inc(o_read, 1)
                        act.wait_ge(o_read, 2 * n)
                        src = o_a[:, n - 1] if isinstance(n, int) else \
                            o_a[:, bass.ds(n - 1, 1)].rearrange("p a b -> p (a b)")
                        act.nop(nofuse=True)
                        A(C[0], src, ACT.Square).then_inc(o_sq, 1)
                    if s == 30:
                        log_exp()
                        act.wait_ge(o_sums, n)
                        A(two(v["at"]), g2(2), ACT.Ln, scale=1.0 / P, bias=con("eps")).then_inc(o_log, 1)
                        act.wait_ge(o_log, n + 1)
                        A(v["at"], v["at"], ACT.Exp, scale=-0.5).then_inc(o_scale, 1)
                    if last(n) and 22 <= s < 30:
                        k = s - 22
                        act.wait_ge(xc_ready, k + 1)
                        if k >= 2:
                            act.wait_ge(var_ps, k - 1)
                        A(v[("c4", "extq")[k % 2]][:, 0:TOK], conf[:, k], ACT.Square).then_inc(xc_sq, 1)

            phase(0)
            with act.Fori(1, H) as n:
                phase(n)
            phase(H)
            log_exp()
            act.wait_ge(var_ps, 8)
            A(two(v["c31"]), job_ps(0), ACT.Ln, scale=1.0 / D, bias=con("eps")).then_inc(ln_scale, 1)
            act.wait_ge(ln_scale, 1)
            A(v["c31"], v["c31"], ACT.Exp, scale=-0.5).then_inc(ln_scale, 1)
            for k in range(KB):
                act.wait_ge(ln_scaled, k + 1)
                A(conf[:, k], conf[:, k], ACT.Silu, scale=pcol("ln_g", k),
                  bias=pcol("ln_b", k)).then_inc(b_silu, 1)
            for k in range(KB):
                act.wait_ge(mixed, k + 1)
                if k == 0:
                    act.wait_ge(job_done, 64)
                A(in_hi[:, k], conf[:, k], ACT.Copy).then_inc(high_ready, 1)

            for j in range(8):
                split(8, j + 1)
                act.wait_ge(job_done, 65 + j)
                A(two(gate[:, j]), job_ps(j % 2), ACT.Copy).then_inc(act_read, 1)
                act.wait_ge(act_read, 65 + j)
                if j >= 2:
                    act.wait_ge(y_sum, j - 1)
                A(v[("c4", "extq")[j % 2]][:, 0:TOK], gate[:, j], ACT.Square).then_inc(y_sq, 1)
            log_exp()
            act.wait_ge(ms_ps, 1)
            A(two(v["c31"]), g2(0), ACT.Ln, scale=1.0 / D, bias=con("eps")).then_inc(ms_scale, 1)
            act.wait_ge(ms_scale, 1)
            A(v["c31"], v["c31"], ACT.Exp, scale=-0.5).then_inc(ms_scale, 1)
            for k in range(KB):
                act.wait_ge(mid_ready, k + 1)
                A(in_hi[:, k], conf[:, k], ACT.Copy, scale=pcol("pre_ffn", k)).then_inc(high_ready, 1)
            for k in range(KB):
                if k >= 2:
                    act.wait_ge(mid_sum, k - 1)
                A(v[("sig", "zs")[k % 2]], conf[:, k], ACT.Square).then_inc(mid_sq, 1)

            def group(gr, tail=False):
                m = 2 * gr + 9
                for j in range(8):
                    split(m, j + 1)
                    act.wait_ge(job_done, 16 * gr + 73 + j)
                    act.wait_ge(f_square, 8 * gr + j + 1)
                    A(two(f_tmp[:, j % 2]), job_ps(j % 2), ACT.Relu).then_inc(act_read, 1)
                    act.wait_ge(act_read, 8 * gr + 73 + j)
                    A(f_hi[:, j], f_tmp[:, j % 2], ACT.Square).then_inc(f_high, 1)
                for j in range(8):
                    if not (tail and j == 7):
                        split(m + 1, j + 1)
                    if tail:
                        act.wait_ge(dve_read, 8 * gr + 9 + j)
                        if j >= 2:
                            act.wait_ge(out_sum, j - 1)
                        A(v[("sig", "zs")[j % 2]], o_a[:, j], ACT.Square).then_inc(out_sq, 1)

            with act.Fori(0, FFN_GROUPS - 1) as gr:
                group(gr)
            log_exp()
            act.wait_ge(ms2_ps, 1)
            A(two(gate[:, 1]), g2(0), ACT.Ln, scale=1.0 / D, bias=con("eps")).then_inc(ms2_log, 1)
            act.wait_ge(ms2_log, 1)
            A(gate[:, 2], gate[:, 1], ACT.Exp, scale=-2.0).then_inc(ms2_log, 1)
            group(FFN_GROUPS - 1, tail=True)
            log_exp()
            act.wait_ge(var3, 1)
            A(gate[:, 3], gate[:, 3], ACT.Ln, scale=1.0 / D, bias=con("eps")).then_inc(ms3_log, 1)
            act.wait_ge(expo, 1)
            A(gate[:, 4], gate[:, 4], ACT.Exp, scale=-1.0).then_inc(out_scale, 1)

        @block.vector
        def _(dve):
            ve = nc.vector

            def tt(out, a, b, op):
                return ve.tensor_tensor(out, a, b, op)

            def stt(out, a, s_, b, op0, op1):
                return ve.scalar_tensor_tensor(out=out, in0=a, scalar=s_, in1=b, op0=op0, op1=op1)

            ve.memset(g(3)[:, 0:80], 0.0)
            ve.memset(g(2)[:, 0:128], 0.0).then_inc(log_zero, 1)
            for e in EXTS:
                ve.memset(e[:, 0:QK_TAPS - 1], 0.0)
            ve.memset(v["gext"][:, 0:CF_TAPS - 1], 0.0)
            ve.memset(csum[:], 0.0).then_inc(csum_done, 1)
            dve.sem_inc(ss_ready, 1)
            dve.sem_inc(head_out, 1)
            dve.sem_inc(zs_ready, 1)
            dve.sem_inc(f_square, 2)
            dve.wait_ge(consts_landed, 32)
            dve.wait_ge(scale, 2)
            for k in range(KB):
                tt(o_a[:, k], xt[:, k], v["c31"], ALU.mult).then_inc(x_scaled, 1)
            for k in range(KB):
                dve.wait_ge(high_ready, k + 1)
                stt(in_lo[:, k], o_a[:, k], pcol("pre_mix", k), in_hi[:, k].bitcast(F32),
                    ALU.mult, ALU.subtract).then_inc(in_ready, 1)

            def logits():
                sc = v["gk"]
                r3 = lambda ap: ap.rearrange("p (t h) -> p t h", t=5)
                dve.wait_ge(log_ps, 1)
                lp = g(3)[:, 0:80].rearrange("p (t c) -> p t c", t=5)
                tt(r3(sc[:, 0:40]), lp[:, :, H:2 * H], lpar[:, 0:H].unsqueeze(1).to_broadcast([P, 5, H]),
                   ALU.add).then_inc(log_dve, 1)
                dve.wait_ge(log_act, 4)
                dve.wait_ge(log_dve, 1)
                stt(sc[:, 200:240], sc[:, 0:40], 0.0, sc[:, 120:160], ALU.max, ALU.add).then_inc(log_dve, 1)
                dve.wait_ge(log_dve, 2)
                stt(r3(cols[:, 0:40]), r3(sc[:, 200:240]), -1.0,
                    sc[:, 160:168].unsqueeze(1).to_broadcast([P, 5, H]), ALU.mult, ALU.mult).then_inc(log_dve, 2)
                dve.wait_ge(cum_ps, 1)
                ve.tensor_copy(cols[:, 40:80], g(2)[:, 0:40]).then_inc(log_dve, 1)

            def tap_of(n):
                tp = tap[:].rearrange("p (h c) -> p h c", h=H)
                return tp[:, n] if isinstance(n, int) else \
                    tp[:, bass.ds(n, 1)].rearrange("p a c -> p (a c)")

            def conf_taps(h, a, b):
                ge = v["gext"]
                out_s = v["c31"][:, SEQ:TOK].rearrange("p (s t) -> p s t", s=NS)
                for t in range(a, b):
                    w = ct[:, t:t + 1]
                    if t == 0:
                        ve.tensor_scalar(v["c31"][:, 0:SEQ], ge[:, 0:SEQ], w, None, ALU.mult).then_inc(conv31, 1)
                        ve.tensor_scalar(out_s, seqs(ge, GXT, GXS, 0, LS), w, None, ALU.mult).then_inc(conv31, 1)
                        continue
                    dve.wait_ge(conv31, 62 * h + 2 * t - 1)
                    stt(v["c31"][:, 0:SEQ], ge[:, t:t + SEQ], w, v["c31"][:, 0:SEQ], ALU.mult,
                        ALU.add).then_inc(conv31, 1)
                    dve.wait_ge(conv31, 62 * h + 2 * t)
                    r = stt(out_s, seqs(ge, GXT, GXS, t, LS), w, out_s, ALU.mult, ALU.add)
                    r.then_inc(conv31, 1)

            def qkv_conv(n, i):
                e, c4 = EXTS[i], v["c4"]
                out_s = c4[:, SEQ:TOK].rearrange("p (s t) -> p s t", s=NS)
                dve.wait_ge(act_read, 8 * n + (3 if first(n) else -2) + i)
                dve.wait_ge(halo_used, 4 * n + 1 + i)
                if i == 0:
                    dve.wait_ge(gext_ready, n + 1 if first(n) else n)
                else:
                    dve.wait_ge(act_conv, 3 * n + i)
                for t in range(QK_TAPS):
                    w = qt[:, QK_TAPS * i + t:QK_TAPS * i + t + 1]
                    if t == 0:
                        ve.tensor_scalar(c4[:, 0:SEQ], e[:, 0:SEQ], w, None, ALU.mult).then_inc(conv4, 1)
                        ve.tensor_scalar(out_s, seqs(e, EXT, EXS, 0, LS), w, None, ALU.mult).then_inc(conv4, 1)
                        continue
                    dve.wait_ge(conv4, 24 * n + 8 * i + 2 * t - 1)
                    stt(c4[:, 0:SEQ], e[:, t:t + SEQ], w, c4[:, 0:SEQ], ALU.mult, ALU.add).then_inc(conv4, 1)
                    dve.wait_ge(conv4, 24 * n + 8 * i + 2 * t)
                    r = stt(out_s, seqs(e, EXT, EXS, t, LS), w, out_s, ALU.mult, ALU.add)
                    r.then_inc(conv4, 1)
                dve.wait_ge(conv4, 24 * n + 8 * i + 8)
                dve.sem_inc(conv4_done, 1)

            def phase(n):
                gdn, proj = not first(n), not last(n)
                t2 = STEPS_1
                if gdn:
                    if isinstance(n, int):
                        src = cols[:].rearrange("p (a h) -> p a h", h=H)[:, :, n - 1:n]
                    else:
                        src = cols[:].rearrange("p (a h) -> p a h", h=H)[:, :, bass.ds(n - 1, 1)]
                    dve.wait_ge(cols_ready, 2)
                    ve.tensor_copy(hc[:].unsqueeze(2), src).then_inc(hc_ready, 1)
                for s in range(32):
                    if gdn and (s < 17 if last(n) else s < 20 and s not in (4, 8, 12)):
                        conf_taps(n - 1, t2, t2 + 1)
                        t2 += 1
                        if t2 == CF_TAPS:
                            dve.wait_ge(conv31, 62 * n)
                            dve.sem_inc(conv31_done, 1)
                    if gdn and proj and s == 4:
                        ve.tensor_copy(qt[:], tap_of(n)[:, 0:3 * QK_TAPS]).then_inc(taps_cur, 1)
                        dve.wait_ge(taps_cur, 2 * n + 1)
                    if proj and s == (21 if gdn else 20):
                        if gdn:
                            dve.wait_ge(conf_ready, n)
                        else:
                            dve.wait_ge(taps_landed, 16)
                        if first(n):
                            ve.tensor_copy(qt[:], tap_of(n)[:, 0:3 * QK_TAPS]).then_inc(taps_cur, 1)
                        ve.tensor_copy(ct[:], tap_of(n)[:, 3 * QK_TAPS:TAPW]).then_inc(taps_cur, 1)
                        dve.wait_ge(taps_cur, 2 * n + 2)
                        dve.wait_ge(gext_ready, n + 1)
                    own = (21, 22, 23, 26, 27, 30, 31) if first(n) else (22, 23, 24, 25, 26, 28, 30)
                    if proj and s in own:
                        i = own.index(s)
                        conf_taps(n, 2 * i, 2 * i + 2)
                    if proj and s in conv_slots(n, 0):
                        qkv_conv(n, conv_slots(n, 0).index(s))
                    if first(n) and s == 20:
                        logits()
                    if last(n) and 22 <= s < 30:
                        k = s - 22
                        if k == 0:
                            dve.wait_ge(mu_ready, 1)
                        tt(conf[:, k], conf[:, k], csum[:], ALU.subtract).then_inc(xc_ready, 1)
                    if not gdn:
                        continue
                    if s == 0:
                        dve.wait_ge(kq_scale, 4 * n - 2)
                        tt(v["kn"], v["kc"], v["at"], ALU.mult).then_inc(kq_ready, 1)
                        dve.wait_ge(kq_scale, 4 * n)
                        tt(v["qn"], v["qc"], v["ui"], ALU.mult).then_inc(kq_ready, 1)
                    if s == 2:
                        dve.wait_ge(k_tr, n)
                        dve.wait_ge(hc_ready, n)
                        tt(pr(v["gk"]), g4(0), hcol(EGAM), ALU.mult)
                        tt(pr(v["ko"]), g4(0), hcol(KOF), ALU.mult)
                        tt(smw(v["gk"]), g(2)[0:SMP, 0:P], hcol_s(EGAM, P), ALU.mult)
                        tt(smw(v["ko"]), g(2)[0:SMP, 0:P], hcol_s(KOF, P), ALU.mult).then_inc(gk_ready, 1)
                    if s == 3:
                        dve.wait_ge(gam_ps, n)
                        dve.wait_ge(gm_ready, n)
                        tt(v["dm"][:, 0:SEQ], g(1), v["qk"][:, 0:SEQ], ALU.subtract)
                        tt(sm(v["dm"]), g(3)[0:SMP, 0:SMP], sm(v["qk"]), ALU.subtract).then_inc(dm_diff, 1)
                    if s == 5:
                        dve.wait_ge(kk_ps, n)
                        dve.wait_ge(db_ready, n)
                        tt(v["at"][:, 0:SEQ], g(0), v["db"][:, 0:SEQ], ALU.mult)
                        tt(sm(v["at"]), g(2)[0:SMP, 0:SMP], sm(v["db"]), ALU.mult).then_inc(at_ready, 1)
                        dve.wait_ge(qk_ps, n)
                        tt(v["qk"][:, 0:SEQ], g(1), v["dm"][:, 0:SEQ], ALU.mult)
                        tt(sm(v["qk"]), g(3)[0:SMP, 0:SMP], sm(v["dm"]), ALU.mult).then_inc(qk_ready, 1)
                    if s == 7:
                        dve.wait_ge(c_tr, n)
                        dve.wait_ge(qk_ready, n)
                        tt(pr(v["dm"]), con("ident").unsqueeze(1).to_broadcast([P, TILES, P]), g4(0),
                           ALU.subtract)
                        tt(sm(v["dm"]), con("ident", SMP)[:, 0:SMP], g(2)[0:SMP, 0:SMP],
                           ALU.subtract).then_inc(t_ready, 1)
                    if s in (10, 12, 14, 16, 18, 20):
                        l = (s - 6) // 2
                        if l < LEVELS:
                            dve.wait_ge(dt_ps, 5 * n - 6 + l)
                            dve.wait_ge(t_ready, 6 * n - 7 + l)
                            r = tt(v["dm"][:, 0:SEQ], v["dm"][:, 0:SEQ], g(0), ALU.subtract)
                            if l < LEVELS_S:
                                r = tt(sm(v["dm"]), sm(v["dm"]), g(2)[0:SMP, 0:SMP], ALU.subtract)
                            r.then_inc(t_ready, 1)
                        dve.wait_ge(du_ps, 6 * n - 7 + l)
                        if l > 2:
                            dve.wait_ge(ui_ready, 6 * n - 8 + l)
                        else:
                            dve.wait_ge(u0_ready, n)
                        r = tt(v["ui"][:, 0:SEQ], v["ui"][:, 0:SEQ], g(1), ALU.subtract)
                        if l <= LEVELS_S:
                            r = tt(sm(v["ui"]), sm(v["ui"]), g(3)[0:SMP, 0:SMP], ALU.subtract)
                        r.then_inc(ui_ready, 1)
                    if s in (22, 24, 26, 28):
                        c = (s - 22) // 2
                        dve.wait_ge(s_ps, TILES * n - 3 + c)
                        if c == 0:
                            dve.wait_ge(ss_landed, 16 * n)
                            ve.tensor_copy(v["s"], g(0)[:, 0:P]).then_inc(s_ready, 1)
                        else:
                            dve.wait_ge(s_ready, TILES * n - 4 + c)
                            stt(v["s"], v["s"], v["eg"][:, c * P + P - 1:c * P + P], g(0)[:, 0:P],
                                ALU.mult, ALU.add).then_inc(s_ready, 1)
                    if s == 29:
                        dve.wait_ge(ss_ps, n)
                        dve.wait_ge(ss_decayed, n)
                        tt(v["ss"], v["ss"], ps[:, 4:6, :].rearrange("p a b -> p (a b)"),
                           ALU.add).then_inc(ss_ready, 1)
                    if s == 31:
                        dve.wait_ge(o_scale, n)
                        o = o_a[:, n - 1] if isinstance(n, int) else \
                            o_a[:, bass.ds(n - 1, 1)].rearrange("p a b -> p (a b)")
                        tt(v["db"], o, v["at"], ALU.mult).then_inc(o_scaled, 1)
                        dve.wait_ge(o_scaled, n)
                        dve.wait_ge(zs_ready, n + 1)
                        stt(o, v["db"], pcol("delta_g", 0), v["zs"], ALU.mult, ALU.mult).then_inc(head_out, 1)
                if first(n):
                    qkv_conv(n, 2)

            phase(0)
            with dve.Fori(1, H) as n:
                phase(n)
            phase(H)
            dve.wait_ge(ln_scale, 2)
            for k in range(KB):
                tt(conf[:, k], conf[:, k], v["c31"], ALU.mult).then_inc(ln_scaled, 1)
            for k in range(KB):
                dve.wait_ge(b_gated, k + 1)
                tt(conf[:, k], conf[:, k], o_a[:, k], ALU.add).then_inc(mixed, 1)
                if k:
                    dve.wait_ge(high_ready, 8 + k)
                    tt(in_lo[:, k - 1], conf[:, k - 1], in_hi[:, k - 1].bitcast(F32),
                       ALU.subtract).then_inc(in_ready, 1)
            dve.wait_ge(high_ready, 16)
            tt(in_lo[:, 7], conf[:, 7], in_hi[:, 7].bitcast(F32), ALU.subtract).then_inc(in_ready, 1)
            dve.wait_ge(mixed, 8)
            for k in range(KB):
                ve.memset(o_a[:, k], 0.0).then_inc(dve_read, 1)

            dve.wait_ge(ms_scale, 2)
            dve.wait_ge(x_again, 16)
            dve.wait_ge(act_read, 72)
            dve.wait_ge(job_done, 72)
            for k in range(KB):
                tt(gate[:, k], gate[:, k], v["c31"], ALU.mult).then_inc(y_scaled, 1)
                dve.wait_ge(y_scaled, k + 1)
                stt(conf[:, k], gate[:, k], pcol("post_mix", k), xt[:, k], ALU.mult,
                    ALU.add).then_inc(mid_ready, 1)
                if k:
                    dve.wait_ge(high_ready, 16 + k)
                    stt(in_lo[:, k - 1], conf[:, k - 1], pcol("pre_ffn", k - 1),
                        in_hi[:, k - 1].bitcast(F32), ALU.mult, ALU.subtract).then_inc(in_ready, 1)
            dve.wait_ge(high_ready, 24)
            stt(in_lo[:, 7], conf[:, 7], pcol("pre_ffn", 7), in_hi[:, 7].bitcast(F32),
                ALU.mult, ALU.subtract).then_inc(in_ready, 1)

            def group(gr):
                for j in range(8):
                    dve.wait_ge(act_read, 8 * gr + 73 + j)
                    tt(f_tmp[:, 2 + j % 2], f_tmp[:, j % 2], f_tmp[:, j % 2], ALU.mult).then_inc(f_square, 1)
                    dve.wait_ge(f_square, 8 * gr + 3 + j)
                    dve.wait_ge(f_high, 8 * gr + 1 + j)
                    tt(f_lo[:, j], f_tmp[:, 2 + j % 2], f_hi[:, j].bitcast(F32),
                       ALU.subtract).then_inc(f_ready, 1)
                for j in range(8):
                    dve.wait_ge(job_done, 16 * gr + 81 + j)
                    tt(two(o_a[:, j]), two(o_a[:, j]), job_ps(j % 2), ALU.add).then_inc(dve_read, 1)

            with dve.Fori(0, FFN_GROUPS) as gr:
                group(gr)

            dve.wait_ge(ms2_log, 2)
            dve.wait_ge(ms3_ps, 1)
            tt(two(gate[:, 3]), g2(2), two(gate[:, 2]), ALU.mult).then_inc(var3, 1)
            dve.wait_ge(ms3_log, 1)
            stt(gate[:, 4], gate[:, 3], 0.5, gate[:, 1], ALU.mult, ALU.add).then_inc(expo, 1)
            dve.wait_ge(out_scale, 1)
            for k in range(KB):
                tt(o_a[:, k], o_a[:, k], gate[:, 4], ALU.mult).then_inc(out_scaled, 1)
                dve.wait_ge(out_scaled, k + 1)
                stt(o_a[:, k], o_a[:, k], pcol("post_ffn", k), conf[:, k], ALU.mult,
                    ALU.add).then_inc(y_ready, 1)

        @block.gpsimd
        def _(pool):
            gp = nc.gpsimd

            def tt(out, a, b, op):
                return gp.tensor_tensor(out, a, b, op)

            def split(m, off):
                pool.wait_ge(w_high, 8 * m + off + 1)
                tt(w_lo[:, off % 2], raw[:, off % RING], w_hi[:, off % 2].bitcast(F32),
                   ALU.subtract).then_inc(w_low, 1)

            pool.wait_ge(consts_landed, 32)
            split(0, 0)

            def bc(ap):
                return ap.unsqueeze(1).to_broadcast([P, TILES, P])

            def level(n, l):
                c = C[(l - 1) % 2]
                if l == 3:
                    pool.wait_ge(c_tr, n)
                if l > 3:
                    pool.wait_ge(x_ps, 6 * n - 9 + l)
                r = tt(pr(c), pr(v["at"]), lvl(l), ALU.mult)
                if l <= LEVELS_S:
                    r = tt(sm(c), sm(v["at"]), lvl_s(l), ALU.mult)
                r.then_inc(c_ready, 1)

            def phase(n):
                gdn, proj = not first(n), not last(n)
                if gdn:
                    pool.wait_ge(hc_ready, n)
                    tt(pr(v["dm"]), bc(con("tri")), hcol(G), ALU.mult)
                    tt(sm(v["dm"]), con("tri_s", SMP), hcol_s(G, SMP), ALU.mult).then_inc(gtri_ready, 1)
                    tt(pr(v["qk"]), bc(con("big")), hcol(GAM), ALU.add)
                    tt(sm(v["qk"]), con("big_s", SMP), hcol_s(GAM, SMP), ALU.add).then_inc(gm_ready, 1)
                for s in range(33):
                    off = split_off(n, s)
                    if off is not None:
                        split(n, off)
                    pos, j = evac(n, s)
                    if j == GA:
                        pool.wait_ge(act_read, 8 * n - 2 + pos)
                        tt(v["zs"], v["zs"], v["sig"], ALU.mult).then_inc(zs_ready, 1)
                    if proj and s == (20 if first(n) else 2):
                        pool.wait_ge(halo_landed, 16 * n + 16)
                        if gdn:
                            pool.wait_ge(conv4_done, 3 * n)
                        pool.nop(nofuse=True)
                        for i in range(3):
                            gp.tensor_copy(seqs(EXTS[i], EXT, EXS, 0, QK_TAPS - 1),
                                           halo[:, 24 * i:24 * i + 24].rearrange("p (s t) -> p s t", s=NS)
                                           ).then_inc(halo_used, 1)
                    if j == CB:
                        ge = v["gext"]
                        if gdn:
                            pool.wait_ge(conv31_done, n)
                            pool.nop(nofuse=True)
                        gp.tensor_copy(seqs(ge, GXT, GXS, 0, CF_TAPS - 1),
                                       halo[:, 72:HALO].rearrange("p (s t) -> p s t", s=NS)).then_inc(halo_used, 1)
                        pool.wait_ge(act_read, 8 * n - 2 + pos)
                        tt(ge[:, CF_TAPS - 1:GXT], v["c4"][:, 0:SEQ], v["sig"][:, 0:SEQ], ALU.mult)
                        tt(seqs(ge, GXT, GXS, CF_TAPS - 1, LS),
                           v["c4"][:, SEQ:TOK].rearrange("p (s t) -> p s t", s=NS),
                           v["sig"][:, SEQ:TOK].rearrange("p (s t) -> p s t", s=NS),
                           ALU.mult).then_inc(gext_ready, 1)
                        pool.wait_ge(gext_ready, n + 1)
                        pool.wait_ge(halo_used, 4 * n + 4)
                        if gdn:
                            pool.wait_ge(crows_stored, 16 * n)
                        pool.nop(nofuse=True)
                        gp.tensor_copy(c_rows[:, 0:CF_TAPS - 1], ge[:, GXT - CF_TAPS + 1:GXT])
                        gp.tensor_copy(c_rows[:, CF_TAPS - 1:].rearrange("p (s t) -> p s t", s=NS),
                                       seqs(ge, GXT, GXS, LS, CF_TAPS - 1)).then_inc(crows_ready, 1)
                    if j is not None and j >= Q:
                        i = j - Q
                        pool.wait_ge(act_read, 8 * n - 2 + pos)
                        if gdn and i == 0:
                            pool.wait_ge(qrows_stored, 16 * n)
                        pool.nop(nofuse=True)
                        gp.tensor_copy(q_rows[:, 27 * i:27 * i + 3], EXTS[i][:, EXT - 3:EXT])
                        gp.tensor_copy(q_rows[:, 27 * i + 3:27 * i + 27].rearrange("p (s t) -> p s t", s=NS),
                                       seqs(EXTS[i], EXT, EXS, LS, 3)).then_inc(qrows_ready, 1)
                    if gdn and s == (18 if last(n) else 21):
                        pool.wait_ge(conf_ready, n)
                        if isinstance(n, int):
                            src = conf[:, n - 1]
                        else:
                            src = conf[:, bass.ds(n - 1, 1)].rearrange("p a b -> p (a b)")
                        pool.wait_ge(csum_done, n)
                        tt(csum[:], csum[:], src, ALU.add).then_inc(csum_done, 1)
                    if not gdn:
                        continue
                    if s == 3:
                        pool.wait_ge(dm_ready, n)
                        tt(pr(v["db"]), pr(v["dm"]), hcol(BETA), ALU.mult)
                        tt(sm(v["db"]), sm(v["dm"]), hcol_s(BETA, SMP), ALU.mult).then_inc(db_ready, 1)
                    if s == 5:
                        pool.wait_ge(at_ready, n)
                        level(n, 1)
                        level(n, 2)
                    if s == 6:
                        pool.wait_ge(c_ready, 7 * n - 6)
                        tt(pr(v["ui"]), bc(con("ident")), pr(C[0]), ALU.subtract)
                        tt(sm(v["ui"]), con("ident", SMP)[:, 0:SMP], sm(C[0]), ALU.subtract).then_inc(u0_ready, 1)
                        pool.wait_ge(qk_ps, n)
                        tt(v["qn"], v["qn"], v["eg"], ALU.mult).then_inc(qd_ready, 1)
                    if s == 8:
                        pool.wait_ge(u0_ready, n)
                        level(n, 3)
                    if s in (10, 12, 14, 16):
                        level(n, s // 2 - 1)
                    if s == 22:
                        pool.wait_ge(kd_ready, 2 * n)
                        tt(v["um"][:, 0:NS * SMP].rearrange("p (q t) -> p q t", q=NS),
                           sm(v["kn"], P).unsqueeze(1).to_broadcast([P, NS, SMP]),
                           con("colm").rearrange("p (q t) -> p q t", q=NS), ALU.mult).then_inc(kdm_ready, 1)
                    if s == 25:
                        pool.wait_ge(us_ready, n)
                        tt(v["um"][0:SMP, :].rearrange("p (q c) -> p q c", q=NS),
                           smw(v["u"]).unsqueeze(1).to_broadcast([SMP, NS, P]),
                           con("rowm", SMP).unsqueeze(2).to_broadcast([SMP, NS, P]),
                           ALU.mult).then_inc(um_ready, 1)
                    if s == 28:
                        pool.wait_ge(o_ps, n)
                        tt(v["ss"].rearrange("p (q c) -> p q c", q=NS),
                           v["ss"].rearrange("p (q c) -> p q c", q=NS),
                           v["eg"][:, SEQ + LS - 1:TOK:LS].unsqueeze(2).to_broadcast([P, NS, P]),
                           ALU.mult).then_inc(ss_decayed, 1)

            phase(0)
            with pool.Fori(1, H) as n:
                phase(n)
            phase(H)
            for k in range(KB):
                pool.wait_ge(b_silu, k + 1)
                tt(conf[:, k], conf[:, k], gate[:, k], ALU.mult).then_inc(b_gated, 1)

            for j in range(8):
                split(8, j + 1)
                pool.wait_ge(y_sq, j + 1)
                src = v[("c4", "extq")[j % 2]][:, 0:TOK]
                if j:
                    pool.wait_ge(y_sum, j)
                    tt(csum[:], csum[:], src, ALU.add).then_inc(y_sum, 1)
                else:
                    gp.tensor_copy(csum[:], src).then_inc(y_sum, 1)
            pool.wait_ge(ms_ps, 1)
            for k in range(KB):
                pool.wait_ge(mid_sq, k + 1)
                src = v[("sig", "zs")[k % 2]]
                if k:
                    pool.wait_ge(mid_sum, k)
                    tt(csum[:], csum[:], src, ALU.add).then_inc(mid_sum, 1)
                else:
                    gp.tensor_copy(csum[:], src).then_inc(mid_sum, 1)

            def group(gr, tail=False):
                m = 2 * gr + 9
                for j in range(8):
                    split(m, j + 1)
                for j in range(8):
                    if not (tail and j == 7):
                        split(m + 1, j + 1)
                    if tail:
                        pool.wait_ge(out_sq, j + 1)
                        src = v[("sig", "zs")[j % 2]]
                        if j:
                            pool.wait_ge(out_sum, j)
                            tt(gate[:, 5], gate[:, 5], src, ALU.add).then_inc(out_sum, 1)
                        else:
                            gp.tensor_copy(gate[:, 5], src).then_inc(out_sum, 1)

            with pool.Fori(0, FFN_GROUPS - 1) as gr:
                group(gr)
            group(FFN_GROUPS - 1, tail=True)


def shape_constants():
    i, j = np.indices((P, P))
    a, b = np.indices((SMP, SMP))
    same = a // LS == b // LS
    out = np.zeros((P, CONSTS), np.float32)

    def put(nm, value, at=0):
        o = OFF[nm][0] + at
        out[:value.shape[0], o:o + value.shape[1]] = value

    def half(r, c, n):
        return (r // (2 * n) == c // (2 * n)) & (r // n < c // n)

    put("ident", i == j)
    put("ones", np.ones((P, P)))
    put("tri", i <= j)
    put("suf", i > j)
    put("big", np.where(j < i, BIG, 0))
    put("tri_s", same & (a <= b))
    put("suf_s", same & (a > b))
    put("big_s", np.where(same & (b >= a), 0, BIG))
    for l in range(LEVELS):
        put("lvl", half(i, j, 2 ** l), l * P)
    for l in range(LEVELS_S):
        put("lvl_s", half(a, b, 2 ** l), l * SMP)
    for q in range(NS):
        put("colm", np.tile(np.arange(SMP) // LS == q, (P, 1)), q * SMP)
    put("rowm", np.arange(SMP)[:, None] // LS == np.arange(NS)[None, :])
    put("eps", np.full((P, 1), EPS))
    put("eps128", np.full((P, 1), P * EPS))
    return out


def channels(a):
    a = a.reshape(a.shape[:-1] + (-1, P))
    return np.moveaxis(a, (-1, -2), (0, 1))


def job_weights(w):
    return w.reshape(KB, P, -1, P).transpose(2, 1, 0, 3)


_OUTS = [("y", (P, KB, TOK)), ("s_prompt", (H, P, P)), ("s_sample", (H, P, NS * P)),
         ("qkv_rows", (H, P, 81)), ("conf_rows", (H, P, 9 * (CF_TAPS - 1)))]


def kernel(x_prompt, x_sample, state_delta, state_qkv_conv, state_conf_conv, w_in, conv_qkv_w,
           a_log, dt_bias, delta_norm_g, conf_dw_w, conf_dw_b, conf_ln_g, conf_ln_b, w_out,
           g_pre_mix, g_post_mix, g_pre_ffn, g_post_ffn, w_up, w_down):
    import concourse.bacc as bacc
    from concourse.bass_utils import run_bass_kernel_spmd

    f = lambda a: np.ascontiguousarray(np.asarray(a))
    x = np.concatenate([f(x_prompt)[0], f(x_sample).reshape(SMP, D)], 0)
    wi = f(w_in)[0]
    o1 = 3 * D
    o2 = o1 + 2 * H
    qkv = job_weights(wi[:, :o1])
    rest = job_weights(wi[:, o2:])
    z, ca, cb, ga, gb = (rest[8 * i:8 * i + 8] for i in range(5))
    parts = []
    for n in range(H + 1):
        for kind in (FIRST if n == 0 else LAST if n == H else MIDDLE).values():
            parts.append({Z: z, GA: ga, GB: gb}[kind][n - 1] if kind <= GB else
                         {CA: ca, CB: cb, Q: qkv, K: qkv[H:], V: qkv[2 * H:]}[kind][n])
    parts += list(job_weights(f(w_out)[0]))
    up = job_weights(f(w_up)[0])
    down = f(w_down)[0]
    for gr in range(FFN_GROUPS):
        parts += list(up[8 * gr:8 * gr + 8])
        parts += list(job_weights(down[D * gr:D * gr + D]))
    w_all = np.stack(parts)

    par = np.zeros((P, len(PARAMS), KB), np.float32)
    for i, a in enumerate((g_pre_mix, g_post_mix, g_pre_ffn, g_post_ffn, conf_ln_g, conf_ln_b)):
        par[:, i] = channels(f(a)[0])
    par[:, 6, 0] = f(delta_norm_g)[0]
    cq = channels(f(conv_qkv_w)[0]).reshape(P, 3, H, QK_TAPS).transpose(0, 2, 1, 3).reshape(P, H, 12)
    taps = np.concatenate([cq, channels(f(conf_dw_w)[0]), channels(f(conf_dw_b)[0])[:, :, None]], 2)
    hq = channels(f(state_qkv_conv)[0]).reshape(P, 3, H, 24).transpose(2, 0, 1, 3).reshape(H, P, 72)
    hf = channels(f(state_conf_conv)[0]).reshape(P, H, 240).transpose(1, 0, 2)
    halos = np.concatenate([hq, hf], 2)
    halos = np.concatenate([halos, np.zeros((1, P, HALO), np.float32)], 0)
    arrays = {
        "x_t": channels(x).reshape(P, KB, TOK),
        "w_all": w_all,
        "w_log": wi[:, o1:o2].reshape(KB, P, 2 * H).transpose(1, 0, 2).reshape(P, KB * 2 * H),
        "log_par": np.tile(np.concatenate([f(dt_bias)[0], f(a_log)[0]])[None], (P, 1)),
        "consts": shape_constants(),
        "params": par.reshape(P, -1),
        "taps": taps.reshape(P, -1),
        "halos": halos,
        "s_in": f(state_delta)[0].transpose(1, 2, 0, 3).reshape(H, P, NS * P),
    }
    nc = bacc.Bacc("TRN2", target_bir_lowering=False, num_devices=1)
    arrays = {k + "_in": np.ascontiguousarray(a) for k, a in arrays.items()}
    args = [nc.dram_tensor(k, a.shape, mybir.dt.from_np(a.dtype), kind="ExternalInput").ap()
            for k, a in arrays.items()]
    args += [nc.dram_tensor(k + "_out", s, F32, kind="ExternalOutput").ap() for k, s in _OUTS]
    build(nc, *args)
    res = run_bass_kernel_spmd(nc, [arrays], core_ids=[0]).results[0]
    y, sp, ss, qr, cr = (np.asarray(res[k + "_out"]) for k, _ in _OUTS)
    y = y.transpose(2, 1, 0).reshape(TOK, D)
    qr = qr.reshape(H, P, 3, 27).transpose(3, 2, 0, 1).reshape(27, 3 * D)
    cr = cr.reshape(H, P, 9, CF_TAPS - 1).transpose(2, 3, 0, 1).reshape(9, CF_TAPS - 1, D)
    return (y[:SEQ].reshape(1, SEQ, D), y[SEQ:].reshape(NS, LS, D), sp.reshape(1, 1, H, P, P),
            qr[:3].reshape(1, 1, 3, 3 * D), cr[:1].reshape(1, 1, CF_TAPS - 1, D),
            ss.reshape(H, P, NS, P).transpose(2, 0, 1, 3).reshape(1, NS, H, P, P),
            qr[3:].reshape(1, NS, 3, 3 * D), cr[1:].reshape(1, NS, CF_TAPS - 1, D))
```

```python
from contextlib import ExitStack

import numpy as np

import concourse.bass as bass
import concourse.mybir as mybir

F32 = mybir.dt.float32
F32R = mybir.dt.float32r
BF16 = mybir.dt.bfloat16
ACT = mybir.ActivationFunctionType
ALU = mybir.AluOpType

P = 128
D = 1024
H = 8
KB = D // P
SEQ = 512
NS, LS = 8, 8
SMP = NS * LS
TOK = SEQ + SMP
HALF = TOK // 2
TILES = SEQ // P
QK_TAPS, CF_TAPS = 4, 31
EXT = SEQ + QK_TAPS - 1
EXS = LS + QK_TAPS - 1
GXT = SEQ + CF_TAPS - 1
GXS = LS + CF_TAPS - 1
EPS = 1e-6
BIG = 1e30
FFN_GROUPS = 4
PROJ_JOBS = 8 * H
OUT_JOB0 = PROJ_JOBS
FFN_JOB0 = PROJ_JOBS + H
JOBS = FFN_JOB0 + FFN_GROUPS * 2 * H
RING = 4
LEVELS = 7
STEPS = LEVELS + 1
LEVELS_S = 3
STEPS_1 = 20
Z, GA, GB, CA, CB, Q, K, V = range(8)
FIRST = {3: CA, 4: CB, 5: Q, 6: K, 7: V}
MIDDLE = {0: Q, 1: K, 2: V, 3: CA, 4: CB, 5: Z, 6: GA, 7: GB}
LAST = {0: Z, 1: GA, 2: GB}
LAST_SEGS = (0, 3, 6, 8, 10, 12, 14, 16, 18, 21, 24, 27)

_LAYOUT = [("ident", P), ("ones", P), ("tri", P), ("suf", P), ("tri_s", SMP), ("suf_s", SMP),
           ("eps", 1), ("eps128", 1), ("big", P), ("big_s", SMP), ("lvl", LEVELS * P),
           ("lvl_s", LEVELS_S * SMP), ("strict", P), ("colm", NS * SMP), ("rowm", NS)]
OFF, _o = {}, 0
for _n, _w in _LAYOUT:
    OFF[_n] = (_o, _o + _w)
    _o += _w
CONSTS = _o
WIDE = OFF["big"][0]
PARAMS = ["pre_mix", "post_mix", "pre_ffn", "post_ffn", "ln_g", "ln_b", "delta_g"]
TAPW = 3 * QK_TAPS + CF_TAPS + 1
HALO = 3 * NS * (QK_TAPS - 1) + NS * (CF_TAPS - 1)


def build(nc, x_t, w_all, w_log, log_par, consts, params, taps, halos, s_in,
          y_out, s_prompt, s_sample, qkv_rows, conf_rows):
    with ExitStack() as ctx:
        def sb(name, width, dt=F32):
            return ctx.enter_context(nc.sbuf_tensor(name, [P, width], dt))

        def sem(name):
            return ctx.enter_context(nc.semaphore(name))

        names = [("kn", TOK), ("qn", TOK), ("eg", TOK), ("dm", TOK), ("db", TOK), ("at", TOK),
                 ("qk", TOK),
                 ("gk", SEQ + P), ("ko", SEQ + P), ("vt", SEQ + P), ("u", SEQ + P),
                 ("s", P), ("ss", NS * P), ("um", NS * P),
                 ("extq", EXT + NS * EXS), ("extk", EXT + NS * EXS), ("extv", EXT + NS * EXS),
                 ("gext", GXT + NS * GXS), ("c4", TOK), ("c31", TOK),
                 ("qc", TOK), ("kc", TOK), ("vc", TOK),
                 ("us", SMP), ("cs0", SMP), ("cs1", SMP), ("sig", TOK), ("zs", TOK)]
        work_at = -(-nc.sbuf_base // 32) * 32
        c_r, x_r = (sb("c0_r", SEQ, F32R), sb("c1_r", SEQ, F32R)), sb("x_r", SEQ, F32R)
        t_r, u_r = sb("t_r", SEQ, F32R), sb("u_r", SEQ, F32R)
        work = sb("work", sum(w for _, w in names))
        at, v = 0, {}
        for nm, w in names:
            v[nm] = work[:, at:at + w]
            at += w
        xt = nc.alloc_sbuf_tensor_at("xt", [P, KB, TOK], F32, offset=work_at)
        f_hi = nc.alloc_sbuf_tensor_at("f_hi", [P, KB, TOK], F32R, offset=work_at + 4 * KB * TOK)
        f_lo = nc.alloc_sbuf_tensor_at("f_lo", [P, KB, TOK], F32R, offset=work_at + 8 * KB * TOK)
        f_tmp = nc.alloc_sbuf_tensor_at("f_tmp", [P, 4, TOK], F32, offset=work_at + 12 * KB * TOK)


        def blocks(name, dt=F32):
            return ctx.enter_context(nc.sbuf_tensor(name, [P, KB, TOK], dt))

        in_hi, in_lo = blocks("in_hi", F32R), blocks("in_lo", F32R)
        o_a = blocks("o_a")
        gate = blocks("gate")
        conf = blocks("conf")
        raw = ctx.enter_context(nc.sbuf_tensor("raw", [P, RING, KB, P], F32))
        w_hi = ctx.enter_context(nc.sbuf_tensor("w_hi", [P, 2, KB, P], F32R))
        w_lo = ctx.enter_context(nc.sbuf_tensor("w_lo", [P, 2, KB, P], F32R))
        cst, masks = sb("cst", WIDE), sb("masks", CONSTS - WIDE, BF16)
        par = sb("par", len(PARAMS) * KB)
        tap = sb("tap", KB * TAPW)
        halo = sb("halo", HALO)
        lpar = sb("lpar", 2 * H)
        wlog = sb("wlog", KB * 2 * H)
        cols = sb("cols", 5 * 5 * H)
        hc = sb("hc", 25)
        qt, ct = sb("qt", 3 * QK_TAPS), sb("ct", CF_TAPS + 1)
        q_rows, c_rows = sb("q_rows", 3 * 27), sb("c_rows", 9 * (CF_TAPS - 1))
        csum = sb("csum", TOK)
        ps = ctx.enter_context(nc.psum_tensor("ps", [P, 8, 512], F32))

        mask_in = gate[:].rearrange("p k t -> p (k t)")[:, 0:CONSTS - WIDE]

        def con(nm, rows=P):
            a, b = OFF[nm]
            return cst[0:rows, a:b] if b <= WIDE else masks[0:rows, a - WIDE:b - WIDE]

        def lvl(l):
            a = OFF["lvl"][0] - WIDE + (l - 1) * P
            return masks[:, a:a + P].unsqueeze(1).to_broadcast([P, TILES, P])

        def lvl_s(l):
            a = OFF["lvl_s"][0] - WIDE + (l - 1) * SMP
            return masks[0:SMP, a:a + SMP]

        def pcol(nm, k):
            a = PARAMS.index(nm) * KB + k
            return par[:, a:a + 1]

        def job_ps(j2):
            return ps[:, 2 * j2:2 * j2 + 2, 0:HALF]

        def g(i):
            return ps[:, 4 + i, :]

        def g2(i):
            return ps[:, 4 + i:6 + i, 0:HALF]

        def two(ap):
            return ap.rearrange("p (a b) -> p a b", a=2)

        def pr(ap):
            return ap[:, 0:SEQ].rearrange("p (a b) -> p a b", a=TILES)

        def tile(ap, c):
            return ap[:, c * P:c * P + P]

        def sm(ap, rows=SMP):
            return ap[0:rows, SEQ:SEQ + SMP]

        def smw(ap):
            return ap[0:SMP, SEQ:SEQ + P]

        def g4(i):
            return g(i).rearrange("p (a b) -> p a b", a=TILES)

        def hcol(kind):
            return hc[:, 5 * kind:5 * kind + TILES].unsqueeze(2).to_broadcast([P, TILES, P])

        def hcol_s(kind, width):
            return hc[0:SMP, 5 * kind + 4:5 * kind + 5].to_broadcast([SMP, width])

        def seqs(ap, first, width, start, n):
            return ap[:, first:first + NS * width].rearrange("p (s t) -> p s t", s=NS)[
                :, :, start:start + n]

        EXTS = (v["extq"], v["extk"], v["extv"])
        CONV = (v["qc"], v["kc"], v["vc"])
        G, GAM, EGAM, KOF, BETA = range(5)
        c_s = (v["cs0"], v["cs1"])
        u_all = v["dm"]

        raw_landed = [sem(f"raw_landed{r}") for r in range(RING)]
        consts_landed, x_landed, taps_landed = sem("consts_landed"), sem("x_landed"), sem("taps_landed")
        log_landed, halo_landed, ss_landed = sem("log_landed"), sem("halo_landed"), sem("ss_landed")
        x_again = sem("x_again")
        states_stored, crows_stored, qrows_stored = sem("states_stored"), sem("crows_stored"), sem("qrows_stored")
        y_stored = sem("y_stored")
        w_high, w_low, job_done = sem("w_high"), sem("w_low"), sem("job_done")
        act_read = sem("act_read")
        dve_read = sem("dve_read")
        in_ready = sem("in_ready")
        squares, sums, scale = sem("squares"), sem("sums"), sem("scale")
        x_scaled, high_ready = sem("x_scaled"), sem("high_ready")
        log_ps, log_zero, log_act, log_dve = sem("log_ps"), sem("log_zero"), sem("log_act"), sem("log_dve")
        cum_ps, cols_ready = sem("cum_ps"), sem("cols_ready")
        gext_ready, halo_used = sem("gext_ready"), sem("halo_used")
        conv4, conv4_done, act_conv = sem("conv4"), sem("conv4_done"), sem("act_conv")
        conv31, conv31_done, conf_ready, csum_done = sem("conv31"), sem("conv31_done"), sem("conf_ready"), sem("csum_done")
        taps_cur = sem("taps_cur")
        zs_ready = sem("zs_ready")
        crows_ready, qrows_ready = sem("crows_ready"), sem("qrows_ready")
        hc_ready, gtri_ready, gm_ready = sem("hc_ready"), sem("gtri_ready"), sem("gm_ready")
        kq_sq, kq_sums, kq_scale, kq_ready = sem("kq_sq"), sem("kq_sums"), sem("kq_scale"), sem("kq_ready")
        k_tr, v_tr, gk_ready, vt_ready = sem("k_tr"), sem("v_tr"), sem("gk_ready"), sem("vt_ready")
        gam_ps, kk_ps, qk_ps = sem("gam_ps"), sem("kk_ps"), sem("qk_ps")
        dm_diff, eg_ready, dm_ready, db_ready = sem("dm_diff"), sem("eg_ready"), sem("dm_ready"), sem("db_ready")
        at_ready, qk_ready, qd_ready, c_ready = sem("at_ready"), sem("qk_ready"), sem("qd_ready"), sem("c_ready")
        c_tr, t_ready, u0_ready, ui_ready = sem("c_tr"), sem("t_ready"), sem("u0_ready"), sem("ui_ready")
        x_ps, x_ready, dt_ps, du_ps = sem("x_ps"), sem("x_ready"), sem("dt_ps"), sem("du_ps")
        kd_ps, kd_ready, kdm_ready = sem("kd_ps"), sem("kd_ready"), sem("kdm_ready")
        u_ps, u_ready, s_ps, s_ready = sem("u_ps"), sem("u_ready"), sem("s_ps"), sem("s_ready")
        us_ps, us_ready, um_ready, os_ps = sem("us_ps"), sem("us_ready"), sem("um_ready"), sem("os_ps")
        o_ps, o_read, o_sq, o_sums = sem("o_ps"), sem("o_read"), sem("o_sq"), sem("o_sums")
        o_scale, o_scaled, ss_decayed, ss_ps = sem("o_scale"), sem("o_scaled"), sem("ss_decayed"), sem("ss_ps")
        ss_ready, head_out = sem("ss_ready"), sem("head_out")
        mu_ps, mu_ready, xc_ready, xc_sq = sem("mu_ps"), sem("mu_ready"), sem("xc_ready"), sem("xc_sq")
        var_ps = sem("var_ps")
        ln_scale, ln_scaled, b_silu, b_gated = sem("ln_scale"), sem("ln_scaled"), sem("b_silu"), sem("b_gated")
        mixed = sem("mixed")
        y_sq, y_sum, ms_ps, ms_scale = sem("y_sq"), sem("y_sum"), sem("ms_ps"), sem("ms_scale")
        y_scaled, mid_ready = sem("y_scaled"), sem("mid_ready")
        mid_sq, ms2_ps, ms2_log = sem("mid_sq"), sem("ms2_ps"), sem("ms2_log")
        f_ready, f_high = sem("f_ready"), sem("f_high")
        out_sq, ms3_ps, var3, ms3_log = sem("out_sq"), sem("ms3_ps"), sem("var3"), sem("ms3_log")
        expo, out_scale, out_scaled, y_ready = sem("expo"), sem("out_scale"), sem("out_scaled"), sem("y_ready")

        def last(n):
            return isinstance(n, int) and n == H

        def first(n):
            return isinstance(n, int) and n == 0

        def jobs(n):
            return FIRST if first(n) else LAST if last(n) else MIDDLE

        def done_slot(n, j):
            return (8, 16, 27)[j] if last(n) else 4 * j + 3

        mid_sum, out_sum = sem("mid_sum"), sem("out_sum")
        o_log, f_square, tmi_ready = sem("o_log"), sem("f_square"), sem("tmi_ready")
        masks_landed = sem("masks_landed")

        block = ctx.enter_context(nc.Block())

        @block.sync
        def _(sp):
            def weights(m, off, dst=None):
                j = 8 * m + off
                if not (isinstance(j, int) and j < RING):
                    sp.wait_ge(w_high, j - RING + 1)
                    sp.wait_ge(w_low, j - RING + 1)
                sp.dma_start(raw[:, off % RING], w_all[j] if isinstance(j, int) else
                             w_all[bass.ds(j, 1)].rearrange("a p k c -> p (a k) c")).then_inc(
                                 raw_landed[off % RING], 16)

            sp.dma_start(xt[:, 0:4], x_t[:, 0:4]).then_inc(x_landed, 16)
            sp.dma_start(xt[:, 4:8], x_t[:, 4:8]).then_inc(x_landed, 16)
            sp.dma_start(cst[:], consts[:, 0:WIDE]).then_inc(consts_landed, 16)
            sp.dma_start(par[:], params).then_inc(consts_landed, 16)
            weights(0, 0)
            sp.dma_start(tap[:], taps).then_inc(taps_landed, 16)
            sp.dma_start(mask_in, consts[:, WIDE:CONSTS]).then_inc(masks_landed, 16)
            sp.dma_start(lpar[:], log_par).then_inc(log_landed, 16)
            sp.dma_start(wlog[:], w_log).then_inc(log_landed, 16)
            for j in range(1, 5):
                weights(0, j)

            def phase(n):
                if first(n):
                    sp.dma_start(halo[:], halos[0]).then_inc(halo_landed, 16)
                for j in jobs(n):
                    weights(n, j + 2)
                if not last(n):
                    sp.wait_ge(halo_used, 4 * n + 4)
                    sp.dma_start(halo[:], halos[n + 1] if isinstance(n, int) else
                                 halos[bass.ds(n + 1, 1)].rearrange("a p c -> (a p) c")).then_inc(
                                     halo_landed, 16)
                    sp.wait_ge(crows_ready, n + 1)
                    sp.dma_start(conf_rows[n] if isinstance(n, int) else
                                 conf_rows[bass.ds(n, 1)].rearrange("a p c -> (a p) c"),
                                 c_rows[:]).then_inc(crows_stored, 16)
                if not first(n):
                    d = n - 1
                    sp.wait_ge(s_ready, TILES * n)
                    sp.dma_start(s_prompt[d] if isinstance(n, int) else
                                 s_prompt[bass.ds(d, 1)].rearrange("a p c -> (a p) c"),
                                 v["s"]).then_inc(states_stored, 16)
                    sp.wait_ge(ss_ready, n + 1)
                    sp.dma_start(s_sample[d] if isinstance(n, int) else
                                 s_sample[bass.ds(d, 1)].rearrange("a p c -> (a p) c"),
                                 v["ss"]).then_inc(states_stored, 16)
                if not last(n):
                    sp.wait_ge(qrows_ready, 3 * n + 3)
                    sp.dma_start(qkv_rows[n] if isinstance(n, int) else
                                 qkv_rows[bass.ds(n, 1)].rearrange("a p c -> (a p) c"),
                                 q_rows[:]).then_inc(qrows_stored, 16)
                    if not first(n):
                        sp.wait_ge(states_stored, 32 * n)
                    sp.dma_start(v["ss"], s_in[n] if isinstance(n, int) else
                                 s_in[bass.ds(n, 1)].rearrange("a p c -> (a p) c")).then_inc(
                                     ss_landed, 16)

            phase(0)
            with sp.Fori(1, H) as n:
                phase(n)
            phase(H)
            sp.wait_ge(states_stored, 32 * H)
            for off in (5, 6, 7):
                weights(8, off)
            sp.wait_ge(head_out, H + 1)
            sp.dma_start(xt[:], x_t).then_inc(x_again, 16)
            with sp.Fori(9, 9 + 2 * FFN_GROUPS) as m:
                for off in range(8):
                    weights(m, off)
            for k in range(KB):
                sp.wait_ge(y_ready, k + 1)
                sp.dma_start(y_out[:, k], o_a[:, k]).then_inc(y_stored, 16)
            sp.wait_ge(y_stored, 16 * KB)
            sp.wait_ge(crows_stored, 16 * H)
            sp.wait_ge(qrows_stored, 16 * H)

        @block.tensor
        def _(pe):
            mm = nc.tensor.matmul

            def segment(m, off, i, hi, lo, waits=None, free=()):
                if i == 0:
                    pe.wait_ge(w_high, 8 * m + off + 1)
                    pe.wait_ge(w_low, 8 * m + off + 1)
                    for s_, n_ in free:
                        pe.wait_ge(s_, n_)
                w = off % 2
                for k in (2 * i, 2 * i + 1):
                    if waits:
                        pe.wait_ge(waits[0], waits[1] + k + 1)
                    for p3, (a, b) in enumerate(((w_hi, hi), (w_lo, hi), (w_hi, lo))):
                        for h in range(2):
                            r = mm(ps[:, 2 * w + h, 0:HALF], a[:, w, k],
                                   b[:, k, h * HALF:(h + 1) * HALF],
                                   start=k == 0 and p3 == 0, stop=k == KB - 1 and p3 == 2)
                if i == 3:
                    r.then_inc(job_done, 1)

            def ones_sum(dst, src, start=True, stop=True):
                for h in range(2):
                    r = mm(dst[:, h], con("ones"), src[:, h * HALF:(h + 1) * HALF],
                           start=start, stop=stop)
                return r

            pe.wait_ge(consts_landed, 32)
            for k in range(KB):
                if k % 2 == 0:
                    pe.wait_ge(squares, k // 2 + 1)
                r = ones_sum(g2(0), conf[:, k], k == 0, k == KB - 1)
            r.then_inc(sums, 1)

            def logits():
                pe.wait_ge(log_landed, 32)
                pe.wait_ge(log_zero, 1)
                for t in range(5):
                    n = P if t < TILES else SMP
                    for k in range(KB):
                        for part in (in_hi, in_lo):
                            r = mm(g(3)[0:n, 16 * t:16 * t + 16],
                                   part[:, k, P * t:P * t + n].bitcast(F32),
                                   wlog[:, 16 * k:16 * k + 16],
                                   start=k == 0 and part is in_hi, stop=k == KB - 1 and part is in_lo)
                r.then_inc(log_ps, 1)
                pe.wait_ge(log_dve, 4)
                for i, (a, b) in enumerate((("tri", "tri_s"), ("suf", "suf_s"))):
                    mm(g(2)[:, 64 * i:64 * i + 32], con(a), cols[:, 0:32], start=True, stop=True)
                    r = mm(g(2)[0:SMP, 64 * i + 32:64 * i + 40], con(b, SMP), cols[0:SMP, 32:40],
                           start=True, stop=True)
                r.then_inc(cum_ps, 1)

            def phase(n):
                gdn, proj = not first(n), not last(n)
                segs = 0
                for s in range(32):
                    if last(n):
                        if s in LAST_SEGS:
                            i = LAST_SEGS.index(s)
                            segment(n, i // 4 - 3, i % 4, in_hi, in_lo,
                                    free=[(act_read, 8 * n + i // 4 - 4)])
                    elif s >= 12 or gdn:
                        j = s // 4
                        fr = [] if first(n) and j <= 4 else [(act_read, 8 * n + j - 4)]
                        w_ = (in_ready, 0) if first(n) and j == 3 else None
                        segment(n, j - 3, s % 4, in_hi, in_lo, waits=w_, free=fr)
                    if first(n) and s == 19:
                        logits()
                    if not gdn:
                        continue
                    if s == 0:
                        pe.wait_ge(ss_ready, n)
                        pe.wait_ge(kq_sq, 2 * n - 1)
                        ones_sum(g2(0), v["gk"]).then_inc(kq_sums, 1)
                        pe.wait_ge(o_log, n)
                        pe.wait_ge(kq_sq, 2 * n)
                        ones_sum(g2(2), v["vt"]).then_inc(kq_sums, 1)
                    if s == 2:
                        pe.wait_ge(kq_scale, 4 * n)
                        pe.wait_ge(kq_ready, 2 * n - 1)
                        for c in range(TILES):
                            nc.tensor.transpose(tile(g(0), c), tile(v["kn"], c), con("ident"))
                        nc.tensor.transpose(g(2)[0:SMP, 0:P], sm(v["kn"], P), con("ident")).then_inc(k_tr, 1)
                        for c in range(TILES):
                            nc.tensor.transpose(tile(g(1), c), tile(v["vc"], c), con("ident"))
                        nc.tensor.transpose(g(3)[0:SMP, 0:P], sm(v["vc"], P), con("ident")).then_inc(v_tr, 1)
                    if s == 3:
                        pe.wait_ge(gtri_ready, n)
                        pe.wait_ge(vt_ready, n)
                        mm(g(1), con("ones"), v["dm"][:, 0:SEQ], start=True, stop=True)
                        mm(g(3)[:, 0:SMP], con("ones", SMP), sm(v["dm"]), start=True,
                           stop=True).then_inc(gam_ps, 1)
                    if s == 4:
                        pe.wait_ge(gk_ready, n)
                        for c in range(TILES):
                            mm(tile(g(0), c), tile(v["kn"], c), tile(v["kn"], c), start=True, stop=True)
                        mm(g(2)[0:SMP, 0:SMP], sm(v["kn"], P), sm(v["kn"], P), start=True,
                           stop=True).then_inc(kk_ps, 1)
                    if s == 5:
                        pe.wait_ge(eg_ready, n)
                        pe.wait_ge(kq_ready, 2 * n)
                        for c in range(TILES):
                            mm(tile(g(1), c), tile(v["kn"], c), tile(v["qn"], c), start=True, stop=True)
                        mm(g(3)[0:SMP, 0:SMP], sm(v["kn"], P), sm(v["qn"], P), start=True,
                           stop=True).then_inc(qk_ps, 1)
                    if s == 7:
                        pe.wait_ge(c_ready, STEPS * n - 7)
                        for c in range(TILES):
                            nc.tensor.transpose(tile(g(0), c), tile(c_r[0], c).bitcast(F32), con("ident"))
                        nc.tensor.transpose(g(2)[0:SMP, 0:SMP], c_s[0][0:SMP],
                                            con("ident", SMP)[:, 0:SMP]).then_inc(c_tr, 1)
                    if s in range(8, 21, 2):
                        l = (s - 4) // 2
                        w, t = c_r[(l - 1) % 2], t_r
                        if l == STEPS:
                            w, t = v["db"], t_r.bitcast(F32)
                        pe.wait_ge(c_ready, STEPS * n - 8 + l)
                        pe.wait_ge(t_ready, LEVELS * n - 8 + l)
                        for c in range(TILES):
                            r = mm(tile(g(0), c), tile(w, c), tile(t, c),
                                   start=True, stop=True)
                        if l <= LEVELS_S:
                            r = mm(g(2)[0:SMP, 0:SMP], c_s[(l - 1) % 2][0:SMP], sm(v["dm"]), start=True, stop=True)
                        r.then_inc(x_ps, 1)
                    if s in range(9, 22, 2):
                        l = (s - 5) // 2
                        pe.wait_ge(x_ready, LEVELS * n - 8 + l)
                        if l == 2:
                            pe.wait_ge(u0_ready, n)
                        else:
                            pe.wait_ge(ui_ready, LEVELS * n - 9 + l)
                        if l <= LEVELS:
                            for c in range(TILES):
                                r = mm(tile(g(0), c), tile(u_r, c), tile(x_r, c), start=True, stop=True)
                            if l < LEVELS_S:
                                r = mm(g(2)[0:SMP, 0:SMP], v["us"][0:SMP], sm(v["db"]), start=True, stop=True)
                            r.then_inc(dt_ps, 1)
                        for c in range(TILES):
                            r = mm(tile(g(1), c), tile(x_r, c), tile(u_r, c), start=True, stop=True)
                        if l <= LEVELS_S:
                            r = mm(g(3)[0:SMP, 0:SMP], sm(v["db"]), v["us"][0:SMP], start=True, stop=True)
                        r.then_inc(du_ps, 1)
                    if s == 22:
                        pe.wait_ge(ui_ready, LEVELS * n)
                        for c in range(TILES):
                            mm(tile(g(0), c), tile(v["gk"], c), tile(u_all, c), start=True, stop=True)
                        mm(g(2)[:, 0:SMP], smw(v["gk"]), v["us"][0:SMP], start=True,
                           stop=True).then_inc(kd_ps, 1)
                    if s in (22, 24, 26, 28):
                        c = (s - 22) // 2
                        if c:
                            pe.wait_ge(s_ready, TILES * n - 4 + c)
                        r = mm(g(1)[:, 0:P], tile(u_all, c), tile(v["vt"], c), start=True,
                               stop=c == 0)
                        if c:
                            r = mm(g(1)[:, 0:P], tile(v["kn"], c), v["s"], start=False, stop=True)
                        r.then_inc(u_ps, 1)
                        if c:
                            mm(tile(g(3), c), v["s"], tile(v["qn"], c), start=True, stop=False)
                    if s in (23, 25, 27, 29):
                        c = (s - 23) // 2
                        if c == 0:
                            pe.wait_ge(kd_ready, 2 * n - 1)
                            pe.wait_ge(qd_ready, n)
                        pe.wait_ge(u_ready, TILES * n - 3 + c)
                        mm(g(0)[:, 0:P], tile(v["ko"], c), tile(v["u"], c), start=True,
                           stop=True).then_inc(s_ps, 1)
                        r = mm(tile(g(3), c), tile(v["u"], c), tile(v["qk"], c), start=c == 0, stop=True)
                        if c == TILES - 1:
                            r.then_inc(o_ps, 1)
                    if s == 25:
                        pe.wait_ge(kdm_ready, n)
                        pe.wait_ge(kd_ready, 2 * n)
                        pe.wait_ge(ss_landed, 16 * n)
                        pe.nop(nofuse=True)
                        mm(g(2)[0:SMP, 0:P], v["us"][0:SMP], smw(v["vt"]), start=True, stop=False)
                        for q in range(NS):
                            r = mm(g(2)[0:SMP, 0:P], v["um"][:, q * SMP:(q + 1) * SMP],
                                   tile(v["ss"], q), start=False, stop=q == NS - 1)
                        r.then_inc(us_ps, 1)
                    if s == 27:
                        pe.wait_ge(us_ready, n)
                        mm(g(2)[:, 0:SMP], smw(v["u"]), sm(v["qk"]), start=True, stop=True)
                        for q in range(NS):
                            cols_q = slice(q * LS, (q + 1) * LS)
                            r = mm(g(2)[:, cols_q], tile(v["ss"], q), sm(v["qn"], P)[:, cols_q],
                                   start=False, stop=True, skip_group_check=True)
                        r.then_inc(os_ps, 1)
                    if s == 30:
                        pe.wait_ge(um_ready, n)
                        pe.wait_ge(s_ready, TILES * n)
                        for q in range(2):
                            r = mm(g(q), smw(v["ko"]), v["um"][0:SMP, q * SEQ:(q + 1) * SEQ],
                                   start=True, stop=True)
                        r.then_inc(ss_ps, 1)
                    if s == 31:
                        pe.wait_ge(o_sq, n)
                        pe.wait_ge(o_read, 2 * n)
                        ones_sum(g2(2), v["gk"]).then_inc(o_sums, 1)
                    if last(n) and s == 18:
                        pe.wait_ge(csum_done, H + 1)
                        pe.wait_ge(act_read, 63)
                        ones_sum(job_ps(0), csum).then_inc(mu_ps, 1)
                    if last(n) and 21 <= s < 29:
                        k = s - 21
                        pe.wait_ge(xc_sq, k + 1)
                        ones_sum(job_ps(0), v[("c4", "extq")[k % 2]][:, 0:TOK], k == 0,
                                 k == KB - 1).then_inc(var_ps, 1)

            phase(0)
            with pe.Fori(1, H) as n:
                phase(n)
            phase(H)

            for j in range(8):
                for i in range(4):
                    free = [(act_read, 64 + j - 1)] if j else [(ln_scale, 1)]
                    segment(8, j, i, in_hi, in_lo, waits=(in_ready, 8) if j == 0 else None, free=free)
            pe.wait_ge(y_sum, 8)
            ones_sum(g2(0), csum).then_inc(ms_ps, 1)

            def group(gr, tail=False):
                m = 2 * gr + 9
                for j in range(8):
                    free = [(dve_read, 8 * gr + 7 + j)] if j < 2 else [(act_read, 8 * gr + 72 + j - 1)]
                    for i in range(4):
                        segment(m, j, i, in_hi, in_lo, waits=(in_ready, 16) if j == 0 else None, free=free)
                for j in range(8):
                    free = [(act_read, 8 * gr + 79 + j)] if j < 2 else [(dve_read, 8 * gr + 8 + j - 1)]
                    for i in range(4):
                        segment(m + 1, j, i, f_hi, f_lo, waits=(f_ready, 8 * gr) if j == 0 else None, free=free)

            pe.wait_ge(act_read, 72)
            with pe.Fori(0, FFN_GROUPS - 1) as gr:
                group(gr)
            pe.wait_ge(mid_sum, 8)
            ones_sum(g2(0), csum).then_inc(ms2_ps, 1)
            group(FFN_GROUPS - 1)
            pe.wait_ge(out_sum, 8)
            ones_sum(g2(2), gate[:, 5]).then_inc(ms3_ps, 1)

        def split_off(n, s):
            if last(n):
                return {0: -2, 9: -1, 17: 0}.get(s)
            if s % 4 or s == 32 or (first(n) and s < 12):
                return None
            return s // 4 - 2

        def conv_slots(n, d):
            return (24 + d, 28 + d, 32) if first(n) else (4 + 3 * d // 2, 8 + 3 * d // 2, 12 + 3 * d // 2)

        def evac(n, s):
            for j, kind in jobs(n).items():
                if done_slot(n, j) + 1 == s:
                    return j, kind
            return None, None

        @block.scalar
        def _(act):
            A = nc.scalar.activation

            def log_exp():
                act.preload_act_table_set("natural_log_exp_and_others")

            def split(m, off):
                act.wait_ge(raw_landed[off % RING], 32 * m + 16 * (off // RING) + 16)
                if not (isinstance(m, int) and 8 * m + off < 2):
                    act.wait_ge(job_done, 8 * m + off - 1)
                nc.scalar.copy(w_hi[:, off % 2], raw[:, off % RING]).then_inc(w_high, 1)

            act.sem_inc(o_log, 1)
            act.wait_ge(x_landed, 32)
            for k in range(4):
                A(conf[:, 2 * k:2 * k + 2], xt[:, 2 * k:2 * k + 2], ACT.Square).then_inc(squares, 1)
            act.wait_ge(consts_landed, 32)
            split(0, 0)
            log_exp()
            act.wait_ge(sums, 1)
            A(two(v["c31"]), g2(0), ACT.Ln, scale=1.0 / D, bias=con("eps")).then_inc(scale, 1)
            act.wait_ge(scale, 1)
            A(v["c31"], v["c31"], ACT.Exp, scale=-0.5).then_inc(scale, 1)
            for k in range(KB):
                act.wait_ge(x_scaled, k + 1)
                A(in_hi[:, k], o_a[:, k], ACT.Copy, scale=pcol("pre_mix", k)).then_inc(high_ready, 1)

            def logits():
                sc = v["gk"]
                lp = g(3)[:, 0:80].rearrange("p (t c) -> p t c", t=5)
                log_exp()
                act.wait_ge(log_landed, 32)
                A(sc[:, 160:168], lpar[:, H:2 * H], ACT.Exp)
                act.wait_ge(log_dve, 1)
                A(cols[:, 160:200].rearrange("p (t h) -> p t h", t=5), lp[:, :, 0:H],
                  ACT.Sigmoid).then_inc(log_act, 1)
                A(sc[:, 40:80], sc[:, 0:40], ACT.Abs).then_inc(log_act, 1)
                act.wait_ge(log_act, 2)
                A(sc[:, 80:120], sc[:, 40:80], ACT.Exp, scale=-1.0).then_inc(log_act, 1)
                act.wait_ge(log_act, 3)
                A(sc[:, 120:160], sc[:, 80:120], ACT.Ln, bias=1.0).then_inc(log_act, 1)
                act.wait_ge(log_dve, 5)
                A(cols[:, 80:120], g(2)[:, 0:40], ACT.Exp).then_inc(cols_ready, 1)
                A(cols[:, 120:160], g(2)[:, 64:104], ACT.Exp).then_inc(cols_ready, 1)

            def squares_kq(n):
                act.wait_ge(act_conv, 3 * n + 2)
                A(v["gk"][:, 0:TOK], v["kc"], ACT.Square).then_inc(kq_sq, 1)
                A(v["vt"][:, 0:TOK], v["qc"], ACT.Square).then_inc(kq_sq, 1)

            def phase(n):
                gdn = not first(n)
                if gdn:
                    log_exp()
                for s in range(33):
                    off = split_off(n, s)
                    if off is not None:
                        split(n, off)
                    pos, j = evac(n, s)
                    if pos is not None:
                        act.wait_ge(job_done, 8 * n - 2 + pos)
                        src = job_ps((pos + 1) % 2)
                        if j == Z:
                            A(two(v["zs"]), src, ACT.Silu).then_inc(act_read, 1)
                        if j == GA:
                            act.wait_ge(gext_ready, n if last(n) else n + 1)
                            A(two(v["sig"]), src, ACT.Sigmoid).then_inc(act_read, 1)
                        if j == GB:
                            dst = gate[:, n - 1] if isinstance(n, int) else gate[:, bass.ds(n - 1, 1)]
                            A(dst.rearrange("p (a b) -> p a b", a=2) if isinstance(n, int) else
                              dst.rearrange("p o (a b) -> p (o a) b", a=2), src,
                              ACT.Sigmoid if last(n) else ACT.Copy).then_inc(act_read, 1)
                        if j == CA:
                            if gdn:
                                act.wait_ge(act_conv, 3 * n + 3)
                            A(two(v["c4"]), src, ACT.Copy).then_inc(act_read, 1)
                        if j == CB:
                            if gdn:
                                act.wait_ge(zs_ready, n)
                            A(two(v["sig"]), src, ACT.Sigmoid).then_inc(act_read, 1)
                        if j is not None and j >= Q:
                            e = EXTS[j - Q]
                            if gdn:
                                act.wait_ge(qrows_ready, 3 * n - 2 + j - Q)
                            A(e[:, 3:3 + HALF], src[:, 0], ACT.Copy)
                            A(e[:, 3 + HALF:EXT], src[:, 1, 0:SEQ - HALF], ACT.Copy)
                            A(seqs(e, EXT, EXS, 3, LS),
                              src[:, 1, SEQ - HALF:HALF].rearrange("p (s t) -> p s t", s=NS),
                              ACT.Copy).then_inc(act_read, 1)
                    if not last(n) and s in conv_slots(n, 2):
                        i = conv_slots(n, 2).index(s)
                        act.wait_ge(conv4_done, 3 * n + i + 1)
                        A(CONV[i], v["c4"], ACT.Silu).then_inc(act_conv, 1)
                    if first(n) and s == 20:
                        logits()
                    if gdn and s == 12:
                        act.wait_ge(conv31_done, n)
                        dst = conf[:, n - 1] if isinstance(n, int) else \
                            conf[:, bass.ds(n - 1, 1)].rearrange("p a b -> p (a b)")
                        A(dst, v["c31"], ACT.Identity, bias=ct[:, CF_TAPS:CF_TAPS + 1]).then_inc(conf_ready, 1)
                    if first(n) and s == 31:
                        squares_kq(n)
                    if last(n) and 17 <= s < 24:
                        act.wait_ge(act_read, 61)
                        A(gate[:, s - 17], gate[:, s - 17], ACT.Sigmoid)
                    if last(n) and s == 19:
                        act.wait_ge(mu_ps, 1)
                        A(two(csum[:]), job_ps(0), ACT.Copy, scale=1.0 / D).then_inc(mu_ready, 1)
                    if not gdn:
                        continue
                    if s == 0:
                        act.wait_ge(head_out, n)
                        act.wait_ge(kq_sums, 2 * n - 1)
                        A(two(v["at"]), g2(0), ACT.Ln, bias=con("eps")).then_inc(kq_scale, 1)
                        act.wait_ge(kq_scale, 4 * n - 3)
                        A(v["at"], v["at"], ACT.Exp, scale=-0.5).then_inc(kq_scale, 1)
                        act.wait_ge(kq_sums, 2 * n)
                        A(two(v["db"]), g2(2), ACT.Ln, scale=float(P), bias=con("eps128")).then_inc(kq_scale, 1)
                        act.wait_ge(kq_scale, 4 * n - 1)
                        A(v["db"], v["db"], ACT.Exp, scale=-0.5).then_inc(kq_scale, 1)
                    if s == 2:
                        act.wait_ge(v_tr, n)
                        A(v["vt"][:, 0:SEQ], g(1), ACT.Copy)
                        A(smw(v["vt"]), g(3)[0:SMP, 0:P], ACT.Copy).then_inc(vt_ready, 1)
                    if s == 3:
                        act.wait_ge(dm_diff, n)
                        A(v["dm"][:, 0:SEQ], v["dm"][:, 0:SEQ], ACT.Exp)
                        A(sm(v["dm"]), sm(v["dm"]), ACT.Exp).then_inc(dm_ready, 1)
                        A(v["eg"][:, 0:SEQ], g(1), ACT.Exp)
                        A(sm(v["eg"], P), g(3)[:, 0:SMP], ACT.Exp).then_inc(eg_ready, 1)
                    if s in range(8, 19, 2):
                        l = (s - 4) // 2
                        act.wait_ge(x_ps, LEVELS * n - 8 + l)
                        r = A(x_r[:], g(0), ACT.Copy)
                        if l <= LEVELS_S:
                            r = A(sm(v["db"]), g(2)[0:SMP, 0:SMP], ACT.Copy)
                        r.then_inc(x_ready, 1)
                    if s == 22:
                        act.wait_ge(kd_ps, n)
                        A(v["kn"][:, 0:SEQ], g(0), ACT.Copy, scale=-1.0).then_inc(kd_ready, 1)
                        A(sm(v["kn"], P), g(2)[:, 0:SMP], ACT.Copy, scale=-1.0).then_inc(kd_ready, 1)
                    if s in (22, 24, 26, 28):
                        c = (s - 22) // 2
                        act.wait_ge(u_ps, TILES * n - 3 + c)
                        A(tile(v["u"], c), g(1)[:, 0:P], ACT.Copy,
                          scale=hc[:, 5 * BETA + c:5 * BETA + c + 1]).then_inc(u_ready, 1)
                    if s == 25:
                        act.wait_ge(us_ps, n)
                        A(smw(v["u"]), g(2)[0:SMP, 0:P], ACT.Copy,
                          scale=hc[0:SMP, 5 * BETA + 4:5 * BETA + 5]).then_inc(us_ready, 1)
                    if s == 27:
                        act.wait_ge(os_ps, n)
                        dst = o_a[:, n - 1, SEQ:TOK] if isinstance(n, int) else \
                            o_a[:, bass.ds(n - 1, 1), SEQ:TOK].rearrange("p a b -> p (a b)")
                        A(dst, g(2)[:, 0:SMP], ACT.Copy).then_inc(o_read, 1)
                    if s == 29:
                        act.wait_ge(o_ps, n)
                        dst = o_a[:, n - 1, 0:SEQ] if isinstance(n, int) else \
                            o_a[:, bass.ds(n - 1, 1), 0:SEQ].rearrange("p a b -> p (a b)")
                        A(dst, g(3), ACT.Copy).then_inc(o_read, 1)
                        act.wait_ge(o_read, 2 * n)
                        src = o_a[:, n - 1] if isinstance(n, int) else \
                            o_a[:, bass.ds(n - 1, 1)].rearrange("p a b -> p (a b)")
                        act.nop(nofuse=True)
                        A(v["gk"][:, 0:TOK], src, ACT.Square).then_inc(o_sq, 1)
                    if s == 31:
                        log_exp()
                        act.wait_ge(o_sums, n)
                        A(two(v["at"]), g2(2), ACT.Ln, scale=1.0 / P, bias=con("eps")).then_inc(o_log, 1)
                        act.wait_ge(o_log, n + 1)
                        A(v["at"], v["at"], ACT.Exp, scale=-0.5).then_inc(o_scale, 1)
                        if not last(n):
                            squares_kq(n)
                    if last(n) and 20 <= s < 28:
                        k = s - 20
                        act.wait_ge(xc_ready, k + 1)
                        if k >= 2:
                            act.wait_ge(var_ps, k - 1)
                        A(v[("c4", "extq")[k % 2]][:, 0:TOK], conf[:, k], ACT.Square).then_inc(xc_sq, 1)

            phase(0)
            with act.Fori(1, H) as n:
                phase(n)
            phase(H)
            log_exp()
            act.wait_ge(var_ps, 8)
            A(two(v["c31"]), job_ps(0), ACT.Ln, scale=1.0 / D, bias=con("eps")).then_inc(ln_scale, 1)
            act.wait_ge(ln_scale, 1)
            A(v["c31"], v["c31"], ACT.Exp, scale=-0.5).then_inc(ln_scale, 1)
            for k in range(KB):
                act.wait_ge(ln_scaled, k + 1)
                A(conf[:, k], conf[:, k], ACT.Silu, scale=pcol("ln_g", k),
                  bias=pcol("ln_b", k)).then_inc(b_silu, 1)
            for k in range(KB):
                act.wait_ge(mixed, k + 1)
                if k == 0:
                    act.wait_ge(job_done, 64)
                A(in_hi[:, k], conf[:, k], ACT.Copy).then_inc(high_ready, 1)

            for j in range(8):
                split(8, j + 1)
                act.wait_ge(job_done, 65 + j)
                A(two(gate[:, j]), job_ps(j % 2), ACT.Copy).then_inc(act_read, 1)
                act.wait_ge(act_read, 65 + j)
                if j >= 2:
                    act.wait_ge(y_sum, j - 1)
                A(v[("c4", "extq")[j % 2]][:, 0:TOK], gate[:, j], ACT.Square).then_inc(y_sq, 1)
            log_exp()
            act.wait_ge(ms_ps, 1)
            A(two(v["c31"]), g2(0), ACT.Ln, scale=1.0 / D, bias=con("eps")).then_inc(ms_scale, 1)
            act.wait_ge(ms_scale, 1)
            A(v["c31"], v["c31"], ACT.Exp, scale=-0.5).then_inc(ms_scale, 1)
            for k in range(KB):
                act.wait_ge(mid_ready, k + 1)
                A(in_hi[:, k], conf[:, k], ACT.Copy, scale=pcol("pre_ffn", k)).then_inc(high_ready, 1)
            for k in range(KB):
                if k >= 2:
                    act.wait_ge(mid_sum, k - 1)
                A(v[("sig", "zs")[k % 2]], conf[:, k], ACT.Square).then_inc(mid_sq, 1)

            def group(gr, tail=False):
                m = 2 * gr + 9
                for j in range(8):
                    split(m, j + 1)
                    act.wait_ge(job_done, 16 * gr + 73 + j)
                    act.wait_ge(f_square, 8 * gr + j + 1)
                    A(two(f_tmp[:, j % 2]), job_ps(j % 2), ACT.Relu).then_inc(act_read, 1)
                    act.wait_ge(act_read, 8 * gr + 73 + j)
                    A(f_hi[:, j], f_tmp[:, j % 2], ACT.Square).then_inc(f_high, 1)
                for j in range(8):
                    if not (tail and j == 7):
                        split(m + 1, j + 1)
                    if tail:
                        act.wait_ge(dve_read, 8 * gr + 9 + j)
                        if j >= 2:
                            act.wait_ge(out_sum, j - 1)
                        A(v[("sig", "zs")[j % 2]], o_a[:, j], ACT.Square).then_inc(out_sq, 1)

            with act.Fori(0, FFN_GROUPS - 1) as gr:
                group(gr)
            log_exp()
            act.wait_ge(ms2_ps, 1)
            A(two(gate[:, 1]), g2(0), ACT.Ln, scale=1.0 / D, bias=con("eps")).then_inc(ms2_log, 1)
            act.wait_ge(ms2_log, 1)
            A(gate[:, 2], gate[:, 1], ACT.Exp, scale=-2.0).then_inc(ms2_log, 1)
            group(FFN_GROUPS - 1, tail=True)
            log_exp()
            act.wait_ge(var3, 1)
            A(gate[:, 3], gate[:, 3], ACT.Ln, scale=1.0 / D, bias=con("eps")).then_inc(ms3_log, 1)
            act.wait_ge(expo, 1)
            A(gate[:, 4], gate[:, 4], ACT.Exp, scale=-1.0).then_inc(out_scale, 1)

        @block.vector
        def _(dve):
            ve = nc.vector

            def tt(out, a, b, op):
                return ve.tensor_tensor(out, a, b, op)

            def stt(out, a, s_, b, op0, op1):
                return ve.scalar_tensor_tensor(out=out, in0=a, scalar=s_, in1=b, op0=op0, op1=op1)

            ve.memset(g(3)[:, 0:80], 0.0)
            ve.memset(g(2)[:, 0:128], 0.0).then_inc(log_zero, 1)
            for e in EXTS:
                ve.memset(e[:, 0:QK_TAPS - 1], 0.0)
            ve.memset(v["gext"][:, 0:CF_TAPS - 1], 0.0)
            ve.memset(csum[:], 0.0).then_inc(csum_done, 1)
            dve.sem_inc(ss_ready, 1)
            dve.sem_inc(head_out, 1)
            dve.sem_inc(zs_ready, 1)
            dve.sem_inc(f_square, 2)
            dve.wait_ge(consts_landed, 32)
            dve.wait_ge(scale, 2)
            for k in range(KB):
                tt(o_a[:, k], xt[:, k], v["c31"], ALU.mult).then_inc(x_scaled, 1)
            for k in range(KB):
                dve.wait_ge(high_ready, k + 1)
                stt(in_lo[:, k], o_a[:, k], pcol("pre_mix", k), in_hi[:, k].bitcast(F32),
                    ALU.mult, ALU.subtract).then_inc(in_ready, 1)

            dve.wait_ge(masks_landed, 16)
            ve.tensor_copy(masks[:], mask_in)

            def logits():
                sc = v["gk"]
                r3 = lambda ap: ap.rearrange("p (t h) -> p t h", t=5)
                dve.wait_ge(log_ps, 1)
                lp = g(3)[:, 0:80].rearrange("p (t c) -> p t c", t=5)
                tt(r3(sc[:, 0:40]), lp[:, :, H:2 * H], lpar[:, 0:H].unsqueeze(1).to_broadcast([P, 5, H]),
                   ALU.add).then_inc(log_dve, 1)
                dve.wait_ge(log_act, 4)
                dve.wait_ge(log_dve, 1)
                stt(sc[:, 200:240], sc[:, 0:40], 0.0, sc[:, 120:160], ALU.max, ALU.add).then_inc(log_dve, 1)
                dve.wait_ge(log_dve, 2)
                stt(r3(cols[:, 0:40]), r3(sc[:, 200:240]), -1.0,
                    sc[:, 160:168].unsqueeze(1).to_broadcast([P, 5, H]), ALU.mult, ALU.mult).then_inc(log_dve, 2)
                dve.wait_ge(cum_ps, 1)
                ve.tensor_copy(cols[:, 40:80], g(2)[:, 0:40]).then_inc(log_dve, 1)

            def tap_of(n):
                tp = tap[:].rearrange("p (h c) -> p h c", h=H)
                return tp[:, n] if isinstance(n, int) else \
                    tp[:, bass.ds(n, 1)].rearrange("p a c -> p (a c)")

            def conf_taps(h, a, b):
                ge = v["gext"]
                out_s = v["c31"][:, SEQ:TOK].rearrange("p (s t) -> p s t", s=NS)
                for t in range(a, b):
                    w = ct[:, t:t + 1]
                    if t == 0:
                        ve.tensor_scalar(v["c31"][:, 0:SEQ], ge[:, 0:SEQ], w, None, ALU.mult).then_inc(conv31, 1)
                        ve.tensor_scalar(out_s, seqs(ge, GXT, GXS, 0, LS), w, None, ALU.mult).then_inc(conv31, 1)
                        continue
                    dve.wait_ge(conv31, 62 * h + 2 * t - 1)
                    stt(v["c31"][:, 0:SEQ], ge[:, t:t + SEQ], w, v["c31"][:, 0:SEQ], ALU.mult,
                        ALU.add).then_inc(conv31, 1)
                    dve.wait_ge(conv31, 62 * h + 2 * t)
                    r = stt(out_s, seqs(ge, GXT, GXS, t, LS), w, out_s, ALU.mult, ALU.add)
                    r.then_inc(conv31, 1)

            def qkv_conv(n, i, a, b):
                e, c4 = EXTS[i], v["c4"]
                out_s = c4[:, SEQ:TOK].rearrange("p (s t) -> p s t", s=NS)
                if a == 0:
                    dve.wait_ge(act_read, 8 * n + (3 if first(n) else -2) + i)
                    dve.wait_ge(halo_used, 4 * n + 1 + i)
                if a == 0 and i == 0:
                    dve.wait_ge(gext_ready, n + 1 if first(n) else n)
                elif a == 0:
                    dve.wait_ge(act_conv, 3 * n + i)
                for t in range(a, b):
                    w = qt[:, QK_TAPS * i + t:QK_TAPS * i + t + 1]
                    if t == 0:
                        ve.tensor_scalar(c4[:, 0:SEQ], e[:, 0:SEQ], w, None, ALU.mult).then_inc(conv4, 1)
                        ve.tensor_scalar(out_s, seqs(e, EXT, EXS, 0, LS), w, None, ALU.mult).then_inc(conv4, 1)
                        continue
                    dve.wait_ge(conv4, 24 * n + 8 * i + 2 * t - 1)
                    stt(c4[:, 0:SEQ], e[:, t:t + SEQ], w, c4[:, 0:SEQ], ALU.mult, ALU.add).then_inc(conv4, 1)
                    dve.wait_ge(conv4, 24 * n + 8 * i + 2 * t)
                    r = stt(out_s, seqs(e, EXT, EXS, t, LS), w, out_s, ALU.mult, ALU.add)
                    r.then_inc(conv4, 1)
                if b == QK_TAPS:
                    dve.wait_ge(conv4, 24 * n + 8 * i + 8)
                    dve.sem_inc(conv4_done, 1)

            def head(n, s):
                if s == 0:
                    dve.wait_ge(kq_scale, 4 * n - 2)
                    tt(v["kn"], v["kc"], v["at"], ALU.mult).then_inc(kq_ready, 1)
                    dve.wait_ge(kq_scale, 4 * n)
                    tt(v["qn"], v["qc"], v["db"], ALU.mult).then_inc(kq_ready, 1)
                if s == 2:
                    dve.wait_ge(k_tr, n)
                    dve.wait_ge(hc_ready, n)
                    tt(pr(v["gk"]), g4(0), hcol(EGAM), ALU.mult)
                    tt(pr(v["ko"]), g4(0), hcol(KOF), ALU.mult)
                    tt(smw(v["gk"]), g(2)[0:SMP, 0:P], hcol_s(EGAM, P), ALU.mult)
                    tt(smw(v["ko"]), g(2)[0:SMP, 0:P], hcol_s(KOF, P), ALU.mult).then_inc(gk_ready, 1)
                if s == 3:
                    dve.wait_ge(gam_ps, n)
                    dve.wait_ge(gm_ready, n)
                    tt(v["dm"][:, 0:SEQ], g(1), v["qk"][:, 0:SEQ], ALU.subtract)
                    tt(sm(v["dm"]), g(3)[0:SMP, 0:SMP], sm(v["qk"]), ALU.subtract).then_inc(dm_diff, 1)
                if s == 5:
                    dve.wait_ge(dm_ready, n)
                    tt(pr(v["db"]), pr(v["dm"]), hcol(BETA), ALU.mult)
                    tt(sm(v["db"]), sm(v["dm"]), hcol_s(BETA, SMP), ALU.mult).then_inc(db_ready, 1)
                    dve.wait_ge(kk_ps, n)
                    dve.wait_ge(db_ready, n)
                    tt(v["at"][:, 0:SEQ], g(0), v["db"][:, 0:SEQ], ALU.mult)
                    tt(sm(v["at"]), g(2)[0:SMP, 0:SMP], sm(v["db"]), ALU.mult).then_inc(at_ready, 1)
                    dve.wait_ge(qk_ps, n)
                    tt(v["qk"][:, 0:SEQ], g(1), v["dm"][:, 0:SEQ], ALU.mult)
                    tt(sm(v["qk"]), g(3)[0:SMP, 0:SMP], sm(v["dm"]), ALU.mult).then_inc(qk_ready, 1)
                if s == 7:
                    dve.wait_ge(c_tr, n)
                    dve.wait_ge(qk_ready, n)
                    tt(pr(t_r), con("ident").unsqueeze(1).to_broadcast([P, TILES, P]), g4(0),
                       ALU.subtract)
                    tt(sm(v["dm"]), con("ident", SMP)[:, 0:SMP], g(2)[0:SMP, 0:SMP],
                       ALU.subtract).then_inc(t_ready, 1)
                if s == 20:
                    dve.wait_ge(x_ps, LEVELS * n)
                    dve.wait_ge(tmi_ready, n)
                    tt(x_r[:], v["um"][:, 0:SEQ], g(0), ALU.add).then_inc(x_ready, 1)
                if s in range(9, 22, 2):
                    l = (s - 5) // 2
                    if l <= LEVELS:
                        dve.wait_ge(dt_ps, (LEVELS - 1) * n - 7 + l)
                        dve.wait_ge(t_ready, LEVELS * n - 8 + l)
                        r = tt(t_r[:], t_r.bitcast(F32)[:, :], g(0), ALU.subtract)
                        if l < LEVELS_S:
                            r = tt(sm(v["dm"]), sm(v["dm"]), g(2)[0:SMP, 0:SMP], ALU.subtract)
                        r.then_inc(t_ready, 1)
                    dve.wait_ge(du_ps, LEVELS * n - 8 + l)
                    if l > 2:
                        dve.wait_ge(ui_ready, LEVELS * n - 9 + l)
                    else:
                        dve.wait_ge(u0_ready, n)
                    dst = u_all[:, 0:SEQ] if l == STEPS else u_r[:]
                    r = tt(dst, u_r.bitcast(F32)[:, :], g(1), ALU.subtract)
                    if l <= LEVELS_S:
                        r = tt(v["us"][0:SMP], v["us"][0:SMP], g(3)[0:SMP, 0:SMP], ALU.subtract)
                    r.then_inc(ui_ready, 1)
                if s in (23, 25, 27, 29):
                    c = (s - 23) // 2
                    dve.wait_ge(s_ps, TILES * n - 3 + c)
                    if c == 0:
                        dve.wait_ge(ss_landed, 16 * n)
                        ve.tensor_copy(v["s"], g(0)[:, 0:P]).then_inc(s_ready, 1)
                    else:
                        dve.wait_ge(s_ready, TILES * n - 4 + c)
                        stt(v["s"], v["s"], v["eg"][:, c * P + P - 1:c * P + P], g(0)[:, 0:P],
                            ALU.mult, ALU.add).then_inc(s_ready, 1)
                if s == 30:
                    dve.wait_ge(ss_ps, n)
                    dve.wait_ge(ss_decayed, n)
                    tt(v["ss"], v["ss"], ps[:, 4:6, :].rearrange("p a b -> p (a b)"),
                       ALU.add).then_inc(ss_ready, 1)
                if s == 31:
                    dve.wait_ge(o_scale, n)
                    o = o_a[:, n - 1] if isinstance(n, int) else \
                        o_a[:, bass.ds(n - 1, 1)].rearrange("p a b -> p (a b)")
                    tt(v["db"], o, v["at"], ALU.mult).then_inc(o_scaled, 1)
                    dve.wait_ge(o_scaled, n)
                    dve.wait_ge(zs_ready, n + 1)
                    stt(o, v["db"], pcol("delta_g", 0), v["zs"], ALU.mult, ALU.mult).then_inc(head_out, 1)

            early = {0: 3, 1: 3, 3: 2, 6: 1, 7: 1, 10: 1}
            late = {s: 2 for s in range(22, 32)}
            late_0 = {21: 3, 22: 3, 23: 3, 25: 2, 26: 3, 27: 2, 30: 2, 31: 2}

            def convolutions(n, s):
                gdn, proj = not first(n), not last(n)
                if gdn and s in early:
                    t = STEPS_1 + sum(early[x] for x in early if x < s)
                    conf_taps(n - 1, t, t + early[s])
                    if t + early[s] == CF_TAPS:
                        dve.wait_ge(conv31, 62 * n)
                        dve.sem_inc(conv31_done, 1)
                if gdn and proj and s == 4:
                    ve.tensor_copy(qt[:], tap_of(n)[:, 0:3 * QK_TAPS]).then_inc(taps_cur, 1)
                    dve.wait_ge(taps_cur, 2 * n + 1)
                if proj and s == (21 if gdn else 20):
                    if gdn:
                        dve.wait_ge(conf_ready, n)
                    else:
                        dve.wait_ge(taps_landed, 16)
                    if first(n):
                        ve.tensor_copy(qt[:], tap_of(n)[:, 0:3 * QK_TAPS]).then_inc(taps_cur, 1)
                    ve.tensor_copy(ct[:], tap_of(n)[:, 3 * QK_TAPS:TAPW]).then_inc(taps_cur, 1)
                    dve.wait_ge(taps_cur, 2 * n + 2)
                    dve.wait_ge(gext_ready, n + 1)
                own = late_0 if first(n) else late
                if proj and s in own:
                    t = sum(own[x] for x in own if x < s)
                    conf_taps(n, t, t + own[s])
                if first(n) and s in (24, 28):
                    qkv_conv(n, (s - 24) // 4, 0, QK_TAPS)
                if gdn and proj and s in (4, 6, 8, 10, 12, 14):
                    i = (s - 4) // 4
                    qkv_conv(n, i, 2 * (s // 2 % 2), 2 * (s // 2 % 2) + 2)

            def phase(n):
                gdn = not first(n)
                if gdn:
                    if isinstance(n, int):
                        src = cols[:].rearrange("p (a h) -> p a h", h=H)[:, :, n - 1:n]
                    else:
                        src = cols[:].rearrange("p (a h) -> p a h", h=H)[:, :, bass.ds(n - 1, 1)]
                    dve.wait_ge(cols_ready, 2)
                    ve.tensor_copy(hc[:].unsqueeze(2), src).then_inc(hc_ready, 1)
                for s in range(32):
                    if not gdn or s < 1:
                        convolutions(n, s)
                    if first(n) and s == 20:
                        logits()
                    if last(n) and 20 <= s < 28:
                        k = s - 20
                        if k == 0:
                            dve.wait_ge(mu_ready, 1)
                        tt(conf[:, k], conf[:, k], csum[:], ALU.subtract).then_inc(xc_ready, 1)
                    if gdn:
                        head(n, s)
                        if s >= 1:
                            convolutions(n, s)
                if first(n):
                    qkv_conv(n, 2, 0, QK_TAPS)

            phase(0)
            with dve.Fori(1, H) as n:
                phase(n)
            phase(H)
            dve.wait_ge(ln_scale, 2)
            for k in range(KB):
                tt(conf[:, k], conf[:, k], v["c31"], ALU.mult).then_inc(ln_scaled, 1)
            for k in range(KB):
                dve.wait_ge(b_gated, k + 1)
                tt(conf[:, k], conf[:, k], o_a[:, k], ALU.add).then_inc(mixed, 1)
                if k:
                    dve.wait_ge(high_ready, 8 + k)
                    tt(in_lo[:, k - 1], conf[:, k - 1], in_hi[:, k - 1].bitcast(F32),
                       ALU.subtract).then_inc(in_ready, 1)
            dve.wait_ge(high_ready, 16)
            tt(in_lo[:, 7], conf[:, 7], in_hi[:, 7].bitcast(F32), ALU.subtract).then_inc(in_ready, 1)
            dve.wait_ge(mixed, 8)
            for k in range(KB):
                ve.memset(o_a[:, k], 0.0).then_inc(dve_read, 1)

            dve.wait_ge(ms_scale, 2)
            dve.wait_ge(x_again, 16)
            dve.wait_ge(act_read, 72)
            dve.wait_ge(job_done, 72)
            for k in range(KB):
                tt(gate[:, k], gate[:, k], v["c31"], ALU.mult).then_inc(y_scaled, 1)
                dve.wait_ge(y_scaled, k + 1)
                stt(conf[:, k], gate[:, k], pcol("post_mix", k), xt[:, k], ALU.mult,
                    ALU.add).then_inc(mid_ready, 1)
                if k:
                    dve.wait_ge(high_ready, 16 + k)
                    stt(in_lo[:, k - 1], conf[:, k - 1], pcol("pre_ffn", k - 1),
                        in_hi[:, k - 1].bitcast(F32), ALU.mult, ALU.subtract).then_inc(in_ready, 1)
            dve.wait_ge(high_ready, 24)
            stt(in_lo[:, 7], conf[:, 7], pcol("pre_ffn", 7), in_hi[:, 7].bitcast(F32),
                ALU.mult, ALU.subtract).then_inc(in_ready, 1)

            def group(gr):
                for j in range(8):
                    dve.wait_ge(act_read, 8 * gr + 73 + j)
                    tt(f_tmp[:, 2 + j % 2], f_tmp[:, j % 2], f_tmp[:, j % 2], ALU.mult).then_inc(f_square, 1)
                    dve.wait_ge(f_square, 8 * gr + 3 + j)
                    dve.wait_ge(f_high, 8 * gr + 1 + j)
                    tt(f_lo[:, j], f_tmp[:, 2 + j % 2], f_hi[:, j].bitcast(F32),
                       ALU.subtract).then_inc(f_ready, 1)
                for j in range(8):
                    dve.wait_ge(job_done, 16 * gr + 81 + j)
                    tt(two(o_a[:, j]), two(o_a[:, j]), job_ps(j % 2), ALU.add).then_inc(dve_read, 1)

            with dve.Fori(0, FFN_GROUPS) as gr:
                group(gr)

            dve.wait_ge(ms2_log, 2)
            dve.wait_ge(ms3_ps, 1)
            tt(two(gate[:, 3]), g2(2), two(gate[:, 2]), ALU.mult).then_inc(var3, 1)
            dve.wait_ge(ms3_log, 1)
            stt(gate[:, 4], gate[:, 3], 0.5, gate[:, 1], ALU.mult, ALU.add).then_inc(expo, 1)
            dve.wait_ge(out_scale, 1)
            for k in range(KB):
                tt(o_a[:, k], o_a[:, k], gate[:, 4], ALU.mult).then_inc(out_scaled, 1)
                dve.wait_ge(out_scaled, k + 1)
                stt(o_a[:, k], o_a[:, k], pcol("post_ffn", k), conf[:, k], ALU.mult,
                    ALU.add).then_inc(y_ready, 1)

        @block.gpsimd
        def _(pool):
            gp = nc.gpsimd

            def tt(out, a, b, op):
                return gp.tensor_tensor(out, a, b, op)

            def split(m, off):
                pool.wait_ge(w_high, 8 * m + off + 1)
                tt(w_lo[:, off % 2], raw[:, off % RING], w_hi[:, off % 2].bitcast(F32),
                   ALU.subtract).then_inc(w_low, 1)

            pool.wait_ge(consts_landed, 32)
            split(0, 0)

            def bc(ap):
                return ap.unsqueeze(1).to_broadcast([P, TILES, P])

            def level(n, l):
                cr = c_r[(l - 1) % 2]
                if l == 3:
                    pool.wait_ge(c_tr, n)
                if l > 3:
                    pool.wait_ge(x_ps, LEVELS * n - 10 + l)
                if l == STEPS:
                    r = tt(pr(v["db"]), pr(v["at"]), bc(con("strict")), ALU.mult)
                else:
                    r = tt(pr(cr), pr(v["at"]), lvl(l), ALU.mult)
                if l <= LEVELS_S:
                    r = tt(c_s[(l - 1) % 2][0:SMP], sm(v["at"]), lvl_s(l), ALU.mult)
                r.then_inc(c_ready, 1)

            def phase(n):
                gdn, proj = not first(n), not last(n)
                if gdn:
                    pool.wait_ge(hc_ready, n)
                    tt(pr(v["dm"]), bc(con("tri")), hcol(G), ALU.mult)
                    tt(sm(v["dm"]), con("tri_s", SMP), hcol_s(G, SMP), ALU.mult).then_inc(gtri_ready, 1)
                    tt(pr(v["qk"]), bc(con("big")), hcol(GAM), ALU.add)
                    tt(sm(v["qk"]), con("big_s", SMP), hcol_s(GAM, SMP), ALU.add).then_inc(gm_ready, 1)
                for s in range(33):
                    off = split_off(n, s)
                    if off is not None:
                        split(n, off)
                    pos, j = evac(n, s)
                    if j == GA:
                        pool.wait_ge(act_read, 8 * n - 2 + pos)
                        tt(v["zs"], v["zs"], v["sig"], ALU.mult).then_inc(zs_ready, 1)
                    if proj and s == (20 if first(n) else 2):
                        pool.wait_ge(halo_landed, 16 * n + 16)
                        if gdn:
                            pool.wait_ge(conv4_done, 3 * n)
                        pool.nop(nofuse=True)
                        for i in range(3):
                            gp.tensor_copy(seqs(EXTS[i], EXT, EXS, 0, QK_TAPS - 1),
                                           halo[:, 24 * i:24 * i + 24].rearrange("p (s t) -> p s t", s=NS)
                                           ).then_inc(halo_used, 1)
                    if j == CB:
                        ge = v["gext"]
                        if gdn:
                            pool.wait_ge(conv31_done, n)
                            pool.nop(nofuse=True)
                        gp.tensor_copy(seqs(ge, GXT, GXS, 0, CF_TAPS - 1),
                                       halo[:, 72:HALO].rearrange("p (s t) -> p s t", s=NS)).then_inc(halo_used, 1)
                        pool.wait_ge(act_read, 8 * n - 2 + pos)
                        tt(ge[:, CF_TAPS - 1:GXT], v["c4"][:, 0:SEQ], v["sig"][:, 0:SEQ], ALU.mult)
                        tt(seqs(ge, GXT, GXS, CF_TAPS - 1, LS),
                           v["c4"][:, SEQ:TOK].rearrange("p (s t) -> p s t", s=NS),
                           v["sig"][:, SEQ:TOK].rearrange("p (s t) -> p s t", s=NS),
                           ALU.mult).then_inc(gext_ready, 1)
                        pool.wait_ge(gext_ready, n + 1)
                        pool.wait_ge(halo_used, 4 * n + 4)
                        if gdn:
                            pool.wait_ge(crows_stored, 16 * n)
                        pool.nop(nofuse=True)
                        gp.tensor_copy(c_rows[:, 0:CF_TAPS - 1], ge[:, GXT - CF_TAPS + 1:GXT])
                        gp.tensor_copy(c_rows[:, CF_TAPS - 1:].rearrange("p (s t) -> p s t", s=NS),
                                       seqs(ge, GXT, GXS, LS, CF_TAPS - 1)).then_inc(crows_ready, 1)
                    if j is not None and j >= Q:
                        i = j - Q
                        pool.wait_ge(act_read, 8 * n - 2 + pos)
                        if gdn and i == 0:
                            pool.wait_ge(qrows_stored, 16 * n)
                        pool.nop(nofuse=True)
                        gp.tensor_copy(q_rows[:, 27 * i:27 * i + 3], EXTS[i][:, EXT - 3:EXT])
                        gp.tensor_copy(q_rows[:, 27 * i + 3:27 * i + 27].rearrange("p (s t) -> p s t", s=NS),
                                       seqs(EXTS[i], EXT, EXS, LS, 3)).then_inc(qrows_ready, 1)
                    if gdn and s == 13:
                        pool.wait_ge(conf_ready, n)
                        if isinstance(n, int):
                            src = conf[:, n - 1]
                        else:
                            src = conf[:, bass.ds(n - 1, 1)].rearrange("p a b -> p (a b)")
                        pool.wait_ge(csum_done, n)
                        tt(csum[:], csum[:], src, ALU.add).then_inc(csum_done, 1)
                    if not gdn:
                        continue
                    if s == 5:
                        pool.wait_ge(at_ready, n)
                        level(n, 1)
                        level(n, 2)
                    if s == 6:
                        pool.wait_ge(c_ready, STEPS * n - 7)
                        tt(pr(u_r), bc(con("ident")), pr(c_r[0].bitcast(F32)), ALU.subtract)
                        tt(v["us"][0:SMP], con("ident", SMP)[:, 0:SMP], c_s[0][0:SMP], ALU.subtract).then_inc(u0_ready, 1)
                        pool.wait_ge(qk_ps, n)
                        tt(v["qn"], v["qn"], v["eg"], ALU.mult).then_inc(qd_ready, 1)
                    if s == 7:
                        pool.wait_ge(u0_ready, n)
                        level(n, 3)
                    if s in (8, 10, 12, 14, 16):
                        level(n, s // 2)
                    if s == 19:
                        pool.wait_ge(t_ready, LEVELS * n)
                        tt(pr(v["um"]), pr(t_r.bitcast(F32)), bc(con("ident")), ALU.subtract).then_inc(tmi_ready, 1)
                    if s == 22:
                        pool.wait_ge(kd_ready, 2 * n)
                        tt(v["um"][:, 0:NS * SMP].rearrange("p (q t) -> p q t", q=NS),
                           sm(v["kn"], P).unsqueeze(1).to_broadcast([P, NS, SMP]),
                           con("colm").rearrange("p (q t) -> p q t", q=NS), ALU.mult).then_inc(kdm_ready, 1)
                    if s == 26:
                        pool.wait_ge(us_ready, n)
                        tt(v["um"][0:SMP, :].rearrange("p (q c) -> p q c", q=NS),
                           smw(v["u"]).unsqueeze(1).to_broadcast([SMP, NS, P]),
                           con("rowm", SMP).unsqueeze(2).to_broadcast([SMP, NS, P]),
                           ALU.mult).then_inc(um_ready, 1)
                    if s == 29:
                        pool.wait_ge(o_ps, n)
                        tt(v["ss"].rearrange("p (q c) -> p q c", q=NS),
                           v["ss"].rearrange("p (q c) -> p q c", q=NS),
                           v["eg"][:, SEQ + LS - 1:TOK:LS].unsqueeze(2).to_broadcast([P, NS, P]),
                           ALU.mult).then_inc(ss_decayed, 1)

            phase(0)
            with pool.Fori(1, H) as n:
                phase(n)
            phase(H)
            for k in range(KB):
                pool.wait_ge(b_silu, k + 1)
                tt(conf[:, k], conf[:, k], gate[:, k], ALU.mult).then_inc(b_gated, 1)

            for j in range(8):
                split(8, j + 1)
                pool.wait_ge(y_sq, j + 1)
                src = v[("c4", "extq")[j % 2]][:, 0:TOK]
                if j:
                    pool.wait_ge(y_sum, j)
                    tt(csum[:], csum[:], src, ALU.add).then_inc(y_sum, 1)
                else:
                    gp.tensor_copy(csum[:], src).then_inc(y_sum, 1)
            pool.wait_ge(ms_ps, 1)
            for k in range(KB):
                pool.wait_ge(mid_sq, k + 1)
                src = v[("sig", "zs")[k % 2]]
                if k:
                    pool.wait_ge(mid_sum, k)
                    tt(csum[:], csum[:], src, ALU.add).then_inc(mid_sum, 1)
                else:
                    gp.tensor_copy(csum[:], src).then_inc(mid_sum, 1)

            def group(gr, tail=False):
                m = 2 * gr + 9
                for j in range(8):
                    split(m, j + 1)
                for j in range(8):
                    if not (tail and j == 7):
                        split(m + 1, j + 1)
                    if tail:
                        pool.wait_ge(out_sq, j + 1)
                        src = v[("sig", "zs")[j % 2]]
                        if j:
                            pool.wait_ge(out_sum, j)
                            tt(gate[:, 5], gate[:, 5], src, ALU.add).then_inc(out_sum, 1)
                        else:
                            gp.tensor_copy(gate[:, 5], src).then_inc(out_sum, 1)

            with pool.Fori(0, FFN_GROUPS - 1) as gr:
                group(gr)
            group(FFN_GROUPS - 1, tail=True)


def shape_constants():
    i, j = np.indices((P, P))
    a, b = np.indices((SMP, SMP))
    same = a // LS == b // LS
    out = np.zeros((P, CONSTS), np.float32)

    def put(nm, value, at=0):
        o = OFF[nm][0] + at
        out[:value.shape[0], o:o + value.shape[1]] = value

    def half(r, c, n):
        return (r // (2 * n) == c // (2 * n)) & (r // n < c // n)

    put("ident", i == j)
    put("ones", np.ones((P, P)))
    put("tri", i <= j)
    put("suf", i > j)
    put("big", np.where(j < i, BIG, 0))
    put("tri_s", same & (a <= b))
    put("suf_s", same & (a > b))
    put("big_s", np.where(same & (b >= a), 0, BIG))
    for l in range(LEVELS):
        put("lvl", half(i, j, 2 ** l), l * P)
    for l in range(LEVELS_S):
        put("lvl_s", half(a, b, 2 ** l), l * SMP)
    for q in range(NS):
        put("colm", np.tile(np.arange(SMP) // LS == q, (P, 1)), q * SMP)
    put("strict", i < j)
    put("rowm", np.arange(SMP)[:, None] // LS == np.arange(NS)[None, :])
    put("eps", np.full((P, 1), EPS))
    put("eps128", np.full((P, 1), P * EPS))
    return out


def channels(a):
    a = a.reshape(a.shape[:-1] + (-1, P))
    return np.moveaxis(a, (-1, -2), (0, 1))


def job_weights(w):
    return w.reshape(KB, P, -1, P).transpose(2, 1, 0, 3)


_OUTS = [("y", (P, KB, TOK)), ("s_prompt", (H, P, P)), ("s_sample", (H, P, NS * P)),
         ("qkv_rows", (H, P, 81)), ("conf_rows", (H, P, 9 * (CF_TAPS - 1)))]


def kernel(x_prompt, x_sample, state_delta, state_qkv_conv, state_conf_conv, w_in, conv_qkv_w,
           a_log, dt_bias, delta_norm_g, conf_dw_w, conf_dw_b, conf_ln_g, conf_ln_b, w_out,
           g_pre_mix, g_post_mix, g_pre_ffn, g_post_ffn, w_up, w_down):
    import concourse.bacc as bacc
    from concourse.bass_utils import run_bass_kernel_spmd

    f = lambda a: np.ascontiguousarray(np.asarray(a))
    x = np.concatenate([f(x_prompt)[0], f(x_sample).reshape(SMP, D)], 0)
    wi = f(w_in)[0]
    o1 = 3 * D
    o2 = o1 + 2 * H
    qkv = job_weights(wi[:, :o1])
    rest = job_weights(wi[:, o2:])
    z, ca, cb, ga, gb = (rest[8 * i:8 * i + 8] for i in range(5))
    parts = []
    for n in range(H + 1):
        for kind in (FIRST if n == 0 else LAST if n == H else MIDDLE).values():
            parts.append({Z: z, GA: ga, GB: gb}[kind][n - 1] if kind <= GB else
                         {CA: ca, CB: cb, Q: qkv, K: qkv[H:], V: qkv[2 * H:]}[kind][n])
    parts += list(job_weights(f(w_out)[0]))
    up = job_weights(f(w_up)[0])
    down = f(w_down)[0]
    for gr in range(FFN_GROUPS):
        parts += list(up[8 * gr:8 * gr + 8])
        parts += list(job_weights(down[D * gr:D * gr + D]))
    w_all = np.stack(parts)

    par = np.zeros((P, len(PARAMS), KB), np.float32)
    for i, a in enumerate((g_pre_mix, g_post_mix, g_pre_ffn, g_post_ffn, conf_ln_g, conf_ln_b)):
        par[:, i] = channels(f(a)[0])
    par[:, 6, 0] = f(delta_norm_g)[0]
    cq = channels(f(conv_qkv_w)[0]).reshape(P, 3, H, QK_TAPS).transpose(0, 2, 1, 3).reshape(P, H, 12)
    taps = np.concatenate([cq, channels(f(conf_dw_w)[0]), channels(f(conf_dw_b)[0])[:, :, None]], 2)
    hq = channels(f(state_qkv_conv)[0]).reshape(P, 3, H, 24).transpose(2, 0, 1, 3).reshape(H, P, 72)
    hf = channels(f(state_conf_conv)[0]).reshape(P, H, 240).transpose(1, 0, 2)
    halos = np.concatenate([hq, hf], 2)
    halos = np.concatenate([halos, np.zeros((1, P, HALO), np.float32)], 0)
    arrays = {
        "x_t": channels(x).reshape(P, KB, TOK),
        "w_all": w_all,
        "w_log": wi[:, o1:o2].reshape(KB, P, 2 * H).transpose(1, 0, 2).reshape(P, KB * 2 * H),
        "log_par": np.tile(np.concatenate([f(dt_bias)[0], f(a_log)[0]])[None], (P, 1)),
        "consts": shape_constants(),
        "params": par.reshape(P, -1),
        "taps": taps.reshape(P, -1),
        "halos": halos,
        "s_in": f(state_delta)[0].transpose(1, 2, 0, 3).reshape(H, P, NS * P),
    }
    nc = bacc.Bacc("TRN2", target_bir_lowering=False, num_devices=1)
    arrays = {k + "_in": np.ascontiguousarray(a) for k, a in arrays.items()}
    args = [nc.dram_tensor(k, a.shape, mybir.dt.from_np(a.dtype), kind="ExternalInput").ap()
            for k, a in arrays.items()]
    args += [nc.dram_tensor(k + "_out", s, F32, kind="ExternalOutput").ap() for k, s in _OUTS]
    build(nc, *args)
    res = run_bass_kernel_spmd(nc, [arrays], core_ids=[0]).results[0]
    y, sp, ss, qr, cr = (np.asarray(res[k + "_out"]) for k, _ in _OUTS)
    y = y.transpose(2, 1, 0).reshape(TOK, D)
    qr = qr.reshape(H, P, 3, 27).transpose(3, 2, 0, 1).reshape(27, 3 * D)
    cr = cr.reshape(H, P, 9, CF_TAPS - 1).transpose(2, 3, 0, 1).reshape(9, CF_TAPS - 1, D)
    return (y[:SEQ].reshape(1, SEQ, D), y[SEQ:].reshape(NS, LS, D), sp.reshape(1, 1, H, P, P),
            qr[:3].reshape(1, 1, 3, 3 * D), cr[:1].reshape(1, 1, CF_TAPS - 1, D),
            ss.reshape(H, P, NS, P).transpose(2, 0, 1, 3).reshape(1, NS, H, P, P),
            qr[3:].reshape(1, NS, 3, 3 * D), cr[1:].reshape(1, NS, CF_TAPS - 1, D))
```

```python
from contextlib import ExitStack

import numpy as np

import concourse.bass as bass
import concourse.mybir as mybir

F32 = mybir.dt.float32
F32R = mybir.dt.float32r
BF16 = mybir.dt.bfloat16
ACT = mybir.ActivationFunctionType
ALU = mybir.AluOpType

P = 128
D = 1024
H = 8
KB = D // P
SEQ = 512
NS, LS = 8, 8
SMP = NS * LS
TOK = SEQ + SMP
HALF = TOK // 2
TILES = SEQ // P
QK_TAPS, CF_TAPS = 4, 31
EXT = SEQ + QK_TAPS - 1
EXS = LS + QK_TAPS - 1
GXT = SEQ + CF_TAPS - 1
GXS = LS + CF_TAPS - 1
EPS = 1e-6
BIG = 1e30
FFN_GROUPS = 4
PROJ_JOBS = 8 * H
OUT_JOB0 = PROJ_JOBS
FFN_JOB0 = PROJ_JOBS + H
JOBS = FFN_JOB0 + FFN_GROUPS * 2 * H
RING = 4
LEVELS = 7
STEPS = LEVELS + 1
LEVELS_S = 3
STEPS_1 = 20
Z, GA, GB, CA, CB, Q, K, V = range(8)
FIRST = {3: CA, 4: CB, 5: Q, 6: K, 7: V}
MIDDLE = {0: Q, 1: K, 2: V, 3: CA, 4: CB, 5: Z, 6: GA, 7: GB}
LAST = {0: Z, 1: GA, 2: GB}
POOL_BLOCKS = (0, 1, 2)
STORE_ORDER = (3, 4, 0, 5, 6, 1, 7, 2)
LAST_SEGS = (0, 1, 2, 5, 8, 10, 12, 14, 16, 18, 21, 24)

_LAYOUT = [("ident", P), ("ones", P), ("tri", P), ("suf", P), ("tri_s", SMP), ("suf_s", SMP),
           ("eps", 1), ("eps128", 1), ("big", P), ("big_s", SMP), ("lvl", LEVELS * P),
           ("lvl_s", LEVELS_S * SMP), ("strict", P), ("colm", NS * SMP), ("rowm", NS)]
OFF, _o = {}, 0
for _n, _w in _LAYOUT:
    OFF[_n] = (_o, _o + _w)
    _o += _w
CONSTS = _o
WIDE = OFF["big"][0]
PARAMS = ["pre_mix", "post_mix", "pre_ffn", "post_ffn", "ln_g", "ln_b", "delta_g"]
TAPW = 3 * QK_TAPS + CF_TAPS + 1
HALO = 3 * NS * (QK_TAPS - 1) + NS * (CF_TAPS - 1)


def build(nc, x_t, w_all, w_log, log_par, consts, params, taps, halos, s_in,
          y_out, s_prompt, s_sample, qkv_rows, conf_rows):
    with ExitStack() as ctx:
        def sb(name, width, dt=F32):
            return ctx.enter_context(nc.sbuf_tensor(name, [P, width], dt))

        def sem(name):
            return ctx.enter_context(nc.semaphore(name))

        names = [("kn", TOK), ("qn", TOK), ("eg", TOK), ("dm", TOK), ("db", TOK), ("at", TOK),
                 ("qk", TOK),
                 ("gk", SEQ + P), ("ko", SEQ + P), ("vt", SEQ + P), ("u", SEQ + P),
                 ("s", P), ("ss", NS * P), ("um", NS * P),
                 ("extq", EXT + NS * EXS), ("extk", EXT + NS * EXS), ("extv", EXT + NS * EXS),
                 ("gext", GXT + NS * GXS), ("c4", TOK), ("c31", TOK),
                 ("qc", TOK), ("kc", TOK), ("vc", TOK),
                 ("us", SMP), ("cs0", SMP), ("cs1", SMP), ("sig", TOK), ("zs", TOK)]
        work_at = -(-nc.sbuf_base // 32) * 32
        c_r, x_r = (sb("c0_r", SEQ, F32R), sb("c1_r", SEQ, F32R)), sb("x_r", SEQ, F32R)
        t_r, u_r = sb("t_r", SEQ, F32R), sb("u_r", SEQ, F32R)
        work = sb("work", sum(w for _, w in names))
        at, v = 0, {}
        for nm, w in names:
            v[nm] = work[:, at:at + w]
            at += w
        xt = nc.alloc_sbuf_tensor_at("xt", [P, KB, TOK], F32, offset=work_at)
        f_hi = nc.alloc_sbuf_tensor_at("f_hi", [P, KB, TOK], F32R, offset=work_at + 4 * KB * TOK)
        f_lo = nc.alloc_sbuf_tensor_at("f_lo", [P, KB, TOK], F32R, offset=work_at + 8 * KB * TOK)
        f_tmp = nc.alloc_sbuf_tensor_at("f_tmp", [P, 4, TOK], F32, offset=work_at + 12 * KB * TOK)


        def blocks(name, dt=F32):
            return ctx.enter_context(nc.sbuf_tensor(name, [P, KB, TOK], dt))

        in_hi, in_lo = blocks("in_hi", F32R), blocks("in_lo", F32R)
        o_a = blocks("o_a")
        gate = blocks("gate")
        conf = blocks("conf")
        raw = ctx.enter_context(nc.sbuf_tensor("raw", [P, RING, KB, P], F32))
        w_hi = ctx.enter_context(nc.sbuf_tensor("w_hi", [P, 2, KB, P], F32R))
        w_lo = ctx.enter_context(nc.sbuf_tensor("w_lo", [P, 2, KB, P], F32R))
        cst, masks = sb("cst", WIDE), sb("masks", CONSTS - WIDE, BF16)
        par = sb("par", len(PARAMS) * KB)
        tap = sb("tap", KB * TAPW)
        halo = sb("halo", HALO)
        lpar = sb("lpar", 2 * H)
        wlog = sb("wlog", KB * 2 * H)
        cols = sb("cols", 5 * 5 * H)
        hc = sb("hc", 25)
        qt, ct = sb("qt", 3 * QK_TAPS), sb("ct", CF_TAPS + 1)
        q_rows, c_rows = sb("q_rows", 3 * 27), sb("c_rows", 9 * (CF_TAPS - 1))
        csum = sb("csum", TOK)
        ps = ctx.enter_context(nc.psum_tensor("ps", [P, 8, 512], F32))

        mask_in = gate[:].rearrange("p k t -> p (k t)")[:, 0:CONSTS - WIDE]

        def con(nm, rows=P):
            a, b = OFF[nm]
            return cst[0:rows, a:b] if b <= WIDE else masks[0:rows, a - WIDE:b - WIDE]

        def lvl(l):
            a = OFF["lvl"][0] - WIDE + (l - 1) * P
            return masks[:, a:a + P].unsqueeze(1).to_broadcast([P, TILES, P])

        def lvl_s(l):
            a = OFF["lvl_s"][0] - WIDE + (l - 1) * SMP
            return masks[0:SMP, a:a + SMP]

        def pcol(nm, k):
            a = PARAMS.index(nm) * KB + k
            return par[:, a:a + 1]

        def job_ps(j2):
            return ps[:, 2 * j2:2 * j2 + 2, 0:HALF]

        def g(i):
            return ps[:, 4 + i, :]

        def g2(i):
            return ps[:, 4 + i:6 + i, 0:HALF]

        def two(ap):
            return ap.rearrange("p (a b) -> p a b", a=2)

        def pr(ap):
            return ap[:, 0:SEQ].rearrange("p (a b) -> p a b", a=TILES)

        def tile(ap, c):
            return ap[:, c * P:c * P + P]

        def sm(ap, rows=SMP):
            return ap[0:rows, SEQ:SEQ + SMP]

        def smw(ap):
            return ap[0:SMP, SEQ:SEQ + P]

        def g4(i):
            return g(i).rearrange("p (a b) -> p a b", a=TILES)

        def hcol(kind):
            return hc[:, 5 * kind:5 * kind + TILES].unsqueeze(2).to_broadcast([P, TILES, P])

        def hcol_s(kind, width):
            return hc[0:SMP, 5 * kind + 4:5 * kind + 5].to_broadcast([SMP, width])

        def seqs(ap, first, width, start, n):
            return ap[:, first:first + NS * width].rearrange("p (s t) -> p s t", s=NS)[
                :, :, start:start + n]

        EXTS = (v["extq"], v["extk"], v["extv"])
        CONV = (v["qc"], v["kc"], v["vc"])
        G, GAM, EGAM, KOF, BETA = range(5)
        c_s = (v["cs0"], v["cs1"])
        u_all = v["dm"]

        raw_landed = [sem(f"raw_landed{r}") for r in range(RING)]
        consts_landed, x_landed, taps_landed = sem("consts_landed"), [sem(f"x_landed{i}") for i in range(KB // 2)], sem("taps_landed")
        log_landed, halo_landed, ss_landed = sem("log_landed"), sem("halo_landed"), sem("ss_landed")
        x_again = sem("x_again")
        states_stored, crows_stored, qrows_stored = sem("states_stored"), sem("crows_stored"), sem("qrows_stored")
        y_stored = sem("y_stored")
        w_high, w_low, job_done = sem("w_high"), sem("w_low"), sem("job_done")
        act_read = sem("act_read")
        dve_read = sem("dve_read")
        in_ready = sem("in_ready")
        squares, sums, scale = sem("squares"), sem("sums"), sem("scale")
        x_scaled, high_ready = sem("x_scaled"), sem("high_ready")
        log_ps, log_zero, log_act, log_dve = sem("log_ps"), sem("log_zero"), sem("log_act"), sem("log_dve")
        cum_ps, cols_ready = sem("cum_ps"), sem("cols_ready")
        gext_ready, halo_used = sem("gext_ready"), sem("halo_used")
        conv4, conv4_done, act_conv = sem("conv4"), sem("conv4_done"), sem("act_conv")
        conv31, conv31_done, conf_ready, csum_done = sem("conv31"), sem("conv31_done"), sem("conf_ready"), sem("csum_done")
        taps_cur = sem("taps_cur")
        zs_ready = sem("zs_ready")
        crows_ready, qrows_ready = sem("crows_ready"), sem("qrows_ready")
        hc_ready, gtri_ready, gm_ready = sem("hc_ready"), sem("gtri_ready"), sem("gm_ready")
        kq_sq, kq_sums, kq_scale, kq_ready = sem("kq_sq"), sem("kq_sums"), sem("kq_scale"), sem("kq_ready")
        k_tr, v_tr, gk_ready, vt_ready = sem("k_tr"), sem("v_tr"), sem("gk_ready"), sem("vt_ready")
        gam_ps, kk_ps, qk_ps = sem("gam_ps"), sem("kk_ps"), sem("qk_ps")
        dm_diff, eg_ready, dm_ready, db_ready = sem("dm_diff"), sem("eg_ready"), sem("dm_ready"), sem("db_ready")
        at_ready, qk_ready, qd_ready, c_ready = sem("at_ready"), sem("qk_ready"), sem("qd_ready"), sem("c_ready")
        c_tr, t_ready, u0_ready, ui_ready = sem("c_tr"), sem("t_ready"), sem("u0_ready"), sem("ui_ready")
        x_ps, x_ready, dt_ps, du_ps = sem("x_ps"), sem("x_ready"), sem("dt_ps"), sem("du_ps")
        kd_ps, kd_ready, kdm_ready = sem("kd_ps"), sem("kd_ready"), sem("kdm_ready")
        u_ps, u_ready, s_ps, s_ready = sem("u_ps"), sem("u_ready"), sem("s_ps"), sem("s_ready")
        us_ps, us_ready, um_ready, os_ps = sem("us_ps"), sem("us_ready"), sem("um_ready"), sem("os_ps")
        o_ps, o_read, o_sq, o_sums = sem("o_ps"), sem("o_read"), sem("o_sq"), sem("o_sums")
        o_scale, o_scaled, ss_decayed, ss_ps = sem("o_scale"), sem("o_scaled"), sem("ss_decayed"), sem("ss_ps")
        ss_ready, head_out = sem("ss_ready"), sem("head_out")
        mu_ps, mu_ready, xc_ready, xc_sq = sem("mu_ps"), sem("mu_ready"), sem("xc_ready"), sem("xc_sq")
        var_ps = sem("var_ps")
        ln_scale, ln_scaled, b_silu, b_gated = sem("ln_scale"), sem("ln_scaled"), sem("b_silu"), sem("b_gated")
        mixed = sem("mixed")
        y_sq, y_sum, ms_ps, ms_scale = sem("y_sq"), sem("y_sum"), sem("ms_ps"), sem("ms_scale")
        y_scaled, mid_ready = sem("y_scaled"), sem("mid_ready")
        mid_sq, ms2_ps, ms2_log = sem("mid_sq"), sem("ms2_ps"), sem("ms2_log")
        f_ready, f_high = sem("f_ready"), sem("f_high")
        out_sq, ms3_ps, var3, ms3_log = sem("out_sq"), sem("ms3_ps"), sem("var3"), sem("ms3_log")
        expo, out_scale, out_scaled, y_ready = sem("expo"), sem("out_scale"), sem("out_scaled"), sem("y_ready")

        def last(n):
            return isinstance(n, int) and n == H

        def first(n):
            return isinstance(n, int) and n == 0

        def jobs(n):
            return FIRST if first(n) else LAST if last(n) else MIDDLE

        def done_slot(n, j):
            return LAST_SEGS[4 * j + 3] if last(n) else 4 * j + 3

        mid_sum, out_sum = sem("mid_sum"), sem("out_sum")
        o_log, f_square, tmi_ready = sem("o_log"), sem("f_square"), sem("tmi_ready")
        masks_landed, x_scaled_p, pair_sums = sem("masks_landed"), sem("x_scaled_p"), sem("pair_sums")
        y_scaled_p, y_ready_p, out_scaled_p = sem("y_scaled_p"), sem("y_ready_p"), sem("out_scaled_p")
        b_gated_d, out_gained = sem("b_gated_d"), sem("out_gained")
        ln_scaled_p, c1_ready = sem("ln_scaled_p"), sem("c1_ready")

        block = ctx.enter_context(nc.Block())

        @block.sync
        def _(sp):
            def weights(m, off):
                j = 8 * m + off
                if not (isinstance(j, int) and j < RING):
                    sp.wait_ge(w_high, j - RING + 1)
                    sp.wait_ge(w_low, j - RING + 1)
                sp.dma_start(raw[:, off % RING], w_all[j] if isinstance(j, int) else
                             w_all[bass.ds(j, 1)].rearrange("a p k c -> p (a k) c")).then_inc(
                                 raw_landed[off % RING], 16)

            for k in range(0, KB, 2):
                sp.dma_start(xt[:, k:k + 2], x_t[:, k:k + 2]).then_inc(x_landed[k // 2], 16)
            sp.dma_start(cst[:], consts[:, 0:WIDE]).then_inc(consts_landed, 16)
            sp.dma_start(par[:], params).then_inc(consts_landed, 16)
            for j in range(2):
                weights(0, j)
            sp.dma_start(tap[:], taps).then_inc(taps_landed, 16)
            sp.dma_start(mask_in, consts[:, WIDE:CONSTS]).then_inc(masks_landed, 16)
            sp.dma_start(lpar[:], log_par).then_inc(log_landed, 16)
            sp.dma_start(wlog[:], w_log).then_inc(log_landed, 16)
            for j in range(2, 5):
                weights(0, j)

            def phase(n):
                if first(n):
                    sp.dma_start(halo[:], halos[0]).then_inc(halo_landed, 16)
                for j in jobs(n):
                    weights(n, j + 2)
                if not last(n):
                    sp.wait_ge(halo_used, 4 * n + 4)
                    sp.dma_start(halo[:], halos[n + 1] if isinstance(n, int) else
                                 halos[bass.ds(n + 1, 1)].rearrange("a p c -> (a p) c")).then_inc(
                                     halo_landed, 16)
                    sp.wait_ge(crows_ready, n + 1)
                    sp.dma_start(conf_rows[n] if isinstance(n, int) else
                                 conf_rows[bass.ds(n, 1)].rearrange("a p c -> (a p) c"),
                                 c_rows[:]).then_inc(crows_stored, 16)
                if not first(n):
                    d = n - 1
                    sp.wait_ge(s_ready, TILES * n)
                    sp.dma_start(s_prompt[d] if isinstance(n, int) else
                                 s_prompt[bass.ds(d, 1)].rearrange("a p c -> (a p) c"),
                                 v["s"]).then_inc(states_stored, 16)
                    sp.wait_ge(ss_ready, n + 1)
                    sp.dma_start(s_sample[d] if isinstance(n, int) else
                                 s_sample[bass.ds(d, 1)].rearrange("a p c -> (a p) c"),
                                 v["ss"]).then_inc(states_stored, 16)
                if not last(n):
                    sp.wait_ge(qrows_ready, 3 * n + 3)
                    sp.dma_start(qkv_rows[n] if isinstance(n, int) else
                                 qkv_rows[bass.ds(n, 1)].rearrange("a p c -> (a p) c"),
                                 q_rows[:]).then_inc(qrows_stored, 16)
                    if not first(n):
                        sp.wait_ge(states_stored, 32 * n)
                    sp.dma_start(v["ss"], s_in[n] if isinstance(n, int) else
                                 s_in[bass.ds(n, 1)].rearrange("a p c -> (a p) c")).then_inc(
                                     ss_landed, 16)

            phase(0)
            with sp.Fori(1, H) as n:
                phase(n)
            phase(H)
            sp.wait_ge(states_stored, 32 * H)
            for off in (5, 6, 7):
                weights(8, off)
            sp.wait_ge(head_out, H + 1)
            sp.dma_start(xt[:], x_t).then_inc(x_again, 16)
            with sp.Fori(9, 9 + 2 * FFN_GROUPS) as m:
                for off in range(8):
                    weights(m, off)
            for k in STORE_ORDER:
                if k in POOL_BLOCKS:
                    sp.wait_ge(y_ready_p, POOL_BLOCKS.index(k) + 1)
                else:
                    sp.wait_ge(y_ready, k + 1 - len(POOL_BLOCKS))
                sp.dma_start(y_out[:, k], o_a[:, k]).then_inc(y_stored, 16)
            sp.wait_ge(y_stored, 16 * KB)
            sp.wait_ge(crows_stored, 16 * H)
            sp.wait_ge(qrows_stored, 16 * H)

        @block.tensor
        def _(pe):
            mm = nc.tensor.matmul

            def segment(m, off, i, hi, lo, waits=None, free=()):
                if i == 0:
                    pe.wait_ge(w_high, 8 * m + off + 1)
                    pe.wait_ge(w_low, 8 * m + off + 1)
                    for s_, n_ in free:
                        pe.wait_ge(s_, n_)
                w = off % 2
                for k in (2 * i, 2 * i + 1):
                    if waits:
                        pe.wait_ge(waits[0], waits[1] + k + 1)
                    for p3, (a, b) in enumerate(((w_hi, hi), (w_lo, hi), (w_hi, lo))):
                        for h in range(2):
                            r = mm(ps[:, 2 * w + h, 0:HALF], a[:, w, k],
                                   b[:, k, h * HALF:(h + 1) * HALF],
                                   start=k == 0 and p3 == 0, stop=k == KB - 1 and p3 == 2)
                if i == 3:
                    r.then_inc(job_done, 1)

            def pair(m, hi, lo, ready, free):
                pe.wait_ge(w_high, 8 * m + 2)
                pe.wait_ge(w_low, 8 * m + 2)
                if free:
                    pe.wait_ge(act_read, free)
                for k in range(KB):
                    pe.wait_ge(in_ready, ready + k + 1)
                    for w in range(2):
                        for p3, (a, b) in enumerate(((w_hi, hi), (w_lo, hi), (w_hi, lo))):
                            for h in range(2):
                                r = mm(ps[:, 2 * w + h, 0:HALF], a[:, w, k],
                                       b[:, k, h * HALF:(h + 1) * HALF],
                                       start=k == 0 and p3 == 0, stop=k == KB - 1 and p3 == 2)
                        if k == KB - 1:
                            r.then_inc(job_done, 1)

            def ones_sum(dst, src, start=True, stop=True):
                for h in range(2):
                    r = mm(dst[:, h], con("ones"), src[:, h * HALF:(h + 1) * HALF],
                           start=start, stop=stop)
                return r

            pe.wait_ge(consts_landed, 32)
            for k in range(0, KB, 2):
                pe.wait_ge(pair_sums, k // 2 + 1)
                r = ones_sum(g2(0), conf[:, k], k == 0, k == KB - 2)
            r.then_inc(sums, 1)

            def logits():
                pe.wait_ge(log_landed, 32)
                pe.wait_ge(log_zero, 1)
                for t in range(5):
                    n = P if t < TILES else SMP
                    for k in range(KB):
                        for part in (in_hi, in_lo):
                            r = mm(g(3)[0:n, 16 * t:16 * t + 16],
                                   part[:, k, P * t:P * t + n].bitcast(F32),
                                   wlog[:, 16 * k:16 * k + 16],
                                   start=k == 0 and part is in_hi, stop=k == KB - 1 and part is in_lo)
                r.then_inc(log_ps, 1)

            def decay_sums():
                pe.wait_ge(log_dve, 4)
                for i, (a, b) in enumerate((("tri", "tri_s"), ("suf", "suf_s"))):
                    mm(g(2)[:, 64 * i:64 * i + 32], con(a), cols[:, 0:32], start=True, stop=True)
                    r = mm(g(2)[0:SMP, 64 * i + 32:64 * i + 40], con(b, SMP), cols[0:SMP, 32:40],
                           start=True, stop=True)
                r.then_inc(cum_ps, 1)

            def phase(n):
                gdn, proj = not first(n), not last(n)
                segs = 0
                for s in range(32):
                    if last(n):
                        if s in LAST_SEGS:
                            i = LAST_SEGS.index(s)
                            segment(n, i // 4 - 3, i % 4, in_hi, in_lo,
                                    free=[(act_read, 8 * n + i // 4 - 4)])
                    elif first(n) and s == 12:
                        pair(0, in_hi, in_lo, 0, None)
                    elif gdn or s >= 20:
                        j = s // 4
                        fr = [(act_read, 8 * n + j - 4)]
                        segment(n, j - 3, s % 4, in_hi, in_lo, free=fr)
                    if first(n) and s == 19:
                        logits()
                    if first(n) and s == 22:
                        decay_sums()
                    if not gdn:
                        continue
                    if s == 0:
                        pe.wait_ge(ss_ready, n)
                        pe.wait_ge(kq_sq, 2 * n - 1)
                        ones_sum(g2(0), v["vt"]).then_inc(kq_sums, 1)
                        pe.wait_ge(o_log, n)
                        pe.wait_ge(kq_sq, 2 * n)
                        ones_sum(g2(2), v["gk"]).then_inc(kq_sums, 1)
                    if s == 2:
                        pe.wait_ge(kq_scale, 4 * n - 1)
                        pe.wait_ge(kq_ready, 2 * n - 1)
                        for c in range(TILES):
                            nc.tensor.transpose(tile(g(0), c), tile(v["kn"], c), con("ident"))
                        nc.tensor.transpose(g(2)[0:SMP, 0:P], sm(v["kn"], P), con("ident")).then_inc(k_tr, 1)
                        for c in range(TILES):
                            nc.tensor.transpose(tile(g(1), c), tile(v["vc"], c), con("ident"))
                        nc.tensor.transpose(g(3)[0:SMP, 0:P], sm(v["vc"], P), con("ident")).then_inc(v_tr, 1)
                    if s == 3:
                        pe.wait_ge(gtri_ready, n)
                        pe.wait_ge(vt_ready, n)
                        mm(g(1), con("ones"), v["dm"][:, 0:SEQ], start=True, stop=True)
                        mm(g(3)[:, 0:SMP], con("ones", SMP), sm(v["dm"]), start=True,
                           stop=True).then_inc(gam_ps, 1)
                    if s == 4:
                        pe.wait_ge(gk_ready, n)
                        for c in range(TILES):
                            mm(tile(g(0), c), tile(v["kn"], c), tile(v["kn"], c), start=True, stop=True)
                        mm(g(2)[0:SMP, 0:SMP], sm(v["kn"], P), sm(v["kn"], P), start=True,
                           stop=True).then_inc(kk_ps, 1)
                    if s == 5:
                        pe.wait_ge(eg_ready, n)
                        pe.wait_ge(kq_ready, 2 * n)
                        for c in range(TILES):
                            mm(tile(g(1), c), tile(v["kn"], c), tile(v["qn"], c), start=True, stop=True)
                        mm(g(3)[0:SMP, 0:SMP], sm(v["kn"], P), sm(v["qn"], P), start=True,
                           stop=True).then_inc(qk_ps, 1)
                    if s == 7:
                        pe.wait_ge(c1_ready, n)
                        for c in range(TILES):
                            nc.tensor.transpose(tile(g(0), c), tile(c_r[0], c).bitcast(F32), con("ident"))
                        nc.tensor.transpose(g(2)[0:SMP, 0:SMP], c_s[0][0:SMP],
                                            con("ident", SMP)[:, 0:SMP]).then_inc(c_tr, 1)
                    if s in range(8, 21, 2):
                        l = (s - 4) // 2
                        w, t = c_r[(l - 1) % 2], t_r
                        if l == STEPS:
                            w, t = v["db"], t_r.bitcast(F32)
                        pe.wait_ge(c_ready, LEVELS * n - 8 + l)
                        pe.wait_ge(t_ready, LEVELS * n - 8 + l)
                        for c in range(TILES):
                            r = mm(tile(g(0), c), tile(w, c), tile(t, c),
                                   start=True, stop=True)
                        if l <= LEVELS_S:
                            r = mm(g(2)[0:SMP, 0:SMP], c_s[(l - 1) % 2][0:SMP], sm(v["dm"]), start=True, stop=True)
                        r.then_inc(x_ps, 1)
                    if s in range(9, 22, 2):
                        l = (s - 5) // 2
                        pe.wait_ge(x_ready, LEVELS * n - 8 + l)
                        if l == 2:
                            pe.wait_ge(u0_ready, n)
                        else:
                            pe.wait_ge(ui_ready, LEVELS * n - 9 + l)
                        if l <= LEVELS:
                            for c in range(TILES):
                                r = mm(tile(g(0), c), tile(u_r, c), tile(x_r, c), start=True, stop=True)
                            if l < LEVELS_S:
                                r = mm(g(2)[0:SMP, 0:SMP], v["us"][0:SMP], sm(v["db"]), start=True, stop=True)
                            r.then_inc(dt_ps, 1)
                        for c in range(TILES):
                            r = mm(tile(g(1), c), tile(x_r, c), tile(u_r, c), start=True, stop=True)
                        if l <= LEVELS_S:
                            r = mm(g(3)[0:SMP, 0:SMP], sm(v["db"]), v["us"][0:SMP], start=True, stop=True)
                        r.then_inc(du_ps, 1)
                    if s == 22:
                        pe.wait_ge(ui_ready, LEVELS * n)
                        for c in range(TILES):
                            mm(tile(g(0), c), tile(v["gk"], c), tile(u_all, c), start=True, stop=True)
                        mm(g(2)[:, 0:SMP], smw(v["gk"]), v["us"][0:SMP], start=True,
                           stop=True).then_inc(kd_ps, 1)
                    if s in (22, 24, 26, 28):
                        c = (s - 22) // 2
                        if c:
                            pe.wait_ge(s_ready, TILES * n - 4 + c)
                        r = mm(g(1)[:, 0:P], tile(u_all, c), tile(v["vt"], c), start=True,
                               stop=c == 0)
                        if c:
                            r = mm(g(1)[:, 0:P], tile(v["kn"], c), v["s"], start=False, stop=True)
                        r.then_inc(u_ps, 1)
                        if c:
                            mm(tile(g(3), c), v["s"], tile(v["qn"], c), start=True, stop=False)
                    if s in (23, 25, 27, 29):
                        c = (s - 23) // 2
                        if c == 0:
                            pe.wait_ge(kd_ready, 2 * n - 1)
                            pe.wait_ge(qd_ready, n)
                        pe.wait_ge(u_ready, TILES * n - 3 + c)
                        mm(g(0)[:, 0:P], tile(v["ko"], c), tile(v["u"], c), start=True,
                           stop=True).then_inc(s_ps, 1)
                        r = mm(tile(g(3), c), tile(v["u"], c), tile(v["qk"], c), start=c == 0, stop=True)
                        if c == TILES - 1:
                            r.then_inc(o_ps, 1)
                    if s == 25:
                        pe.wait_ge(kdm_ready, n)
                        pe.wait_ge(kd_ready, 2 * n)
                        pe.wait_ge(ss_landed, 16 * n)
                        pe.nop(nofuse=True)
                        mm(g(2)[0:SMP, 0:P], v["us"][0:SMP], smw(v["vt"]), start=True, stop=False)
                        for q in range(NS):
                            r = mm(g(2)[0:SMP, 0:P], v["um"][:, q * SMP:(q + 1) * SMP],
                                   tile(v["ss"], q), start=False, stop=q == NS - 1)
                        r.then_inc(us_ps, 1)
                    if s == 27:
                        pe.wait_ge(us_ready, n)
                        mm(g(2)[:, 0:SMP], smw(v["u"]), sm(v["qk"]), start=True, stop=True)
                        for q in range(NS):
                            cols_q = slice(q * LS, (q + 1) * LS)
                            r = mm(g(2)[:, cols_q], tile(v["ss"], q), sm(v["qn"], P)[:, cols_q],
                                   start=False, stop=True, skip_group_check=True)
                        r.then_inc(os_ps, 1)
                    if s == 30:
                        pe.wait_ge(um_ready, n)
                        pe.wait_ge(s_ready, TILES * n)
                        for q in range(2):
                            r = mm(g(q), smw(v["ko"]), v["um"][0:SMP, q * SEQ:(q + 1) * SEQ],
                                   start=True, stop=True)
                        r.then_inc(ss_ps, 1)
                    if s == 31:
                        pe.wait_ge(o_sq, n)
                        pe.wait_ge(o_read, 2 * n)
                        ones_sum(g2(2), v["gk"]).then_inc(o_sums, 1)
                    if last(n) and s == 18:
                        pe.wait_ge(csum_done, H + 1)
                        pe.wait_ge(act_read, 63)
                        ones_sum(job_ps(0), csum).then_inc(mu_ps, 1)
                    if last(n) and 21 <= s < 29:
                        k = s - 21
                        pe.wait_ge(xc_sq, k + 1)
                        ones_sum(job_ps(0), v[("c4", "extq")[k % 2]][:, 0:TOK], k == 0,
                                 k == KB - 1).then_inc(var_ps, 1)

            phase(0)
            with pe.Fori(1, H) as n:
                phase(n)
            phase(H)

            pe.wait_ge(ln_scale, 1)
            pair(8, in_hi, in_lo, 8, 64)
            for j in range(2, 8):
                for i in range(4):
                    segment(8, j, i, in_hi, in_lo, free=[(act_read, 64 + j - 1)])
            pe.wait_ge(y_sum, 8)
            ones_sum(g2(0), csum).then_inc(ms_ps, 1)

            def group(gr, tail=False):
                m = 2 * gr + 9
                if first(gr):
                    pair(9, in_hi, in_lo, 16, 72)
                for j in range(2 if first(gr) else 0, 8):
                    free = [(dve_read, 8 * gr + 7 + j)] if j < 2 else [(act_read, 8 * gr + 72 + j - 1)]
                    for i in range(4):
                        segment(m, j, i, in_hi, in_lo, free=free)
                for j in range(8):
                    free = [(act_read, 8 * gr + 79 + j)] if j < 2 else [(dve_read, 8 * gr + 8 + j - 1)]
                    for i in range(4):
                        segment(m + 1, j, i, f_hi, f_lo, waits=(f_ready, 8 * gr) if j == 0 else None, free=free)
                    if tail and j == 0:
                        pe.wait_ge(mid_sum, 8)
                        ones_sum(g2(0), csum).then_inc(ms2_ps, 1)

            group(0)
            with pe.Fori(1, FFN_GROUPS - 1) as gr:
                group(gr)
            group(FFN_GROUPS - 1, tail=True)
            pe.wait_ge(out_sum, 8)
            ones_sum(g2(2), gate[:, 5]).then_inc(ms3_ps, 1)

        def split_off(n, s):
            if last(n):
                return {0: -2, LAST_SEGS[3] + 1: -1, LAST_SEGS[7] + 1: 0}.get(s)
            if s % 4 or s == 32 or (first(n) and s < 16):
                return None
            return s // 4 - 2

        def conv_slots(n, d):
            return (24 + d, 28 + d, 32) if first(n) else (4 + 2 * d, 8 + 3 * d // 2, 12 + 3 * d // 2)

        def evac(n, s):
            for j, kind in jobs(n).items():
                if done_slot(n, j) + 1 == s:
                    return j, kind
            return None, None

        @block.scalar
        def _(act):
            A = nc.scalar.activation

            def log_exp():
                act.preload_act_table_set("natural_log_exp_and_others")

            def split(m, off):
                act.wait_ge(raw_landed[off % RING], 32 * m + 16 * (off // RING) + 16)
                if not (isinstance(m, int) and 8 * m + off < 2):
                    act.wait_ge(job_done, 8 * m + off - 1)
                nc.scalar.copy(w_hi[:, off % 2], raw[:, off % RING]).then_inc(w_high, 1)

            act.sem_inc(o_log, 1)
            for k in range(4):
                act.wait_ge(x_landed[k], 16)
                A(conf[:, 2 * k:2 * k + 2], xt[:, 2 * k:2 * k + 2], ACT.Square).then_inc(squares, 1)
            act.wait_ge(consts_landed, 32)
            for j in range(2):
                split(0, j)
            log_exp()
            act.wait_ge(sums, 1)
            A(two(v["c31"]), g2(0), ACT.Ln, scale=1.0 / D, bias=con("eps")).then_inc(scale, 1)
            act.wait_ge(scale, 1)
            A(v["c31"], v["c31"], ACT.Exp, scale=-0.5).then_inc(scale, 1)
            for k in range(KB):
                act.wait_ge(x_scaled_p if k % 2 else x_scaled, k // 2 + 1)
                A(in_hi[:, k], o_a[:, k], ACT.Copy, scale=pcol("pre_mix", k)).then_inc(high_ready, 1)

            def logits():
                sc = v["gk"]
                lp = g(3)[:, 0:80].rearrange("p (t c) -> p t c", t=5)
                log_exp()
                act.wait_ge(log_landed, 32)
                A(sc[:, 160:168], lpar[:, H:2 * H], ACT.Exp)
                act.wait_ge(log_dve, 1)
                A(cols[:, 160:200].rearrange("p (t h) -> p t h", t=5), lp[:, :, 0:H],
                  ACT.Sigmoid).then_inc(log_act, 1)
                A(sc[:, 40:80], sc[:, 0:40], ACT.Abs).then_inc(log_act, 1)
                act.wait_ge(log_act, 2)
                A(sc[:, 80:120], sc[:, 40:80], ACT.Exp, scale=-1.0).then_inc(log_act, 1)
                act.wait_ge(log_act, 3)
                A(sc[:, 120:160], sc[:, 80:120], ACT.Ln, bias=1.0).then_inc(log_act, 1)

            def decay_exps():
                act.wait_ge(log_dve, 5)
                A(cols[:, 80:120], g(2)[:, 0:40], ACT.Exp).then_inc(cols_ready, 1)
                A(cols[:, 120:160], g(2)[:, 64:104], ACT.Exp).then_inc(cols_ready, 1)

            def conv_silu(n, i):
                act.wait_ge(conv4_done, 3 * n + i + 1)
                A(CONV[i], v["c4"], ACT.Silu).then_inc(act_conv, 1)

            def square_k(n):
                act.wait_ge(act_conv, 3 * n + 2)
                A(v["vt"][:, 0:TOK], v["kc"], ACT.Square).then_inc(kq_sq, 1)

            def square_q():
                A(v["gk"][:, 0:TOK], v["qc"], ACT.Square).then_inc(kq_sq, 1)

            def phase(n):
                gdn = not first(n)
                for s in range(33):
                    off = split_off(n, s)
                    if off is not None:
                        split(n, off)
                    pos, j = evac(n, s)
                    if pos is not None:
                        act.wait_ge(job_done, 8 * n - 2 + pos)
                        src = job_ps((pos + 1) % 2)
                        if j == Z:
                            A(two(v["zs"]), src, ACT.Silu).then_inc(act_read, 1)
                        if j == GA:
                            act.wait_ge(gext_ready, n if last(n) else n + 1)
                            A(two(v["sig"]), src, ACT.Sigmoid).then_inc(act_read, 1)
                        if j == GB:
                            dst = gate[:, n - 1] if isinstance(n, int) else gate[:, bass.ds(n - 1, 1)]
                            A(dst.rearrange("p (a b) -> p a b", a=2) if isinstance(n, int) else
                              dst.rearrange("p o (a b) -> p (o a) b", a=2), src,
                              ACT.Sigmoid if last(n) else ACT.Copy).then_inc(act_read, 1)
                        if j == CA:
                            if gdn:
                                act.wait_ge(act_conv, 3 * n + 3)
                            A(two(v["c4"]), src, ACT.Copy).then_inc(act_read, 1)
                        if j == CB:
                            if gdn:
                                act.wait_ge(zs_ready, n)
                            A(two(v["sig"]), src, ACT.Sigmoid).then_inc(act_read, 1)
                        if j is not None and j >= Q:
                            e = EXTS[j - Q]
                            if gdn:
                                act.wait_ge(qrows_ready, 3 * n - 2 + j - Q)
                            A(e[:, 3:3 + HALF], src[:, 0], ACT.Copy)
                            A(e[:, 3 + HALF:EXT], src[:, 1, 0:SEQ - HALF], ACT.Copy)
                            A(seqs(e, EXT, EXS, 3, LS),
                              src[:, 1, SEQ - HALF:HALF].rearrange("p (s t) -> p s t", s=NS),
                              ACT.Copy).then_inc(act_read, 1)
                    if not last(n) and s in conv_slots(n, 2)[not first(n):]:
                        conv_silu(n, conv_slots(n, 2).index(s))
                    if first(n) and s == 20:
                        logits()
                    if first(n) and s == 23:
                        decay_exps()
                    if gdn and s == (12 if last(n) else 19):
                        act.wait_ge(conv31_done, n)
                        dst = conf[:, n - 1] if isinstance(n, int) else \
                            conf[:, bass.ds(n - 1, 1)].rearrange("p a b -> p (a b)")
                        A(dst, v["c31"], ACT.Identity, bias=ct[:, CF_TAPS:CF_TAPS + 1]).then_inc(conf_ready, 1)
                    if first(n) and s == 31:
                        square_k(n)
                        square_q()
                    if last(n) and 17 <= s < 24:
                        act.wait_ge(act_read, 61)
                        A(gate[:, s - 17], gate[:, s - 17], ACT.Sigmoid)
                    if last(n) and s == 19:
                        act.wait_ge(mu_ps, 1)
                        A(two(csum[:]), job_ps(0), ACT.Copy, scale=1.0 / D).then_inc(mu_ready, 1)
                    if not gdn:
                        continue
                    if s == 0:
                        act.wait_ge(head_out, n)
                        act.wait_ge(kq_sums, 2 * n - 1)
                        A(two(v["at"]), g2(0), ACT.Ln, bias=con("eps")).then_inc(kq_scale, 1)
                        act.wait_ge(kq_scale, 4 * n - 3)
                        A(v["at"], v["at"], ACT.Exp, scale=-0.5).then_inc(kq_scale, 1)
                        act.wait_ge(kq_sums, 2 * n)
                        A(two(v["db"]), g2(2), ACT.Ln, scale=float(P), bias=con("eps128")).then_inc(kq_scale, 1)
                        act.wait_ge(kq_scale, 4 * n - 1)
                        A(v["db"], v["db"], ACT.Exp, scale=-0.5).then_inc(kq_scale, 1)
                    if s == 2:
                        act.wait_ge(v_tr, n)
                        A(v["vt"][:, 0:SEQ], g(1), ACT.Copy)
                        A(smw(v["vt"]), g(3)[0:SMP, 0:P], ACT.Copy).then_inc(vt_ready, 1)
                    if s == 3:
                        act.wait_ge(dm_diff, n)
                        A(v["dm"][:, 0:SEQ], v["dm"][:, 0:SEQ], ACT.Exp)
                        A(sm(v["dm"]), sm(v["dm"]), ACT.Exp).then_inc(dm_ready, 1)
                        A(v["eg"][:, 0:SEQ], g(1), ACT.Exp)
                        A(sm(v["eg"], P), g(3)[:, 0:SMP], ACT.Exp).then_inc(eg_ready, 1)
                    if s in range(8, 19, 2):
                        l = (s - 4) // 2
                        act.wait_ge(x_ps, LEVELS * n - 8 + l)
                        r = A(x_r[:], g(0), ACT.Copy)
                        if l <= LEVELS_S:
                            r = A(sm(v["db"]), g(2)[0:SMP, 0:SMP], ACT.Copy)
                        r.then_inc(x_ready, 1)
                        if s == 8 and not last(n):
                            conv_silu(n, 0)
                    if s == 22:
                        act.wait_ge(kd_ps, n)
                        A(v["kn"][:, 0:SEQ], g(0), ACT.Copy, scale=-1.0).then_inc(kd_ready, 1)
                        A(sm(v["kn"], P), g(2)[:, 0:SMP], ACT.Copy, scale=-1.0).then_inc(kd_ready, 1)
                    if s in (22, 24, 26, 28):
                        c = (s - 22) // 2
                        act.wait_ge(u_ps, TILES * n - 3 + c)
                        A(tile(v["u"], c), g(1)[:, 0:P], ACT.Copy,
                          scale=hc[:, 5 * BETA + c:5 * BETA + c + 1]).then_inc(u_ready, 1)
                    if s == 25:
                        act.wait_ge(us_ps, n)
                        A(smw(v["u"]), g(2)[0:SMP, 0:P], ACT.Copy,
                          scale=hc[0:SMP, 5 * BETA + 4:5 * BETA + 5]).then_inc(us_ready, 1)
                    if s == 27:
                        act.wait_ge(os_ps, n)
                        dst = o_a[:, n - 1, SEQ:TOK] if isinstance(n, int) else \
                            o_a[:, bass.ds(n - 1, 1), SEQ:TOK].rearrange("p a b -> p (a b)")
                        A(v["gk"][:, SEQ:TOK], g(2)[:, 0:SMP], ACT.Square)
                        A(dst, g(2)[:, 0:SMP], ACT.Copy).then_inc(o_read, 1)
                    if s == 29:
                        act.wait_ge(o_ps, n)
                        dst = o_a[:, n - 1, 0:SEQ] if isinstance(n, int) else \
                            o_a[:, bass.ds(n - 1, 1), 0:SEQ].rearrange("p a b -> p (a b)")
                        A(v["gk"][:, 0:SEQ], g(3), ACT.Square).then_inc(o_sq, 1)
                        A(dst, g(3), ACT.Copy).then_inc(o_read, 1)
                    if s == 31:
                        log_exp()
                        if last(n):
                            act.wait_ge(var_ps, 8)
                            A(two(v["c31"]), job_ps(0), ACT.Ln, scale=1.0 / D, bias=con("eps")).then_inc(ln_scale, 1)
                            act.wait_ge(ln_scale, 1)
                            A(v["c31"], v["c31"], ACT.Exp, scale=-0.5).then_inc(ln_scale, 1)
                        else:
                            square_k(n)
                        act.wait_ge(o_sums, n)
                        A(two(v["at"]), g2(2), ACT.Ln, scale=1.0 / P, bias=con("eps")).then_inc(o_log, 1)
                        act.wait_ge(o_log, n + 1)
                        A(v["at"], v["at"], ACT.Exp, scale=-0.5).then_inc(o_scale, 1)
                        if not last(n):
                            square_q()
                    if last(n) and 20 <= s < 28:
                        k = s - 20
                        act.wait_ge(xc_ready, k + 1)
                        if k >= 2:
                            act.wait_ge(var_ps, k - 1)
                        A(v[("c4", "extq")[k % 2]][:, 0:TOK], conf[:, k], ACT.Square).then_inc(xc_sq, 1)

            phase(0)
            log_exp()
            with act.Fori(1, H) as n:
                phase(n)
            phase(H)
            split(8, 1)
            for k in range(KB + 4):
                if k < KB:
                    act.wait_ge(ln_scaled if k < 4 else ln_scaled_p, k % 4 + 1)
                    A(conf[:, k], conf[:, k], ACT.Silu, scale=pcol("ln_g", k),
                      bias=pcol("ln_b", k)).then_inc(b_silu, 1)
                if k >= 4:
                    act.wait_ge(mixed, k - 3)
                    A(in_hi[:, k - 4], conf[:, k - 4], ACT.Copy).then_inc(high_ready, 1)

            for j in range(8):
                if j == 7:
                    log_exp()
                else:
                    split(8, j + 2)
                act.wait_ge(job_done, 65 + j)
                A(two(gate[:, j]), job_ps(j % 2), ACT.Copy).then_inc(act_read, 1)
                act.wait_ge(act_read, 65 + j)
                if j >= 2:
                    act.wait_ge(y_sum, j - 1)
                A(v[("c4", "extq")[j % 2]][:, 0:TOK], gate[:, j], ACT.Square).then_inc(y_sq, 1)
            split(8, 9)
            act.wait_ge(ms_ps, 1)
            A(two(v["c31"]), g2(0), ACT.Ln, scale=1.0 / D, bias=con("eps")).then_inc(ms_scale, 1)
            act.wait_ge(ms_scale, 1)
            A(v["c31"], v["c31"], ACT.Exp, scale=-0.5).then_inc(ms_scale, 1)
            for k in range(KB):
                act.wait_ge(mid_ready, k + 1)
                A(in_hi[:, k], conf[:, k], ACT.Copy, scale=pcol("pre_ffn", k)).then_inc(high_ready, 1)

            def group(gr, tail=False):
                m = 2 * gr + 9
                for j in range(8):
                    split(m, j + 2)
                    act.wait_ge(job_done, 16 * gr + 73 + j)
                    act.wait_ge(f_square, 8 * gr + j + 1)
                    A(two(f_tmp[:, j % 2]), job_ps(j % 2), ACT.Relu).then_inc(act_read, 1)
                    act.wait_ge(act_read, 8 * gr + 73 + j)
                    A(f_hi[:, j], f_tmp[:, j % 2], ACT.Square).then_inc(f_high, 1)
                    if tail:
                        if j >= 2:
                            act.wait_ge(mid_sum, j - 1)
                        A(v[("sig", "zs")[j % 2]], conf[:, j], ACT.Square).then_inc(mid_sq, 1)
                for j in range(8):
                    if not (tail and j >= 6):
                        split(m + 1, j + 2)
                    if tail and j == 2:
                        log_exp()
                        act.wait_ge(ms2_ps, 1)
                        A(two(gate[:, 1]), g2(0), ACT.Ln, scale=1.0 / D, bias=con("eps")).then_inc(ms2_log, 1)
                        act.wait_ge(ms2_log, 1)
                        A(gate[:, 2], gate[:, 1], ACT.Exp, scale=-2.0).then_inc(ms2_log, 1)
                    if tail:
                        act.wait_ge(dve_read, 8 * gr + 9 + j)
                        if j >= 2:
                            act.wait_ge(out_sum, j - 1)
                        else:
                            act.wait_ge(mid_sum, 7 + j)
                        A(v[("sig", "zs")[j % 2]], o_a[:, j], ACT.Square).then_inc(out_sq, 1)
                        if j in POOL_BLOCKS:
                            act.wait_ge(out_sq, j + 1)
                            A(o_a[:, j], o_a[:, j], ACT.Copy, scale=pcol("post_ffn", j)).then_inc(out_gained, 1)

            with act.Fori(0, FFN_GROUPS - 1) as gr:
                group(gr)
            group(FFN_GROUPS - 1, tail=True)
            log_exp()
            act.wait_ge(var3, 1)
            A(gate[:, 3], gate[:, 3], ACT.Ln, scale=1.0 / D, bias=con("eps")).then_inc(ms3_log, 1)
            act.wait_ge(expo, 1)
            A(gate[:, 4], gate[:, 4], ACT.Exp, scale=-1.0).then_inc(out_scale, 1)

        @block.vector
        def _(dve):
            ve = nc.vector

            def tt(out, a, b, op):
                return ve.tensor_tensor(out, a, b, op)

            def stt(out, a, s_, b, op0, op1):
                return ve.scalar_tensor_tensor(out=out, in0=a, scalar=s_, in1=b, op0=op0, op1=op1)

            ve.memset(g(3)[:, 0:80], 0.0)
            ve.memset(g(2)[:, 0:128], 0.0).then_inc(log_zero, 1)
            for e in EXTS:
                ve.memset(e[:, 0:QK_TAPS - 1], 0.0)
            ve.memset(v["gext"][:, 0:CF_TAPS - 1], 0.0)
            ve.memset(csum[:], 0.0).then_inc(csum_done, 1)
            dve.sem_inc(ss_ready, 1)
            dve.sem_inc(head_out, 1)
            dve.sem_inc(zs_ready, 1)
            dve.sem_inc(f_square, 2)
            dve.wait_ge(consts_landed, 32)
            for k in range(0, KB, 2):
                dve.wait_ge(squares, k // 2 + 1)
                tt(conf[:, k], conf[:, k], conf[:, k + 1], ALU.add).then_inc(pair_sums, 1)
            dve.wait_ge(scale, 2)
            for k in range(KB + 1):
                if k < KB and k % 2 == 0:
                    tt(o_a[:, k], xt[:, k], v["c31"], ALU.mult).then_inc(x_scaled, 1)
                if k:
                    dve.wait_ge(high_ready, k)
                    stt(in_lo[:, k - 1], o_a[:, k - 1], pcol("pre_mix", k - 1),
                        in_hi[:, k - 1].bitcast(F32), ALU.mult, ALU.subtract).then_inc(in_ready, 1)

            dve.wait_ge(masks_landed, 16)
            ve.tensor_copy(masks[:], mask_in)

            def logits():
                sc = v["gk"]
                r3 = lambda ap: ap.rearrange("p (t h) -> p t h", t=5)
                dve.wait_ge(log_ps, 1)
                lp = g(3)[:, 0:80].rearrange("p (t c) -> p t c", t=5)
                tt(r3(sc[:, 0:40]), lp[:, :, H:2 * H], lpar[:, 0:H].unsqueeze(1).to_broadcast([P, 5, H]),
                   ALU.add).then_inc(log_dve, 1)
                dve.wait_ge(log_act, 4)
                dve.wait_ge(log_dve, 1)
                stt(sc[:, 200:240], sc[:, 0:40], 0.0, sc[:, 120:160], ALU.max, ALU.add).then_inc(log_dve, 1)
                dve.wait_ge(log_dve, 2)
                stt(r3(cols[:, 0:40]), r3(sc[:, 200:240]), -1.0,
                    sc[:, 160:168].unsqueeze(1).to_broadcast([P, 5, H]), ALU.mult, ALU.mult).then_inc(log_dve, 2)

            def decay_copy():
                dve.wait_ge(cum_ps, 1)
                ve.tensor_copy(cols[:, 40:80], g(2)[:, 0:40]).then_inc(log_dve, 1)

            def tap_of(n):
                tp = tap[:].rearrange("p (h c) -> p h c", h=H)
                return tp[:, n] if isinstance(n, int) else \
                    tp[:, bass.ds(n, 1)].rearrange("p a c -> p (a c)")

            def conf_taps(h, a, b):
                ge = v["gext"]
                out_s = v["c31"][:, SEQ:TOK].rearrange("p (s t) -> p s t", s=NS)
                for t in range(a, b):
                    w = ct[:, t:t + 1]
                    if t == 0:
                        ve.tensor_scalar(v["c31"][:, 0:SEQ], ge[:, 0:SEQ], w, None, ALU.mult).then_inc(conv31, 1)
                        ve.tensor_scalar(out_s, seqs(ge, GXT, GXS, 0, LS), w, None, ALU.mult).then_inc(conv31, 1)
                        continue
                    dve.wait_ge(conv31, 62 * h + 2 * t - 1)
                    stt(v["c31"][:, 0:SEQ], ge[:, t:t + SEQ], w, v["c31"][:, 0:SEQ], ALU.mult,
                        ALU.add).then_inc(conv31, 1)
                    dve.wait_ge(conv31, 62 * h + 2 * t)
                    r = stt(out_s, seqs(ge, GXT, GXS, t, LS), w, out_s, ALU.mult, ALU.add)
                    r.then_inc(conv31, 1)

            def qkv_conv(n, i, a, b):
                e, c4 = EXTS[i], v["c4"]
                out_s = c4[:, SEQ:TOK].rearrange("p (s t) -> p s t", s=NS)
                if a == 0:
                    dve.wait_ge(act_read, 8 * n + (3 if first(n) else -2) + i)
                    dve.wait_ge(halo_used, 4 * n + 1 + i)
                if a == 0 and i == 0:
                    dve.wait_ge(gext_ready, n + 1 if first(n) else n)
                elif a == 0:
                    dve.wait_ge(act_conv, 3 * n + i)
                for t in range(a, b):
                    w = qt[:, QK_TAPS * i + t:QK_TAPS * i + t + 1]
                    if t == 0:
                        ve.tensor_scalar(c4[:, 0:SEQ], e[:, 0:SEQ], w, None, ALU.mult).then_inc(conv4, 1)
                        ve.tensor_scalar(out_s, seqs(e, EXT, EXS, 0, LS), w, None, ALU.mult).then_inc(conv4, 1)
                        continue
                    dve.wait_ge(conv4, 24 * n + 8 * i + 2 * t - 1)
                    stt(c4[:, 0:SEQ], e[:, t:t + SEQ], w, c4[:, 0:SEQ], ALU.mult, ALU.add).then_inc(conv4, 1)
                    dve.wait_ge(conv4, 24 * n + 8 * i + 2 * t)
                    r = stt(out_s, seqs(e, EXT, EXS, t, LS), w, out_s, ALU.mult, ALU.add)
                    r.then_inc(conv4, 1)
                if b == QK_TAPS:
                    dve.wait_ge(conv4, 24 * n + 8 * i + 8)
                    dve.sem_inc(conv4_done, 1)

            def head(n, s):
                if s == 0:
                    dve.wait_ge(kq_scale, 4 * n - 2)
                    tt(v["kn"], v["kc"], v["at"], ALU.mult).then_inc(kq_ready, 1)
                    dve.wait_ge(kq_scale, 4 * n)
                    tt(v["qn"], v["qc"], v["db"], ALU.mult).then_inc(kq_ready, 1)
                if s == 2:
                    dve.wait_ge(k_tr, n)
                    dve.wait_ge(hc_ready, n)
                    tt(pr(v["gk"]), g4(0), hcol(EGAM), ALU.mult)
                    tt(pr(v["ko"]), g4(0), hcol(KOF), ALU.mult)
                    tt(smw(v["gk"]), g(2)[0:SMP, 0:P], hcol_s(EGAM, P), ALU.mult)
                    tt(smw(v["ko"]), g(2)[0:SMP, 0:P], hcol_s(KOF, P), ALU.mult).then_inc(gk_ready, 1)
                if s == 3:
                    dve.wait_ge(gam_ps, n)
                    dve.wait_ge(gm_ready, n)
                    tt(v["dm"][:, 0:SEQ], g(1), v["qk"][:, 0:SEQ], ALU.subtract)
                    tt(sm(v["dm"]), g(3)[0:SMP, 0:SMP], sm(v["qk"]), ALU.subtract).then_inc(dm_diff, 1)
                if s == 4:
                    dve.wait_ge(dm_ready, n)
                    tt(pr(v["db"]), pr(v["dm"]), hcol(BETA), ALU.mult)
                    tt(sm(v["db"]), sm(v["dm"]), hcol_s(BETA, SMP), ALU.mult).then_inc(db_ready, 1)
                if s == 5:
                    dve.wait_ge(kk_ps, n)
                    dve.wait_ge(db_ready, n)
                    tt(v["at"][:, 0:SEQ], g(0), v["db"][:, 0:SEQ], ALU.mult)
                    tt(sm(v["at"]), g(2)[0:SMP, 0:SMP], sm(v["db"]), ALU.mult).then_inc(at_ready, 1)
                    dve.wait_ge(at_ready, n)
                    tt(pr(c_r[0]), pr(v["at"]), lvl(1), ALU.mult)
                    tt(c_s[0][0:SMP], sm(v["at"]), lvl_s(1), ALU.mult).then_inc(c1_ready, 1)
                    dve.wait_ge(qk_ps, n)
                    tt(v["qk"][:, 0:SEQ], g(1), v["dm"][:, 0:SEQ], ALU.mult)
                    tt(sm(v["qk"]), g(3)[0:SMP, 0:SMP], sm(v["dm"]), ALU.mult).then_inc(qk_ready, 1)
                if s == 7:
                    dve.wait_ge(c_tr, n)
                    dve.wait_ge(qk_ready, n)
                    tt(pr(t_r), con("ident").unsqueeze(1).to_broadcast([P, TILES, P]), g4(0),
                       ALU.subtract)
                    tt(sm(v["dm"]), con("ident", SMP)[:, 0:SMP], g(2)[0:SMP, 0:SMP],
                       ALU.subtract).then_inc(t_ready, 1)
                if s == 20:
                    dve.wait_ge(x_ps, LEVELS * n)
                    dve.wait_ge(tmi_ready, n)
                    tt(x_r[:], v["um"][:, 0:SEQ], g(0), ALU.add).then_inc(x_ready, 1)
                if s in range(9, 22, 2):
                    l = (s - 5) // 2
                    if l <= LEVELS:
                        dve.wait_ge(dt_ps, (LEVELS - 1) * n - 7 + l)
                        dve.wait_ge(t_ready, LEVELS * n - 8 + l)
                        r = tt(t_r[:], t_r.bitcast(F32)[:, :], g(0), ALU.subtract)
                        if l < LEVELS_S:
                            r = tt(sm(v["dm"]), sm(v["dm"]), g(2)[0:SMP, 0:SMP], ALU.subtract)
                        r.then_inc(t_ready, 1)
                    dve.wait_ge(du_ps, LEVELS * n - 8 + l)
                    if l > 2:
                        dve.wait_ge(ui_ready, LEVELS * n - 9 + l)
                    else:
                        dve.wait_ge(u0_ready, n)
                    dst = u_all[:, 0:SEQ] if l == STEPS else u_r[:]
                    r = tt(dst, u_r.bitcast(F32)[:, :], g(1), ALU.subtract)
                    if l <= LEVELS_S:
                        r = tt(v["us"][0:SMP], v["us"][0:SMP], g(3)[0:SMP, 0:SMP], ALU.subtract)
                    r.then_inc(ui_ready, 1)
                if s in (23, 25, 27, 29):
                    c = (s - 23) // 2
                    dve.wait_ge(s_ps, TILES * n - 3 + c)
                    if c == 0:
                        dve.wait_ge(ss_landed, 16 * n)
                        ve.tensor_copy(v["s"], g(0)[:, 0:P]).then_inc(s_ready, 1)
                    else:
                        dve.wait_ge(s_ready, TILES * n - 4 + c)
                        stt(v["s"], v["s"], v["eg"][:, c * P + P - 1:c * P + P], g(0)[:, 0:P],
                            ALU.mult, ALU.add).then_inc(s_ready, 1)
                if s == 30:
                    dve.wait_ge(ss_ps, n)
                    dve.wait_ge(ss_decayed, n)
                    tt(v["ss"], v["ss"], ps[:, 4:6, :].rearrange("p a b -> p (a b)"),
                       ALU.add).then_inc(ss_ready, 1)
                if s == 31:
                    dve.wait_ge(o_scale, n)
                    o = o_a[:, n - 1] if isinstance(n, int) else \
                        o_a[:, bass.ds(n - 1, 1)].rearrange("p a b -> p (a b)")
                    tt(v["db"], o, v["at"], ALU.mult).then_inc(o_scaled, 1)
                    dve.wait_ge(o_scaled, n)
                    dve.wait_ge(zs_ready, n + 1)
                    stt(o, v["db"], pcol("delta_g", 0), v["zs"], ALU.mult, ALU.mult).then_inc(head_out, 1)

            early = {0: 2, 1: 3, 3: 2, 16: 2, 18: 2}
            early_8 = {0: 3, 1: 3, 3: 2, 6: 1, 7: 1, 10: 1}
            late = {s: 2 for s in range(22, 32)}
            late_0 = {21: 3, 22: 3, 23: 3, 25: 2, 26: 3, 27: 2, 30: 2, 31: 2}

            def convolutions(n, s):
                gdn, proj = not first(n), not last(n)
                rest = early_8 if last(n) else early
                if gdn and s in rest:
                    t = STEPS_1 + sum(rest[x] for x in rest if x < s)
                    conf_taps(n - 1, t, t + rest[s])
                    if t + rest[s] == CF_TAPS:
                        dve.wait_ge(conv31, 62 * n)
                        dve.sem_inc(conv31_done, 1)
                if gdn and proj and s == 4:
                    ve.tensor_copy(qt[:], tap_of(n)[:, 0:3 * QK_TAPS]).then_inc(taps_cur, 1)
                    dve.wait_ge(taps_cur, 2 * n + 1)
                if proj and s == (21 if gdn else 20):
                    if gdn:
                        dve.wait_ge(conf_ready, n)
                    else:
                        dve.wait_ge(taps_landed, 16)
                    if first(n):
                        ve.tensor_copy(qt[:], tap_of(n)[:, 0:3 * QK_TAPS]).then_inc(taps_cur, 1)
                    ve.tensor_copy(ct[:], tap_of(n)[:, 3 * QK_TAPS:TAPW]).then_inc(taps_cur, 1)
                    dve.wait_ge(taps_cur, 2 * n + 2)
                    dve.wait_ge(gext_ready, n + 1)
                own = late_0 if first(n) else late
                if proj and s in own:
                    t = sum(own[x] for x in own if x < s)
                    conf_taps(n, t, t + own[s])
                if first(n) and s in (24, 28):
                    qkv_conv(n, (s - 24) // 4, 0, QK_TAPS)
                halves = (4, 7, 8, 10, 12, 14)
                if gdn and proj and s in halves:
                    i, half = divmod(halves.index(s), 2)
                    qkv_conv(n, i, 2 * half, 2 * half + 2)

            def phase(n):
                gdn = not first(n)
                if gdn:
                    if isinstance(n, int):
                        src = cols[:].rearrange("p (a h) -> p a h", h=H)[:, :, n - 1:n]
                    else:
                        src = cols[:].rearrange("p (a h) -> p a h", h=H)[:, :, bass.ds(n - 1, 1)]
                    dve.wait_ge(cols_ready, 2)
                    ve.tensor_copy(hc[:].unsqueeze(2), src).then_inc(hc_ready, 1)
                for s in range(32):
                    if not gdn or s < 1:
                        convolutions(n, s)
                    if first(n) and s == 20:
                        logits()
                    if first(n) and s == 23:
                        decay_copy()
                    if last(n) and 20 <= s < 28:
                        k = s - 20
                        if k == 0:
                            dve.wait_ge(mu_ready, 1)
                        tt(conf[:, k], conf[:, k], csum[:], ALU.subtract).then_inc(xc_ready, 1)
                    if last(n) and s == 31:
                        dve.wait_ge(ln_scale, 2)
                        for k in range(4):
                            tt(conf[:, k], conf[:, k], v["c31"], ALU.mult).then_inc(ln_scaled, 1)
                    if gdn:
                        head(n, s)
                        if s >= 1:
                            convolutions(n, s)
                if first(n):
                    qkv_conv(n, 2, 0, QK_TAPS)

            phase(0)
            with dve.Fori(1, H) as n:
                phase(n)
            phase(H)
            for k in range(KB):
                if k % 2:
                    dve.wait_ge(b_gated, k // 2 + 1)
                else:
                    dve.wait_ge(b_silu, k + 1)
                    tt(conf[:, k], conf[:, k], gate[:, k], ALU.mult).then_inc(b_gated_d, 1)
                    dve.wait_ge(b_gated_d, k // 2 + 1)
                tt(conf[:, k], conf[:, k], o_a[:, k], ALU.add).then_inc(mixed, 1)
                if k:
                    dve.wait_ge(high_ready, 8 + k)
                    tt(in_lo[:, k - 1], conf[:, k - 1], in_hi[:, k - 1].bitcast(F32),
                       ALU.subtract).then_inc(in_ready, 1)
            dve.wait_ge(high_ready, 16)
            tt(in_lo[:, 7], conf[:, 7], in_hi[:, 7].bitcast(F32), ALU.subtract).then_inc(in_ready, 1)
            dve.wait_ge(mixed, 8)
            for k in range(KB):
                ve.memset(o_a[:, k], 0.0).then_inc(dve_read, 1)

            dve.wait_ge(ms_scale, 2)
            dve.wait_ge(x_again, 16)
            dve.wait_ge(act_read, 72)
            dve.wait_ge(job_done, 72)
            for k in range(KB):
                if k == 0:
                    tt(gate[:, k], gate[:, k], v["c31"], ALU.mult).then_inc(y_scaled, 1)
                    dve.wait_ge(y_scaled, 1)
                else:
                    dve.wait_ge(y_scaled_p, k)
                stt(conf[:, k], gate[:, k], pcol("post_mix", k), xt[:, k], ALU.mult,
                    ALU.add).then_inc(mid_ready, 1)
                if k:
                    dve.wait_ge(high_ready, 16 + k)
                    stt(in_lo[:, k - 1], conf[:, k - 1], pcol("pre_ffn", k - 1),
                        in_hi[:, k - 1].bitcast(F32), ALU.mult, ALU.subtract).then_inc(in_ready, 1)
            dve.wait_ge(high_ready, 24)
            stt(in_lo[:, 7], conf[:, 7], pcol("pre_ffn", 7), in_hi[:, 7].bitcast(F32),
                ALU.mult, ALU.subtract).then_inc(in_ready, 1)

            def group(gr):
                for j in range(8):
                    dve.wait_ge(act_read, 8 * gr + 73 + j)
                    tt(f_tmp[:, 2 + j % 2], f_tmp[:, j % 2], f_tmp[:, j % 2], ALU.mult).then_inc(f_square, 1)
                    dve.wait_ge(f_square, 8 * gr + 3 + j)
                    dve.wait_ge(f_high, 8 * gr + 1 + j)
                    tt(f_lo[:, j], f_tmp[:, 2 + j % 2], f_hi[:, j].bitcast(F32),
                       ALU.subtract).then_inc(f_ready, 1)
                for j in range(8):
                    dve.wait_ge(job_done, 16 * gr + 81 + j)
                    tt(two(o_a[:, j]), two(o_a[:, j]), job_ps(j % 2), ALU.add).then_inc(dve_read, 1)

            with dve.Fori(0, FFN_GROUPS) as gr:
                group(gr)

            dve.wait_ge(ms2_log, 2)
            dve.wait_ge(ms3_ps, 1)
            tt(two(gate[:, 3]), g2(2), two(gate[:, 2]), ALU.mult).then_inc(var3, 1)
            dve.wait_ge(ms3_log, 1)
            stt(gate[:, 4], gate[:, 3], 0.5, gate[:, 1], ALU.mult, ALU.add).then_inc(expo, 1)
            dve.wait_ge(out_scale, 1)
            for i, k in enumerate(range(len(POOL_BLOCKS), KB)):
                tt(o_a[:, k], o_a[:, k], gate[:, 4], ALU.mult).then_inc(out_scaled, 1)
                dve.wait_ge(out_scaled, i + 1)
                stt(o_a[:, k], o_a[:, k], pcol("post_ffn", k), conf[:, k], ALU.mult,
                    ALU.add).then_inc(y_ready, 1)

        @block.gpsimd
        def _(pool):
            gp = nc.gpsimd

            def tt(out, a, b, op):
                return gp.tensor_tensor(out, a, b, op)

            def split(m, off):
                pool.wait_ge(w_high, 8 * m + off + 1)
                tt(w_lo[:, off % 2], raw[:, off % RING], w_hi[:, off % 2].bitcast(F32),
                   ALU.subtract).then_inc(w_low, 1)

            pool.wait_ge(consts_landed, 32)
            for j in range(2):
                split(0, j)
            pool.wait_ge(scale, 2)
            for k in range(1, KB, 2):
                tt(o_a[:, k], xt[:, k], v["c31"], ALU.mult).then_inc(x_scaled_p, 1)

            def bc(ap):
                return ap.unsqueeze(1).to_broadcast([P, TILES, P])

            def level(n, l):
                cr = c_r[(l - 1) % 2]
                if l == 3:
                    pool.wait_ge(c_tr, n)
                if l > 3:
                    pool.wait_ge(x_ps, LEVELS * n - 10 + l)
                if l == STEPS:
                    r = tt(pr(v["db"]), pr(v["at"]), bc(con("strict")), ALU.mult)
                else:
                    r = tt(pr(cr), pr(v["at"]), lvl(l), ALU.mult)
                if l <= LEVELS_S:
                    r = tt(c_s[(l - 1) % 2][0:SMP], sm(v["at"]), lvl_s(l), ALU.mult)
                r.then_inc(c_ready, 1)

            def phase(n):
                gdn, proj = not first(n), not last(n)
                if gdn:
                    pool.wait_ge(hc_ready, n)
                    tt(pr(v["dm"]), bc(con("tri")), hcol(G), ALU.mult)
                    tt(sm(v["dm"]), con("tri_s", SMP), hcol_s(G, SMP), ALU.mult).then_inc(gtri_ready, 1)
                    tt(pr(v["qk"]), bc(con("big")), hcol(GAM), ALU.add)
                    tt(sm(v["qk"]), con("big_s", SMP), hcol_s(GAM, SMP), ALU.add).then_inc(gm_ready, 1)
                for s in range(33):
                    off = split_off(n, s)
                    if off is not None:
                        split(n, off)
                    pos, j = evac(n, s)
                    if j == GA:
                        pool.wait_ge(act_read, 8 * n - 2 + pos)
                        tt(v["zs"], v["zs"], v["sig"], ALU.mult).then_inc(zs_ready, 1)
                    if proj and s == (20 if first(n) else 2):
                        pool.wait_ge(halo_landed, 16 * n + 16)
                        if gdn:
                            pool.wait_ge(conv4_done, 3 * n)
                        pool.nop(nofuse=True)
                        for i in range(3):
                            gp.tensor_copy(seqs(EXTS[i], EXT, EXS, 0, QK_TAPS - 1),
                                           halo[:, 24 * i:24 * i + 24].rearrange("p (s t) -> p s t", s=NS)
                                           ).then_inc(halo_used, 1)
                    if j == CB:
                        ge = v["gext"]
                        if gdn:
                            pool.wait_ge(conv31_done, n)
                            pool.nop(nofuse=True)
                        gp.tensor_copy(seqs(ge, GXT, GXS, 0, CF_TAPS - 1),
                                       halo[:, 72:HALO].rearrange("p (s t) -> p s t", s=NS)).then_inc(halo_used, 1)
                        pool.wait_ge(act_read, 8 * n - 2 + pos)
                        tt(ge[:, CF_TAPS - 1:GXT], v["c4"][:, 0:SEQ], v["sig"][:, 0:SEQ], ALU.mult)
                        tt(seqs(ge, GXT, GXS, CF_TAPS - 1, LS),
                           v["c4"][:, SEQ:TOK].rearrange("p (s t) -> p s t", s=NS),
                           v["sig"][:, SEQ:TOK].rearrange("p (s t) -> p s t", s=NS),
                           ALU.mult).then_inc(gext_ready, 1)
                        pool.wait_ge(gext_ready, n + 1)
                        pool.wait_ge(halo_used, 4 * n + 4)
                        if gdn:
                            pool.wait_ge(crows_stored, 16 * n)
                        pool.nop(nofuse=True)
                        gp.tensor_copy(c_rows[:, 0:CF_TAPS - 1], ge[:, GXT - CF_TAPS + 1:GXT])
                        gp.tensor_copy(c_rows[:, CF_TAPS - 1:].rearrange("p (s t) -> p s t", s=NS),
                                       seqs(ge, GXT, GXS, LS, CF_TAPS - 1)).then_inc(crows_ready, 1)
                    if j is not None and j >= Q:
                        i = j - Q
                        pool.wait_ge(act_read, 8 * n - 2 + pos)
                        if gdn and i == 0:
                            pool.wait_ge(qrows_stored, 16 * n)
                        pool.nop(nofuse=True)
                        gp.tensor_copy(q_rows[:, 27 * i:27 * i + 3], EXTS[i][:, EXT - 3:EXT])
                        gp.tensor_copy(q_rows[:, 27 * i + 3:27 * i + 27].rearrange("p (s t) -> p s t", s=NS),
                                       seqs(EXTS[i], EXT, EXS, LS, 3)).then_inc(qrows_ready, 1)
                    if gdn and s == (13 if last(n) else 20):
                        pool.wait_ge(conf_ready, n)
                        if isinstance(n, int):
                            src = conf[:, n - 1]
                        else:
                            src = conf[:, bass.ds(n - 1, 1)].rearrange("p a b -> p (a b)")
                        pool.wait_ge(csum_done, n)
                        tt(csum[:], csum[:], src, ALU.add).then_inc(csum_done, 1)
                    if not gdn:
                        continue
                    if s == 5:
                        pool.wait_ge(at_ready, n)
                        level(n, 2)
                    if s == 6:
                        pool.wait_ge(c1_ready, n)
                        tt(pr(u_r), bc(con("ident")), pr(c_r[0].bitcast(F32)), ALU.subtract)
                        tt(v["us"][0:SMP], con("ident", SMP)[:, 0:SMP], c_s[0][0:SMP], ALU.subtract).then_inc(u0_ready, 1)
                        pool.wait_ge(qk_ps, n)
                        tt(v["qn"], v["qn"], v["eg"], ALU.mult).then_inc(qd_ready, 1)
                    if s == 7:
                        pool.wait_ge(u0_ready, n)
                        level(n, 3)
                    if s in (8, 10, 12, 14, 16):
                        level(n, s // 2)
                    if s == 19:
                        pool.wait_ge(t_ready, LEVELS * n)
                        tt(pr(v["um"]), pr(t_r.bitcast(F32)), bc(con("ident")), ALU.subtract).then_inc(tmi_ready, 1)
                    if s == 22:
                        pool.wait_ge(kd_ready, 2 * n)
                        tt(v["um"][:, 0:NS * SMP].rearrange("p (q t) -> p q t", q=NS),
                           sm(v["kn"], P).unsqueeze(1).to_broadcast([P, NS, SMP]),
                           con("colm").rearrange("p (q t) -> p q t", q=NS), ALU.mult).then_inc(kdm_ready, 1)
                    if s == 26:
                        pool.wait_ge(us_ready, n)
                        tt(v["um"][0:SMP, :].rearrange("p (q c) -> p q c", q=NS),
                           smw(v["u"]).unsqueeze(1).to_broadcast([SMP, NS, P]),
                           con("rowm", SMP).unsqueeze(2).to_broadcast([SMP, NS, P]),
                           ALU.mult).then_inc(um_ready, 1)
                    if s == 29:
                        pool.wait_ge(o_ps, n)
                        tt(v["ss"].rearrange("p (q c) -> p q c", q=NS),
                           v["ss"].rearrange("p (q c) -> p q c", q=NS),
                           v["eg"][:, SEQ + LS - 1:TOK:LS].unsqueeze(2).to_broadcast([P, NS, P]),
                           ALU.mult).then_inc(ss_decayed, 1)

            phase(0)
            with pool.Fori(1, H) as n:
                phase(n)
            phase(H)
            pool.wait_ge(ln_scale, 2)
            for k in (4, 5, -1, 6, -3, 7, -5, -7):
                if k > 0:
                    tt(conf[:, k], conf[:, k], v["c31"], ALU.mult).then_inc(ln_scaled_p, 1)
                else:
                    pool.wait_ge(b_silu, 1 - k)
                    tt(conf[:, -k], conf[:, -k], gate[:, -k], ALU.mult).then_inc(b_gated, 1)
                if k == 5:
                    split(8, 1)

            for j in range(8):
                if j < 7:
                    split(8, j + 2)
                pool.wait_ge(y_sq, j + 1)
                src = v[("c4", "extq")[j % 2]][:, 0:TOK]
                if j:
                    pool.wait_ge(y_sum, j)
                    tt(csum[:], csum[:], src, ALU.add).then_inc(y_sum, 1)
                else:
                    gp.tensor_copy(csum[:], src).then_inc(y_sum, 1)
            split(8, 9)
            pool.wait_ge(ms_scale, 2)
            for k in range(1, KB):
                tt(gate[:, k], gate[:, k], v["c31"], ALU.mult).then_inc(y_scaled_p, 1)

            def group(gr, tail=False):
                m = 2 * gr + 9
                for j in range(8):
                    split(m, j + 2)
                    if tail:
                        pool.wait_ge(mid_sq, j + 1)
                        src = v[("sig", "zs")[j % 2]]
                        if j:
                            pool.wait_ge(mid_sum, j)
                            tt(csum[:], csum[:], src, ALU.add).then_inc(mid_sum, 1)
                        else:
                            gp.tensor_copy(csum[:], src).then_inc(mid_sum, 1)
                for j in range(8):
                    if not (tail and j >= 6):
                        split(m + 1, j + 2)
                    if tail:
                        pool.wait_ge(out_sq, j + 1)
                        src = v[("sig", "zs")[j % 2]]
                        if j:
                            pool.wait_ge(out_sum, j)
                            tt(gate[:, 5], gate[:, 5], src, ALU.add).then_inc(out_sum, 1)
                        else:
                            gp.tensor_copy(gate[:, 5], src).then_inc(out_sum, 1)

            with pool.Fori(0, FFN_GROUPS - 1) as gr:
                group(gr)
            group(FFN_GROUPS - 1, tail=True)
            pool.wait_ge(out_scale, 1)
            pool.wait_ge(out_gained, len(POOL_BLOCKS))
            for i, k in enumerate(POOL_BLOCKS):
                tt(o_a[:, k], o_a[:, k], gate[:, 4], ALU.mult).then_inc(out_scaled_p, 1)
                pool.wait_ge(out_scaled_p, i + 1)
                tt(o_a[:, k], o_a[:, k], conf[:, k], ALU.add).then_inc(y_ready_p, 1)


def shape_constants():
    i, j = np.indices((P, P))
    a, b = np.indices((SMP, SMP))
    same = a // LS == b // LS
    out = np.zeros((P, CONSTS), np.float32)

    def put(nm, value, at=0):
        o = OFF[nm][0] + at
        out[:value.shape[0], o:o + value.shape[1]] = value

    def half(r, c, n):
        return (r // (2 * n) == c // (2 * n)) & (r // n < c // n)

    put("ident", i == j)
    put("ones", np.ones((P, P)))
    put("tri", i <= j)
    put("suf", i > j)
    put("big", np.where(j < i, BIG, 0))
    put("tri_s", same & (a <= b))
    put("suf_s", same & (a > b))
    put("big_s", np.where(same & (b >= a), 0, BIG))
    for l in range(LEVELS):
        put("lvl", half(i, j, 2 ** l), l * P)
    for l in range(LEVELS_S):
        put("lvl_s", half(a, b, 2 ** l), l * SMP)
    for q in range(NS):
        put("colm", np.tile(np.arange(SMP) // LS == q, (P, 1)), q * SMP)
    put("strict", i < j)
    put("rowm", np.arange(SMP)[:, None] // LS == np.arange(NS)[None, :])
    put("eps", np.full((P, 1), EPS))
    put("eps128", np.full((P, 1), P * EPS))
    return out


def channels(a):
    a = a.reshape(a.shape[:-1] + (-1, P))
    return np.moveaxis(a, (-1, -2), (0, 1))


def job_weights(w):
    return w.reshape(KB, P, -1, P).transpose(2, 1, 0, 3)


_OUTS = [("y", (P, KB, TOK)), ("s_prompt", (H, P, P)), ("s_sample", (H, P, NS * P)),
         ("qkv_rows", (H, P, 81)), ("conf_rows", (H, P, 9 * (CF_TAPS - 1)))]


def kernel(x_prompt, x_sample, state_delta, state_qkv_conv, state_conf_conv, w_in, conv_qkv_w,
           a_log, dt_bias, delta_norm_g, conf_dw_w, conf_dw_b, conf_ln_g, conf_ln_b, w_out,
           g_pre_mix, g_post_mix, g_pre_ffn, g_post_ffn, w_up, w_down):
    import concourse.bacc as bacc
    from concourse.bass_utils import run_bass_kernel_spmd

    f = lambda a: np.ascontiguousarray(np.asarray(a))
    x = np.concatenate([f(x_prompt)[0], f(x_sample).reshape(SMP, D)], 0)
    wi = f(w_in)[0]
    o1 = 3 * D
    o2 = o1 + 2 * H
    qkv = job_weights(wi[:, :o1])
    rest = job_weights(wi[:, o2:])
    z, ca, cb, ga, gb = (rest[8 * i:8 * i + 8] for i in range(5))
    parts = []
    for n in range(H + 1):
        for kind in (FIRST if n == 0 else LAST if n == H else MIDDLE).values():
            parts.append({Z: z, GA: ga, GB: gb}[kind][n - 1] if kind <= GB else
                         {CA: ca, CB: cb, Q: qkv, K: qkv[H:], V: qkv[2 * H:]}[kind][n])
    parts += list(job_weights(f(w_out)[0]))
    up = job_weights(f(w_up)[0])
    down = f(w_down)[0]
    for gr in range(FFN_GROUPS):
        parts += list(up[8 * gr:8 * gr + 8])
        parts += list(job_weights(down[D * gr:D * gr + D]))
    w_all = np.stack(parts)

    par = np.zeros((P, len(PARAMS), KB), np.float32)
    for i, a in enumerate((g_pre_mix, g_post_mix, g_pre_ffn, g_post_ffn, conf_ln_g, conf_ln_b)):
        par[:, i] = channels(f(a)[0])
    par[:, 6, 0] = f(delta_norm_g)[0]
    cq = channels(f(conv_qkv_w)[0]).reshape(P, 3, H, QK_TAPS).transpose(0, 2, 1, 3).reshape(P, H, 12)
    taps = np.concatenate([cq, channels(f(conf_dw_w)[0]), channels(f(conf_dw_b)[0])[:, :, None]], 2)
    hq = channels(f(state_qkv_conv)[0]).reshape(P, 3, H, 24).transpose(2, 0, 1, 3).reshape(H, P, 72)
    hf = channels(f(state_conf_conv)[0]).reshape(P, H, 240).transpose(1, 0, 2)
    halos = np.concatenate([hq, hf], 2)
    halos = np.concatenate([halos, np.zeros((1, P, HALO), np.float32)], 0)
    arrays = {
        "x_t": channels(x).reshape(P, KB, TOK),
        "w_all": w_all,
        "w_log": wi[:, o1:o2].reshape(KB, P, 2 * H).transpose(1, 0, 2).reshape(P, KB * 2 * H),
        "log_par": np.tile(np.concatenate([f(dt_bias)[0], f(a_log)[0]])[None], (P, 1)),
        "consts": shape_constants(),
        "params": par.reshape(P, -1),
        "taps": taps.reshape(P, -1),
        "halos": halos,
        "s_in": f(state_delta)[0].transpose(1, 2, 0, 3).reshape(H, P, NS * P),
    }
    nc = bacc.Bacc("TRN2", target_bir_lowering=False, num_devices=1)
    arrays = {k + "_in": np.ascontiguousarray(a) for k, a in arrays.items()}
    args = [nc.dram_tensor(k, a.shape, mybir.dt.from_np(a.dtype), kind="ExternalInput").ap()
            for k, a in arrays.items()]
    args += [nc.dram_tensor(k + "_out", s, F32, kind="ExternalOutput").ap() for k, s in _OUTS]
    build(nc, *args)
    res = run_bass_kernel_spmd(nc, [arrays], core_ids=[0]).results[0]
    y, sp, ss, qr, cr = (np.asarray(res[k + "_out"]) for k, _ in _OUTS)
    y = y.transpose(2, 1, 0).reshape(TOK, D)
    qr = qr.reshape(H, P, 3, 27).transpose(3, 2, 0, 1).reshape(27, 3 * D)
    cr = cr.reshape(H, P, 9, CF_TAPS - 1).transpose(2, 3, 0, 1).reshape(9, CF_TAPS - 1, D)
    return (y[:SEQ].reshape(1, SEQ, D), y[SEQ:].reshape(NS, LS, D), sp.reshape(1, 1, H, P, P),
            qr[:3].reshape(1, 1, 3, 3 * D), cr[:1].reshape(1, 1, CF_TAPS - 1, D),
            ss.reshape(H, P, NS, P).transpose(2, 0, 1, 3).reshape(1, NS, H, P, P),
            qr[3:].reshape(1, NS, 3, 3 * D), cr[1:].reshape(1, NS, CF_TAPS - 1, D))
```
